# Optimizing a Trainium2 kernel written in Bass

```python
import math
import jax
import jax.numpy as jnp
from jax import lax
import numpy as np
import math, functools
import jax, jax.numpy as jnp

D_MODEL = 1024
BATCH = 1
SEQ = 512
DEPTH = 2

N_MIXERS = 2
S5_GROUP = 16
S5_GROUPS = D_MODEL // S5_GROUP
S5_STATE = 64
N_HEADS = 16
HEAD_DIM = D_MODEL // N_HEADS
IDX_HEADS = 8
IDX_DIM = 64
TOPK_MAX = 256
Q_BLOCK = 128
ROPE_THETA = 10000.0
D_FF = ((8 * D_MODEL // 3 + 255) // 256) * 256
N_S5 = (DEPTH + 1) // 2
N_DSA = DEPTH // 2
DSA_PROJ = 3 * D_MODEL + IDX_HEADS * IDX_DIM + IDX_DIM + IDX_HEADS
EPS = 1e-6


def rmsnorm(x, gain):
    xf = x.astype(jnp.float32)
    y = xf * lax.rsqrt(jnp.mean(xf * xf, axis=-1, keepdims=True) + EPS)
    if gain is not None:
        y = y * gain.astype(jnp.float32)
    return y.astype(x.dtype)

def rope_tables(length):
    inv_freq = ROPE_THETA ** (-jnp.arange(0, HEAD_DIM, 2, dtype=jnp.float32) / HEAD_DIM)
    ang = jnp.arange(length, dtype=jnp.float32)[:, None] * inv_freq[None, :]
    return jnp.cos(ang), jnp.sin(ang)

def apply_rope(t, cos, sin):
    tf = t.astype(jnp.float32)
    t1, t2 = jnp.split(tf, 2, axis=-1)
    c = cos[None, :, None, :]
    s = sin[None, :, None, :]
    out = jnp.concatenate([t1 * c - t2 * s, t2 * c + t1 * s], axis=-1)
    return out.astype(t.dtype)

def _ssm_combine(e1, e2):
    a1, b1 = e1
    a2, b2 = e2
    return a1 * a2, a2 * b1 + b2

def s5_mixer(u, lam_re, lam_im, log_dt, b_re, b_im, c_re, c_im, d_skip, w_glu):
    bsz, length, _ = u.shape
    f32 = jnp.float32
    lam = lax.complex(lam_re.astype(f32), lam_im.astype(f32))
    dt = jnp.exp(log_dt.astype(f32))[:, None]
    a_bar = jnp.exp(lam * dt)
    b_bar = ((a_bar - 1.0) / lam)[..., None] * lax.complex(b_re.astype(f32), b_im.astype(f32))
    ug = u.astype(f32).reshape(bsz, length, S5_GROUPS, S5_GROUP).astype(jnp.complex64)
    bu = jnp.einsum('blgh,gph->blgp', ug, b_bar)
    a_seq = jnp.broadcast_to(a_bar, bu.shape)
    _, states = lax.associative_scan(_ssm_combine, (a_seq, bu), axis=1)
    c = lax.complex(c_re.astype(f32), c_im.astype(f32))
    y = jnp.einsum('blgp,ghp->blgh', states, c).real.reshape(bsz, length, D_MODEL)
    y = y + d_skip.astype(f32) * u.astype(f32)
    y = jax.nn.gelu(y).astype(u.dtype)
    val, gate = jnp.split(y @ w_glu, 2, axis=-1)
    return val * jax.nn.sigmoid(gate)

def dsa_mixer(h, w_in, q_gain, k_gain, w_o, cos, sin, topk):
    bsz, length, _ = h.shape
    f32 = jnp.float32
    proj = h @ w_in
    cuts = [D_MODEL, 2 * D_MODEL, 3 * D_MODEL, 3 * D_MODEL + IDX_HEADS * IDX_DIM,
            3 * D_MODEL + IDX_HEADS * IDX_DIM + IDX_DIM]
    q, k, v, qi, ki, wi = jnp.split(proj, cuts, axis=-1)
    q = q.reshape(bsz, length, N_HEADS, HEAD_DIM)
    k = k.reshape(bsz, length, N_HEADS, HEAD_DIM)
    v = v.reshape(bsz, length, N_HEADS, HEAD_DIM)
    qi = qi.reshape(bsz, length, IDX_HEADS, IDX_DIM)
    q = apply_rope(rmsnorm(q, q_gain), cos, sin)
    k = apply_rope(rmsnorm(k, k_gain), cos, sin)
    qi = apply_rope(qi, cos, sin)
    ki = apply_rope(rmsnorm(ki, None)[:, :, None, :], cos, sin)[:, :, 0, :]
    wi = wi.astype(f32) * (IDX_HEADS ** -0.5)
    nb = length // Q_BLOCK
    kpos = jnp.arange(length, dtype=jnp.int32)
    qpos_blocks = kpos.reshape(nb, Q_BLOCK)
    att_scale = HEAD_DIM ** -0.5
    idx_scale = IDX_DIM ** -0.5

    def to_blocks(t):
        return t.reshape(bsz, nb, Q_BLOCK, *t.shape[2:]).swapaxes(0, 1)

    def attend_block(args):
        qb, qib, wb, qpos = args
        s_idx = jnp.einsum('bqhd,bkd->bqhk', qib, ki).astype(f32) * idx_scale
        score = jnp.einsum('bqhk,bqh->bqk', jax.nn.relu(s_idx), wb)
        causal = kpos[None, None, :] <= qpos[None, :, None]
        score = jnp.where(causal, score, -jnp.inf)
        _, sel = lax.top_k(score, topk)
        kg = jax.vmap(lambda kb, ib: kb[ib])(k, sel)
        vg = jax.vmap(lambda vb, ib: vb[ib])(v, sel)
        logits = jnp.einsum('bqhd,bqkhd->bhqk', qb, kg).astype(f32) * att_scale
        valid = (sel <= qpos[None, :, None])[:, None, :, :]
        logits = jnp.where(valid, logits, -jnp.inf)
        p = jax.nn.softmax(logits, axis=-1).astype(vg.dtype)
        return jnp.einsum('bhqk,bqkhd->bqhd', p, vg)

    out = lax.map(attend_block, (to_blocks(q), to_blocks(qi), to_blocks(wi), qpos_blocks))
    out = out.swapaxes(0, 1).reshape(bsz, length, D_MODEL)
    return out @ w_o

def swiglu(h, w_gate_up, w_down):
    gate, up = jnp.split(h @ w_gate_up, 2, axis=-1)
    return (jax.nn.silu(gate) * up) @ w_down

def first_inputs(seed: int = 0) -> dict:
    key = jax.random.key(seed)
    ks = jax.random.split(key, 20)
    f32 = jnp.float32
    nrm = lambda k, shape, s: jax.random.normal(k, shape, f32) * s
    x = jax.random.normal(ks[0], (BATCH, SEQ, D_MODEL), f32)
    n_idx = jnp.arange(S5_STATE, dtype=f32)
    s5_lambda_re = -0.5 + nrm(ks[1], (N_S5, S5_GROUPS, S5_STATE), 0.01)
    s5_lambda_im = math.pi * n_idx[None, None, :] + nrm(ks[2], (N_S5, S5_GROUPS, S5_STATE), 0.01)
    s5_log_dt = jax.random.uniform(ks[3], (N_S5, S5_GROUPS), f32, math.log(1e-3), math.log(1e-1))
    s5_b_re = nrm(ks[4], (N_S5, S5_GROUPS, S5_STATE, S5_GROUP), (2 * S5_GROUP) ** -0.5)
    s5_b_im = nrm(ks[5], (N_S5, S5_GROUPS, S5_STATE, S5_GROUP), (2 * S5_GROUP) ** -0.5)
    s5_c_re = nrm(ks[6], (N_S5, S5_GROUPS, S5_GROUP, S5_STATE), (2 * S5_STATE) ** -0.5)
    s5_c_im = nrm(ks[7], (N_S5, S5_GROUPS, S5_GROUP, S5_STATE), (2 * S5_STATE) ** -0.5)
    s5_d = nrm(ks[8], (N_S5, D_MODEL), 1.0)
    s5_w_glu = nrm(ks[9], (N_S5, D_MODEL, 2 * D_MODEL), D_MODEL ** -0.5)
    dsa_w_in = nrm(ks[10], (N_DSA, D_MODEL, DSA_PROJ), D_MODEL ** -0.5)
    dsa_q_norm = 1.0 + nrm(ks[11], (N_DSA, HEAD_DIM), 0.02)
    dsa_k_norm = 1.0 + nrm(ks[12], (N_DSA, HEAD_DIM), 0.02)
    dsa_w_o = nrm(ks[13], (N_DSA, D_MODEL, D_MODEL), D_MODEL ** -0.5)
    ffn_w_gate_up = nrm(ks[14], (DEPTH, D_MODEL, 2 * D_FF), D_MODEL ** -0.5)
    ffn_w_down = nrm(ks[15], (DEPTH, D_FF, D_MODEL), D_FF ** -0.5)
    norm_mix = 1.0 + nrm(ks[16], (DEPTH, D_MODEL), 0.02)
    norm_ffn = 1.0 + nrm(ks[17], (DEPTH, D_MODEL), 0.02)
    return {'x': x, 's5_lambda_re': s5_lambda_re, 's5_lambda_im': s5_lambda_im, 's5_log_dt': s5_log_dt,
            's5_b_re': s5_b_re, 's5_b_im': s5_b_im, 's5_c_re': s5_c_re, 's5_c_im': s5_c_im,
            's5_d': s5_d, 's5_w_glu': s5_w_glu, 'dsa_w_in': dsa_w_in, 'dsa_q_norm': dsa_q_norm,
            'dsa_k_norm': dsa_k_norm, 'dsa_w_o': dsa_w_o, 'ffn_w_gate_up': ffn_w_gate_up,
            'ffn_w_down': ffn_w_down, 'norm_mix': norm_mix, 'norm_ffn': norm_ffn}

def first_block(x, s5_lambda_re, s5_lambda_im, s5_log_dt, s5_b_re, s5_b_im, s5_c_re, s5_c_im,
              s5_d, s5_w_glu, dsa_w_in, dsa_q_norm, dsa_k_norm, dsa_w_o, ffn_w_gate_up,
              ffn_w_down, norm_mix, norm_ffn):
    length = x.shape[1]
    topk = min(TOPK_MAX, length // 4)
    cos, sin = rope_tables(length)
    for i in range(DEPTH):
        h = rmsnorm(x, norm_mix[i])
        j = i // N_MIXERS
        if i % N_MIXERS == 0:
            mix = s5_mixer(h, s5_lambda_re[j], s5_lambda_im[j], s5_log_dt[j], s5_b_re[j], s5_b_im[j],
                           s5_c_re[j], s5_c_im[j], s5_d[j], s5_w_glu[j])
        else:
            mix = dsa_mixer(h, dsa_w_in[j], dsa_q_norm[j], dsa_k_norm[j], dsa_w_o[j], cos, sin, topk)
        x = x + mix.astype(x.dtype)
        x = x + swiglu(rmsnorm(x, norm_ffn[i]), ffn_w_gate_up[i], ffn_w_down[i]).astype(x.dtype)
    return x


DEPTH_2 = 1

ATT_HEADS = 8
ATT_HEAD_DIM = 64
ATT_WIDTH = ATT_HEADS * ATT_HEAD_DIM
ATT_PATTERNS = ((128, 1), (512, 4), (2048, 16))
ATT_BLOCK = 128
SSD_HEADS = 8
SSD_HEAD_DIM = 64
SSD_WIDTH = SSD_HEADS * SSD_HEAD_DIM
SSD_GROUPS = 2
SSD_STATE = 128
SSD_CHUNK = 128
SSD_CONV_CH = SSD_WIDTH + 2 * SSD_GROUPS * SSD_STATE
DT_MIN = 0.001
DT_MAX = 0.1
LRU_WIDTH = 512
LRU_BLOCKS = 8
LRU_BLOCK_W = LRU_WIDTH // LRU_BLOCKS
LRU_C = 8.0
CONV_WIDTH = 4
D_MIX = ATT_WIDTH + SSD_WIDTH + LRU_WIDTH
IN_COLS = 3 * ATT_WIDTH + SSD_WIDTH + SSD_CONV_CH + SSD_HEADS + 2 * LRU_WIDTH
D_FF_2 = ((8 * D_MODEL + 3 * 256 - 1) // (3 * 256)) * 256
NORM_EPS = 1e-6
SSD_NORM_EPS = 1e-5


def rmsnorm_2(x, g, eps=NORM_EPS):
    xf = x.astype(jnp.float32)
    y = xf * lax.rsqrt(jnp.mean(xf * xf, axis=-1, keepdims=True) + eps)
    return (y * g.astype(jnp.float32)).astype(x.dtype)

def causal_depthwise_conv(x, w, b):
    k_width, s = w.shape[0], x.shape[1]
    xp = jnp.pad(x, ((0, 0), (k_width - 1, 0), (0, 0)))
    y = b + xp[:, k_width - 1:] * w[k_width - 1]
    for k in range(k_width - 1):
        y = y + xp[:, k:k + s] * w[k]
    return y

def split_cols(proj):
    sizes = (ATT_WIDTH, ATT_WIDTH, ATT_WIDTH, SSD_WIDTH, SSD_CONV_CH, SSD_HEADS, LRU_WIDTH, LRU_WIDTH)
    offsets = np.cumsum(sizes)[:-1].tolist()
    return jnp.split(proj, offsets, axis=-1)

def dilated_branch(q, k, v, window, dilation, slopes):
    b, s, h, dh = q.shape
    length = s // dilation
    nb = -(-length // ATT_BLOCK)
    pad = nb * ATT_BLOCK - length

    def to_blocks(t):
        t = t.reshape(b, length, dilation, h, dh).transpose(0, 2, 3, 1, 4)
        t = jnp.pad(t, ((0, 0), (0, 0), (0, 0), (0, pad), (0, 0)))
        return t.reshape(b, dilation, h, nb, ATT_BLOCK, dh)

    def with_prev(t):
        prev = jnp.pad(t[:, :, :, :-1], ((0, 0), (0, 0), (0, 0), (1, 0), (0, 0), (0, 0)))
        return jnp.concatenate([prev, t], axis=4)

    qb, kb, vb = to_blocks(q), to_blocks(k), to_blocks(v)
    kk, vv = with_prev(kb), with_prev(vb)
    scores = jnp.einsum('brhnqd,brhnkd->brhnqk', qb, kk,
                        preferred_element_type=jnp.float32) * (ATT_HEAD_DIM ** -0.5)
    qi = jnp.arange(ATT_BLOCK)[:, None]
    ki = jnp.arange(2 * ATT_BLOCK)[None, :]
    dist = ATT_BLOCK + qi - ki
    band = (dist >= 0) & (dist <= window // dilation)
    valid = band[None] & ((jnp.arange(nb)[:, None, None] > 0) | (ki[None] >= ATT_BLOCK))
    alibi = -slopes[:, None, None] * (dilation * dist).astype(jnp.float32)
    scores = scores + alibi[None, None, :, None]
    scores = jnp.where(valid[None, None, None], scores, -jnp.inf)
    m = jnp.max(scores, axis=-1)
    p = jnp.exp(scores - m[..., None])
    den = jnp.sum(p, axis=-1)
    num = jnp.einsum('brhnqk,brhnkd->brhnqd', p, vv.astype(jnp.float32))

    def from_blocks(t):
        t = t.reshape(b, dilation, h, nb * ATT_BLOCK, *t.shape[5:])[:, :, :, :length]
        t = jnp.moveaxis(t, 3, 1)
        return t.reshape(b, s, h, *t.shape[4:])

    return from_blocks(num), from_blocks(m), from_blocks(den)

def dilated_attention(q, k, v):
    b, s, _ = q.shape
    shp = (b, s, ATT_HEADS, ATT_HEAD_DIM)
    q, k, v = q.reshape(shp), k.reshape(shp), v.reshape(shp)
    slopes = jnp.exp2(-8.0 * jnp.arange(1, ATT_HEADS + 1, dtype=jnp.float32) / ATT_HEADS)
    branches = [dilated_branch(q, k, v, w, d, slopes) for (w, d) in ATT_PATTERNS]
    m_all = functools.reduce(jnp.maximum, [br[1] for br in branches])
    num = jnp.zeros(shp, jnp.float32)
    den = jnp.zeros(shp[:3], jnp.float32)
    for n_g, m_g, d_g in branches:
        e = jnp.exp(m_g - m_all)
        num = num + n_g * e[..., None]
        den = den + d_g * e
    return (num / den[..., None]).reshape(b, s, ATT_WIDTH)

def ssd_chunked_scan(x, dt, a, bm, cm):
    b, s, h, p = x.shape
    n = bm.shape[-1]
    q = SSD_CHUNK
    nc = s // q
    rep = h // bm.shape[2]
    x = x.reshape(b, nc, q, h, p)
    dt = dt.reshape(b, nc, q, h)
    bh = jnp.repeat(bm, rep, axis=2).reshape(b, nc, q, h, n)
    ch = jnp.repeat(cm, rep, axis=2).reshape(b, nc, q, h, n)
    acs = jnp.cumsum(dt * a, axis=2)
    seg = acs[:, :, :, None, :] - acs[:, :, None, :, :]
    causal = jnp.tril(jnp.ones((q, q), dtype=bool))[None, None, :, :, None]
    lmat = jnp.exp(jnp.where(causal, seg, -jnp.inf))
    scores = jnp.einsum('bcihn,bcjhn->bcijh', ch, bh) * lmat * dt[:, :, None, :, :]
    y_diag = jnp.einsum('bcijh,bcjhp->bcihp', scores, x)
    decay_to_end = jnp.exp(acs[:, :, -1:, :] - acs)
    states = jnp.einsum('bcjhn,bcjh,bcjhp->bchpn', bh, decay_to_end * dt, x)
    chunk_decay = jnp.exp(acs[:, :, -1, :])

    def step(carry, inp):
        st, dc = inp
        return dc[:, :, None, None] * carry + st, carry

    _, prev = lax.scan(step, jnp.zeros((b, h, p, n), x.dtype),
                       (jnp.moveaxis(states, 1, 0), jnp.moveaxis(chunk_decay, 1, 0)))
    prev = jnp.moveaxis(prev, 0, 1)
    y_off = jnp.einsum('bcihn,bchpn,bcih->bcihp', ch, prev, jnp.exp(acs))
    return (y_diag + y_off).reshape(b, s, h, p)

def ssd_mixer(z, xbc, dt_raw, conv_w, conv_b, dt_bias, a_log, d_skip, norm_w):
    b, s, _ = z.shape
    f32 = jnp.float32
    xbc = jax.nn.silu(causal_depthwise_conv(xbc, conv_w, conv_b)).astype(f32)
    xs, bm, cm = jnp.split(xbc, [SSD_WIDTH, SSD_WIDTH + SSD_GROUPS * SSD_STATE], axis=-1)
    xs = xs.reshape(b, s, SSD_HEADS, SSD_HEAD_DIM)
    bm = bm.reshape(b, s, SSD_GROUPS, SSD_STATE)
    cm = cm.reshape(b, s, SSD_GROUPS, SSD_STATE)
    dt = jax.nn.softplus(dt_raw.astype(f32) + dt_bias.astype(f32))
    a = -jnp.exp(a_log.astype(f32))
    y = ssd_chunked_scan(xs, dt, a, bm, cm) + d_skip.astype(f32)[:, None] * xs
    y = y.reshape(b, s, SSD_WIDTH) * jax.nn.silu(z.astype(f32))
    yg = y.reshape(b, s, SSD_GROUPS, SSD_WIDTH // SSD_GROUPS)
    yg = yg * lax.rsqrt(jnp.mean(yg * yg, axis=-1, keepdims=True) + SSD_NORM_EPS)
    return yg.reshape(b, s, SSD_WIDTH) * norm_w.astype(f32)

def rglru_mixer(gate_in, x_in, conv_w, conv_b, wa, ba, wx, bx, lam):
    b, s, _ = x_in.shape
    f32 = jnp.float32
    gate = jax.nn.gelu(gate_in.astype(f32))
    xc = causal_depthwise_conv(x_in, conv_w, conv_b).astype(f32)
    xb = xc.reshape(b, s, LRU_BLOCKS, LRU_BLOCK_W)
    r = jax.nn.sigmoid(jnp.einsum('bsnc,ncd->bsnd', xb, wa.astype(f32)).reshape(b, s, LRU_WIDTH) + ba.astype(f32))
    i = jax.nn.sigmoid(jnp.einsum('bsnc,ncd->bsnd', xb, wx.astype(f32)).reshape(b, s, LRU_WIDTH) + bx.astype(f32))
    log_a = -LRU_C * r * jax.nn.softplus(-lam.astype(f32))
    a = jnp.exp(log_a)
    u = jnp.sqrt(-jnp.expm1(2.0 * log_a)) * (i * xc)

    def combine(left, right):
        a_l, h_l = left
        a_r, h_r = right
        return a_l * a_r, a_r * h_l + h_r

    _, h = lax.associative_scan(combine, (a, u), axis=1)
    return h * gate

def swiglu_2(h, w_gate, w_up, w_down):
    return (jax.nn.silu(h @ w_gate) * (h @ w_up)) @ w_down

def hybrid_layer(x, norm_mix, w_in, ssd_conv_w, ssd_conv_b, ssd_dt_bias, ssd_a_log, ssd_d, ssd_norm,
                 lru_conv_w, lru_conv_b, lru_wa, lru_ba, lru_wx, lru_bx, lru_lambda, w_out,
                 norm_ffn, w_gate, w_up, w_down):
    h = rmsnorm_2(x, norm_mix)
    q, k, v, z, xbc, dt_raw, g_lru, x_lru = split_cols(h @ w_in)
    att = dilated_attention(q, k, v).astype(x.dtype)
    ssd = ssd_mixer(z, xbc, dt_raw, ssd_conv_w, ssd_conv_b, ssd_dt_bias, ssd_a_log, ssd_d, ssd_norm).astype(x.dtype)
    lru = rglru_mixer(g_lru, x_lru, lru_conv_w, lru_conv_b, lru_wa, lru_ba, lru_wx, lru_bx, lru_lambda).astype(x.dtype)
    x = x + jnp.concatenate([att, ssd, lru], axis=-1) @ w_out
    x = x + swiglu_2(rmsnorm_2(x, norm_ffn), w_gate, w_up, w_down)
    return x

def second_inputs(seed: int = 0) -> dict:
    key = jax.random.key(seed)
    ks = jax.random.split(key, 24)
    f32 = jnp.float32
    L = DEPTH_2

    def nrm(k, shape, scale):
        return scale * jax.random.normal(k, shape, f32)

    x = nrm(ks[0], (BATCH, SEQ, D_MODEL), 1.0)
    norm_mix = 1.0 + nrm(ks[1], (L, D_MODEL), 0.05)
    w_in = nrm(ks[2], (L, D_MODEL, IN_COLS), D_MODEL ** -0.5)
    ssd_conv_w = nrm(ks[3], (L, CONV_WIDTH, SSD_CONV_CH), CONV_WIDTH ** -0.5)
    ssd_conv_b = nrm(ks[4], (L, SSD_CONV_CH), 0.02)
    dt0 = jnp.exp(jax.random.uniform(ks[5], (L, SSD_HEADS), f32, math.log(DT_MIN), math.log(DT_MAX)))
    ssd_dt_bias = dt0 + jnp.log(-jnp.expm1(-dt0))
    ssd_a_log = jnp.log(jax.random.uniform(ks[6], (L, SSD_HEADS), f32, 1.0, 16.0))
    ssd_d = 1.0 + nrm(ks[7], (L, SSD_HEADS), 0.1)
    ssd_norm = 1.0 + nrm(ks[8], (L, SSD_WIDTH), 0.05)
    lru_conv_w = nrm(ks[9], (L, CONV_WIDTH, LRU_WIDTH), CONV_WIDTH ** -0.5)
    lru_conv_b = nrm(ks[10], (L, LRU_WIDTH), 0.02)
    lru_wa = nrm(ks[11], (L, LRU_BLOCKS, LRU_BLOCK_W, LRU_BLOCK_W), LRU_BLOCK_W ** -0.5)
    lru_ba = nrm(ks[12], (L, LRU_WIDTH), 0.02)
    lru_wx = nrm(ks[13], (L, LRU_BLOCKS, LRU_BLOCK_W, LRU_BLOCK_W), LRU_BLOCK_W ** -0.5)
    lru_bx = nrm(ks[14], (L, LRU_WIDTH), 0.02)
    a_c = jax.random.uniform(ks[15], (L, LRU_WIDTH), f32, 0.9, 0.999)
    a_base = a_c ** (1.0 / LRU_C)
    lru_lambda = jnp.log(a_base) - jnp.log1p(-a_base)
    w_out = nrm(ks[16], (L, D_MIX, D_MODEL), D_MIX ** -0.5)
    norm_ffn = 1.0 + nrm(ks[17], (L, D_MODEL), 0.05)
    w_gate = nrm(ks[18], (L, D_MODEL, D_FF_2), D_MODEL ** -0.5)
    w_up = nrm(ks[19], (L, D_MODEL, D_FF_2), D_MODEL ** -0.5)
    w_down = nrm(ks[20], (L, D_FF_2, D_MODEL), D_FF_2 ** -0.5)
    norm_final = 1.0 + nrm(ks[21], (D_MODEL,), 0.05)
    return {'x': x, 'norm_mix': norm_mix, 'w_in': w_in, 'ssd_conv_w': ssd_conv_w, 'ssd_conv_b': ssd_conv_b,
            'ssd_dt_bias': ssd_dt_bias, 'ssd_a_log': ssd_a_log, 'ssd_d': ssd_d, 'ssd_norm': ssd_norm,
            'lru_conv_w': lru_conv_w, 'lru_conv_b': lru_conv_b, 'lru_wa': lru_wa, 'lru_ba': lru_ba,
            'lru_wx': lru_wx, 'lru_bx': lru_bx, 'lru_lambda': lru_lambda, 'w_out': w_out,
            'norm_ffn': norm_ffn, 'w_gate': w_gate, 'w_up': w_up, 'w_down': w_down, 'norm_final': norm_final}

def second_block(x, norm_mix, w_in, ssd_conv_w, ssd_conv_b, ssd_dt_bias, ssd_a_log, ssd_d, ssd_norm,
              lru_conv_w, lru_conv_b, lru_wa, lru_ba, lru_wx, lru_bx, lru_lambda, w_out,
              norm_ffn, w_gate, w_up, w_down, norm_final):
    for l in range(DEPTH_2):
        x = hybrid_layer(x, norm_mix[l], w_in[l], ssd_conv_w[l], ssd_conv_b[l], ssd_dt_bias[l], ssd_a_log[l],
                         ssd_d[l], ssd_norm[l], lru_conv_w[l], lru_conv_b[l], lru_wa[l], lru_ba[l],
                         lru_wx[l], lru_bx[l], lru_lambda[l], w_out[l], norm_ffn[l], w_gate[l], w_up[l], w_down[l])
    return rmsnorm_2(x, norm_final)


def setup_inputs(seed=0):
    out = dict(first_inputs(seed))
    for name, value in second_inputs(seed + 1).items():
        if name != "x":
            out[name + "_2"] = value
    return out


def reference(
    x, s5_lambda_re, s5_lambda_im, s5_log_dt, s5_b_re, s5_b_im, s5_c_re, s5_c_im, s5_d,
    s5_w_glu, dsa_w_in, dsa_q_norm, dsa_k_norm, dsa_w_o, ffn_w_gate_up, ffn_w_down, norm_mix,
    norm_ffn, norm_mix_2, w_in_2, ssd_conv_w_2, ssd_conv_b_2, ssd_dt_bias_2, ssd_a_log_2,
    ssd_d_2, ssd_norm_2, lru_conv_w_2, lru_conv_b_2, lru_wa_2, lru_ba_2, lru_wx_2, lru_bx_2,
    lru_lambda_2, w_out_2, norm_ffn_2, w_gate_2, w_up_2, w_down_2, norm_final_2,
):
    x = first_block(
        x, s5_lambda_re, s5_lambda_im, s5_log_dt, s5_b_re, s5_b_im, s5_c_re, s5_c_im, s5_d,
        s5_w_glu, dsa_w_in, dsa_q_norm, dsa_k_norm, dsa_w_o, ffn_w_gate_up, ffn_w_down,
        norm_mix, norm_ffn,
    )
    return second_block(
        x, norm_mix_2, w_in_2, ssd_conv_w_2, ssd_conv_b_2, ssd_dt_bias_2, ssd_a_log_2, ssd_d_2,
        ssd_norm_2, lru_conv_w_2, lru_conv_b_2, lru_wa_2, lru_ba_2, lru_wx_2, lru_bx_2,
        lru_lambda_2, w_out_2, norm_ffn_2, w_gate_2, w_up_2, w_down_2, norm_final_2,
    )


_drawn_inputs = setup_inputs


def setup_inputs(seed=0):
    import zlib

    import numpy as np

    out = dict(_drawn_inputs(seed))
    spreads = {}
    factors = {'s5_lambda_re': 52.363,
     'dsa_q_norm': 8.0,
     'dsa_k_norm': 8.0,
     'ssd_conv_b_2': 5.132,
     'ssd_d_2': 4.4,
     'ssd_norm_2': 2.91,
     'lru_ba_2': 64.0,
     'lru_bx_2': 57.412,
     'lru_conv_b_2': 3.732,
     'norm_ffn_2': 3.263}
    for name, (base, spread) in spreads.items():
        noise = np.random.default_rng([zlib.crc32(name.encode()), seed]).standard_normal(out[name].shape)
        drawn = base * np.exp(spread * noise) if base else spread * noise
        out[name] = jnp.asarray(drawn.astype(out[name].dtype))
    for name, factor in factors.items():
        out[name] = (out[name] * factor).astype(out[name].dtype)
    return out
```

```python
import math
from contextlib import ExitStack
from itertools import count

import numpy as np
import concourse.bass as bass
from concourse import mybir

F32 = mybir.dt.float32
F32R = mybir.dt.float32r
ALU = mybir.AluOpType
ACT = mybir.ActivationFunctionType
AX_X = mybir.AxisListType.X

P = 128
D = 1024
T = 512
KT = D // P
TB = T // P
FF = 2816
FT = FF // P
EPS = 1e-6
BIG = 1e30
TAKEN = -3e38

NH, HD, IH = 16, 64, 8
TOPK = 128
SSD_EPS = 1e-5
AH, SH, SG, SN = 8, 8, 2, 128
XT, LT, CW = 8, 4, 4
RATES = ((128, 1), (512, 4), (2048, 16))
GROUP = 512

G, GH, NS = 64, 16, 64
CH = P // GH
NC = T // CH
QG = 16
NQ = G // QG
ROUND = 12582912.0
SIN_SCALE = 6.283185

UNIT = 1024
R = 4
LOOK = 3


def bc(ap, axis, n):
    out = ap.unsqueeze(axis)
    shape = list(out.shape)
    shape[axis] = n
    return out.broadcast_to(shape)


def constant_columns():
    i = np.arange(P)
    cols = {
        "ident": np.eye(P),
        "ones": np.ones((P, P)),
        "tri": i[:, None] <= i[None, :],
        "causal": np.where(i[None, :] <= i[:, None], 0.0, -BIG),
        "causal_t": np.where(i[:, None] <= i[None, :], 0.0, -BIG),
        "same_token": (i[:, None] // GH) == (i[None, :] // GH),
        "tau": np.broadcast_to(np.arange(CH + 1), (P, CH + 1)),
        "chunk": np.broadcast_to(np.arange(NC) - 1, (P, NC)),
        "carry": np.broadcast_to(np.arange(NC) > 0, (P, NC)),
        "sign": np.stack([np.where(i < NS, -1, 1), np.where(i < NS, 1, -1)], 1),
        "eps": np.full((P, 1), EPS),
        "eps_ssd": np.full((P, 1), SSD_EPS),
    }
    return {k: np.asarray(v, np.float32) for k, v in cols.items()}


def rope_tables():
    f = np.float32
    inv = f(10000.0) ** (-np.arange(0, HD, 2, dtype=f) / f(HD))
    a = np.arange(T, dtype=f)[:, None] * inv[None, :].astype(f)
    t = np.stack([np.cos(a), np.sin(a)]).astype(f)
    return np.concatenate([t, t], -1).reshape(2, TB, P, HD).transpose(2, 0, 1, 3)


def dilated_bias():
    dist = np.arange(P)[:, None] + (T - P) - np.arange(T)[None, :]
    count = sum(((dist % rate == 0) & (dist <= span)).astype(np.float64) for span, rate in RATES)
    count = np.where(dist >= 0, count, 0)
    slopes = 2.0 ** (-8.0 * np.arange(1, AH + 1) / AH)
    bias = -slopes[:, None, None] * dist + np.log(np.maximum(count, 1))
    return np.where(count > 0, 8 * bias, -BIG).astype(np.float32).transpose(1, 0, 2)


CONST_WIDTH = {k: v.shape[1] for k, v in constant_columns().items()}
CONST_AT = dict(zip(CONST_WIDTH, np.cumsum([0, *CONST_WIDTH.values()]).tolist()))
N_CONST = sum(CONST_WIDTH.values())

VEC = {"norm_ffn0": KT, "norm_mix1": KT, "norm_ffn1": KT, "norm_mix2": KT, "norm_ffn2": KT, "norm_final": KT}
VEC_AT = dict(zip(VEC, np.cumsum([0, *VEC.values()]).tolist()))
N_VEC = sum(VEC.values())

PHASES = {"glu": 2 * KT, "gu0": 2 * FT, "down0": FT, "dsa": 4 * 7 + 1, "wo": KT, "gu1": 2 * FT, "down1": FT,
          "mix": 33, "out": 12, "gu2": 2 * FT, "down2": FT}
FIRST = dict(zip(PHASES, np.cumsum([0, *PHASES.values()]).tolist()))
N_UNITS = sum(PHASES.values())


def build(nc, d, out):
    ctx = ExitStack()
    with ctx:
        def sem(name):
            return ctx.enter_context(nc.semaphore(name))

        base = (nc.sbuf_base + 63) // 64 * 64
        end = nc.sbuf_usable_end

        def at(name, shape, offset, dt=F32):
            return nc.alloc_sbuf_tensor_at(name, [P, *shape], dt, offset=offset)

        KB = 1024
        RAW, HI, LO = base, base + 16 * KB, base + 32 * KB
        X = base + 48 * KB
        CST = X + 16 * KB
        SCR = CST + 4 * KB
        HT = SCR + 12 * KB
        BIGR = HT + 32 * KB
        assert end - BIGR >= 95 * KB, (end - BIGR)

        raw = [at(f"raw{s}", [UNIT], RAW + 4 * KB * s) for s in range(R)]
        w_hi = [at(f"w_hi{s}", [UNIT], HI + 4 * KB * s, F32R) for s in range(R)]
        w_lo = [at(f"w_lo{s}", [UNIT], LO + 4 * KB * s, F32R) for s in range(R)]
        xT = at("xT", [KT, T], X)
        cst = at("cst", [N_CONST], CST)
        vec = at("vec", [N_VEC], CST + 32 * (-(-N_CONST // 8)))
        assert 4 * (N_CONST + N_VEC + 8) <= 4 * KB, (N_CONST, N_VEC)
        acc = at("acc", [T], SCR)
        sq = [at(f"sq{s}", [T], SCR + 2 * KB * (1 + s)) for s in range(2)]
        rstd = at("rstd", [T], SCR + 6 * KB)
        t32 = [at(f"t32{s}", [T], SCR + 2 * KB * (4 + s)) for s in range(2)]
        h_hi = at("h_hi", [KT, T], HT, F32R)
        h_lo = at("h_lo", [KT, T], HT + 16 * KB, F32R)
        hid_hi = at("hid_hi", [FT, T], BIGR, F32R)
        hid_lo = at("hid_lo", [FT, T], BIGR + 2 * KB * FT, F32R)
        ps = ctx.enter_context(nc.psum_tensor("ps", [P, 8, T], F32))

        def const(name):
            return cst[:, CONST_AT[name]:CONST_AT[name] + CONST_WIDTH[name]]

        ident, ones, eps = const("ident"), const("ones"), const("eps")

        raw_landed = [sem(f"raw_landed{s}") for s in range(R)]
        hi_ready = sem("w_hi_ready")
        lo_ready = sem("w_lo_ready")
        unit_used = sem("unit_used")
        consts_landed = sem("consts_landed")

        def after(s, before=0):
            return lambda n: (s, n + before)

        def unit(k, it=None, per=R):
            if it is None:
                return k % R, k, k // R + 1
            return k % R, it * per + k, it * (per // R) + (k // R + 1)

        def load_units(sp, phase, view):
            n0, n = FIRST[phase], PHASES[phase]
            head = n % R if n0 else R

            def load(k, src, it=None):
                slot, number, _ = unit(k, it)
                if it is not None or k >= R:
                    sp.wait_ge(lo_ready, number - (R - 1))
                sp.dma_start(raw[slot][:], src).then_inc(raw_landed[slot], 16)

            for u in range(head):
                load(n0 + u, view[u])
            if n - head:
                with sp.Fori(0, (n - head) // R) as it:
                    for u in range(R):
                        load(n0 + head + u, view[bass.ds(it * R + (head + u), 1)].rearrange("a p n -> p (a n)"), it)
            assert (n - head) % R == 0

        def split_hi(act, k, it=None, per=R):
            if it is None and k >= N_UNITS:
                return
            slot, number, use = unit(k, it, per)
            act.wait_ge(raw_landed[slot], use * 16)
            if it is not None or k >= R:
                act.wait_ge(unit_used, number - (R - 2))
            act.activation(w_hi[slot][:], raw[slot][:], ACT.Copy).then_inc(hi_ready, 1)

        def split_lo_all(pool):
            def one(k, it=None):
                slot, number, _ = unit(k, it)
                pool.wait_ge(hi_ready, number + 1)
                pool.tensor_tensor(w_lo[slot][:], raw[slot][:], w_hi[slot][:].bitcast(F32), ALU.subtract)\
                    .then_inc(lo_ready, 1)
            with pool.Fori(0, N_UNITS // R) as it:
                for k in range(R):
                    one(k, it)
            for k in range(N_UNITS // R * R, N_UNITS):
                one(k)

        def mm3(pe, o, wh, wl, ah, al, start, stop):
            pe.matmul(o, wh, ah, start=start, stop=False)
            pe.matmul(o, wh, al, start=False, stop=False)
            return pe.matmul(o, wl, ah, start=False, stop=stop)

        RING = RAW
        xs = at("s5_x", [G, NC], X)
        s5_par = at("s5_par", [4, G], RING)
        braw = at("s5_b", [2, G * GH], RING + 1 * KB)
        craw = at("s5_c", [2, G * GH], RING + 9 * KB)
        bbar = at("s5_bbar", [2, G * GH], RING + 17 * KB)
        NT9 = (CH + 1) * G * 4
        pw = [at(f"s5_pw{n}", [CH + 1, G], RING + 25 * KB + NT9 * n) for n in range(7)]
        turn, pw_re, pw_im, pw_ims, pw_re2, pw_imn, wave = pw
        small = at("s5_small", [16, G], RING + 25 * KB + NT9 * 7)
        assert 25 * KB + NT9 * 7 + 16 * G * 4 <= 48 * KB
        dskip = at("s5_dskip", [G], BIGR + 94 * KB)
        o5 = [BIGR]

        def s5buf(name, shape):
            off = o5[0]
            o5[0] += 4 * int(np.prod(shape))
            assert o5[0] <= BIGR + 94 * KB, name
            return at(name, shape, off)

        winT = s5buf("s5_winT", [QG, CH, GH])
        wtmp = s5buf("s5_wtmp", [QG // 2, CH, GH])
        win = s5buf("s5_win", [QG, P + NS])
        wout = s5buf("s5_wout", [QG, CH, GH])
        wotmp = s5buf("s5_wotmp", [QG // 2, CH, GH])
        toep = s5buf("s5_toep", [CH, QG, GH])
        ang = s5buf("s5_ang", [QG, NC])
        sin_t = s5buf("s5_sin", [QG, NC])
        cos_t = s5buf("s5_cos", [QG, NC])
        decay = s5buf("s5_decay", [QG, NC])
        zin = s5buf("s5_zin", [QG, NC])
        zst = s5buf("s5_zst", [QG, NC])
        ztmp = s5buf("s5_ztmp", [QG, NC])
        u_q = s5buf("s5_u", [QG, NC])
        conv = s5buf("s5_conv", [QG, GH])
        dI = s5buf("s5_dI", [G, GH])
        y_q = s5buf("s5_y", [CH, QG * GH])
        cxn = s5buf("s5_cxn", [G * GH])
        sumsq = at("s5_sumsq", [NC], SCR)
        rstd5 = at("s5_rstd", [NC], SCR + 256)
        xsq = at("s5_xsq", [G, NC], BIGR)
        lam_re, lam_im, log_dt, gain5 = (s5_par[:, n, :] for n in range(4))

        S = {n: sem("s5_" + n) for n in (
            "par_landed", "bc_landed", "x_landed", "dt", "turn", "mag", "wave", "powers", "xsq", "sumsq", "sumps",
            "std", "prologue", "winT_ready", "winT_free", "psT_ready", "psT_free", "win_free", "convps",
            "conv_copied", "conv_ready", "toep_landed", "zeroed", "ang_ready", "ang_reduced", "sin_ready",
            "half_ready", "decay_ready", "decay_free", "u_ready", "w_ready", "w_free", "s_ready", "wout_ready",
            "y_done", "y_evac", "yT_begun", "yT_ready", "yT_free", "gelu_ready", "yhi_ready", "ylo_ready", "xT_landed")}
        N_SHIFT = CH * (CH + 1) // 2

        def s5_sync(sp):
            sp.dma_start(s5_par[:], d["s5_par"]).then_inc(S["par_landed"], 16)
            sp.dma_start(cst[:], d["cst"]).then_inc(consts_landed, 16)
            sp.dma_start(vec[:], d["vec"]).then_inc(consts_landed, 16)
            sp.dma_start(xs[:], d["xs5"]).then_inc(S["x_landed"], 16)
            sp.dma_start(braw[:], d["s5_b"]).then_inc(S["bc_landed"], 16)
            sp.dma_start(craw[:], d["s5_c"]).then_inc(S["bc_landed"], 16)
            sp.dma_start(dskip[0:GH, :], d["s5_d"]).then_inc(S["bc_landed"], 16)
            sp.wait_ge(S["zeroed"], 1)
            with sp.Fori(0, NQ) as q:
                sp.wait_ge(S["conv_ready"], q + 1)
                sp.wait_ge(S["y_done"], q * 4 + 1)
                for r in range(CH):
                    for tau in range(r + 1):
                        sp.dma_start(toep[GH * r:GH * (r + 1), tau + CH - 1 - r, :, :],
                                     conv[GH * tau:GH * (tau + 1), :, :]).then_inc(S["toep_landed"], 16)
            sp.wait_ge(S["u_ready"], NQ)
            sp.dma_start(xT[:], d["xT"]).then_inc(S["xT_landed"], 16)
            sp.wait_ge(S["winT_ready"], NQ)
            sp.wait_ge(S["wout_ready"], NQ)
            sp.wait_ge(S["decay_ready"], NQ)

        def s5_gpsimd(pool):
            pool.memset(toep[:], 0.0).then_inc(S["zeroed"], 1)
            pool.wait_ge(consts_landed, 32)
            pool.wait_ge(S["bc_landed"], 48)
            pool.wait_ge(S["powers"], 1)
            cx = craw[:, 0, :].rearrange("p (g h) -> p g h", h=GH)
            cy = craw[:, 1, :].rearrange("p (g h) -> p g h", h=GH)
            H = QG // 2
            with pool.Fori(0, NQ) as q:
                gs = bass.ds(q * QG, QG)
                pool.wait_ge(S["decay_free"], q + 1)
                pool.tensor_tensor(ang[:], bc(turn[:, CH, gs], 2, NC), bc(const("chunk"), 1, QG), ALU.mult)\
                    .then_inc(S["ang_ready"], 1)
                pool.tensor_tensor(decay[:], bc(wave[:, CH, gs], 2, NC), bc(const("carry"), 1, QG), ALU.mult)\
                    .then_inc(S["decay_ready"], 1)
                pool.wait_ge(S["y_done"], q * 4 + 1)
                for half in range(2):
                    hs = bass.ds(q * QG + half * H, H)
                    o = wout[:, half * H:(half + 1) * H, :, :]
                    pool.tensor_tensor(o, bc(pw_re2[:, 1:CH + 1, hs].rearrange("p t g -> p g t"), 3, GH),
                                       bc(cx[:, hs, :], 2, CH), ALU.mult)
                    pool.tensor_tensor(wotmp[:], bc(pw_imn[:, 1:CH + 1, hs].rearrange("p t g -> p g t"), 3, GH),
                                       bc(cy[:, hs, :], 2, CH), ALU.mult)
                    pool.drain()
                    last = pool.tensor_tensor(o, o, wotmp[:], ALU.add)
                    if half == 0:
                        pool.drain()
                last.then_inc(S["wout_ready"], 1)

        def s5_scalar(act):
            act.sem_inc(S["psT_free"], 2)
            act.wait_ge(S["par_landed"], 16)
            act.activation(small[:, 0, :], log_dt, ACT.Exp).then_inc(S["dt"], 1)
            act.wait_ge(S["x_landed"], 16)
            act.activation(xsq[:], xs[:], ACT.Square).then_inc(S["xsq"], 1)
            act.wait_ge(S["turn"], 1)
            act.activation(wave[:], wave[:], ACT.Exp).then_inc(S["mag"], 1)
            act.activation(pw_im[:], turn[:], ACT.Sin, scale=SIN_SCALE)
            act.activation(pw_re[:], turn[:], ACT.Sin, scale=SIN_SCALE / 2)
            act.drain()
            act.activation(pw_re[:], pw_re[:], ACT.Square).then_inc(S["wave"], 1)
            act.wait_ge(S["sumps"], 1)
            act.wait_ge(consts_landed, 32)
            act.activation(rstd5[:], ps[:, 7, 0:NC], ACT.Sqrt, bias=eps, scale=1.0 / D).then_inc(S["std"], 1)
            with act.Fori(0, NQ) as q:
                act.wait_ge(S["ang_reduced"], q + 1)
                act.activation(sin_t[:], ang[:], ACT.Sin, scale=SIN_SCALE).then_inc(S["sin_ready"], 1)
                act.activation(cos_t[:], ang[:], ACT.Sin, scale=SIN_SCALE / 2)
                act.drain()
                act.activation(cos_t[:], cos_t[:], ACT.Square).then_inc(S["half_ready"], 1)
                act.wait_ge(S["win_free"], q + 1)
                for b in range(QG // 4):
                    act.wait_ge(S["psT_ready"], q * 4 + (b + 1))
                    src = ps[:, b % 2, :].rearrange("p (g n) -> p g n", g=4)
                    act.activation(win[:, 4 * b:4 * b + 4, 0:P], src, ACT.Copy)
                    act.activation(win[:, 4 * b:4 * b + 4, P:P + NS], src[:, :, 0:NS], ACT.Copy, scale=-1.0)\
                        .then_inc(S["psT_free"], 1)
                act.wait_ge(S["convps"], q + 1)
                act.wait_ge(S["toep_landed"], q * (16 * N_SHIFT) + 16)
                act.activation(conv[:], ps[:, 2, 0:QG * GH].rearrange("p (g h) -> p g h", g=QG), ACT.Copy)\
                    .then_inc(S["conv_copied"], 1)
                for b in range(QG // 4):
                    act.wait_ge(S["y_done"], q * 4 + (b + 2))
                    act.activation(y_q[0:NC, :, 64 * b:64 * (b + 1)].rearrange("p t (g h) -> p g t h", g=4),
                                   ps[0:NC, b % 2, :].rearrange("p (g t h) -> p g t h", g=4, t=CH), ACT.Copy)\
                        .then_inc(S["y_evac"], 1)
                for m in range(2):
                    act.wait_ge(S["yT_ready"], q * 2 + (m + 1))
                    if m == 0:
                        act.wait_ge(S["yT_free"], q + 1)
                    act.activation(t32[m][:].rearrange("p (c t) -> p t c", t=CH), ps[:, 7, :].rearrange("p (t c) -> p t c", t=CH),
                                   ACT.Gelu_apprx_tanh).then_inc(S["gelu_ready"], 1)
                    act.drain()
                    act.activation(h_hi[:, bass.ds(q * 2 + m, 1), :], t32[m][:].unsqueeze(1), ACT.Copy).then_inc(S["yhi_ready"], 1)

        def s5_vector(dve):
            dve.sem_inc(S["decay_free"], 1)
            dve.sem_inc(S["yT_free"], 1)
            dve.sem_inc(S["w_free"], 1)
            rho, phi, f1, k1 = (small[:, n, :] for n in (1, 2, 3, 4))
            dve.wait_ge(S["dt"], 1)
            dve.tensor_tensor(rho, lam_re, small[:, 0, :], ALU.mult)
            dve.tensor_tensor(phi, lam_im, small[:, 0, :], ALU.mult)
            dve.drain()
            dve.tensor_scalar(f1, phi, 1.0 / (2 * math.pi), None, ALU.mult)
            dve.wait_ge(consts_landed, 32)
            tau = bc(const("tau"), 2, G)
            dve.tensor_tensor(wave[:], bc(rho, 1, CH + 1), tau, ALU.mult)
            dve.drain()
            dve.tensor_scalar(k1, f1, ROUND, -ROUND, ALU.add, ALU.add)
            dve.drain()
            dve.tensor_tensor(f1, f1, k1, ALU.subtract)
            dve.drain()
            dve.tensor_tensor(turn[:], bc(f1, 1, CH + 1), tau, ALU.mult)
            dve.drain()
            dve.tensor_scalar(pw_imn[:], turn[:], ROUND, -ROUND, ALU.add, ALU.add)
            dve.drain()
            dve.tensor_tensor(turn[:], turn[:], pw_imn[:], ALU.subtract).then_inc(S["turn"], 1)
            dve.wait_ge(S["xsq"], 1)
            dve.tensor_reduce(sumsq[:], xsq[:].rearrange("p g c -> p c g"), AX_X, ALU.add).then_inc(S["sumsq"], 1)
            dve.wait_ge(S["wave"], 1)
            dve.tensor_scalar(pw_re[:], pw_re[:], -2.0, 1.0, ALU.mult, ALU.add)
            dve.tensor_tensor(pw_im[:], pw_im[:], wave[:], ALU.mult)
            dve.drain()
            dve.tensor_tensor(pw_re[:], pw_re[:], wave[:], ALU.mult)
            sg = const("sign")
            dve.tensor_scalar(pw_ims[:], pw_im[:], sg[:, 0:1], None, ALU.mult)
            dve.tensor_scalar(pw_imn[:], pw_im[:], -1.0, None, ALU.mult)
            dve.drain()
            dve.tensor_scalar(pw_re2[:], pw_re[:], sg[:, 1:2], None, ALU.mult).then_inc(S["powers"], 1)
            a1, den, t0, t1, qr, qi, t2, t3 = (small[:, n, :] for n in range(5, 13))
            ai = pw_im[:, 1, :]
            dve.tensor_scalar(a1, pw_re[:, 1, :], -1.0, None, ALU.add)
            dve.tensor_tensor(t0, lam_re, lam_re, ALU.mult)
            dve.tensor_tensor(t1, lam_im, lam_im, ALU.mult)
            dve.drain()
            dve.tensor_tensor(den, t0, t1, ALU.add)
            dve.tensor_tensor(t2, ai, lam_re, ALU.mult)
            dve.tensor_tensor(t3, a1, lam_im, ALU.mult)
            dve.drain()
            dve.reciprocal(den, den)
            dve.tensor_tensor(t0, a1, lam_re, ALU.mult)
            dve.tensor_tensor(t1, ai, lam_im, ALU.mult)
            dve.tensor_tensor(qi, t2, t3, ALU.subtract)
            dve.drain()
            dve.tensor_tensor(qr, t0, t1, ALU.add)
            dve.tensor_tensor(qi, qi, den, ALU.mult)
            dve.drain()
            dve.tensor_tensor(qr, qr, den, ALU.mult)
            dve.tensor_scalar(qi, qi, sg[:, 0:1], None, ALU.mult)
            dve.drain()
            dve.wait_ge(S["bc_landed"], 48)
            b0, b1 = (braw[:, n, :].rearrange("p (g h) -> p g h", h=GH) for n in range(2))
            bx, by = (bbar[:, n, :].rearrange("p (g h) -> p g h", h=GH) for n in range(2))
            c0 = craw[:, 0, :]
            scr = wtmp[:].rearrange("p g t h -> p (g t h)").rearrange("p (g h) -> p g h", h=GH)
            scr2 = y_q[:].rearrange("p t n -> p (t n)")[:, 0:G * GH].rearrange("p (g h) -> p g h", h=GH)
            dve.tensor_tensor(bx, b0, bc(qr, 2, GH), ALU.mult)
            dve.tensor_tensor(by, b1, bc(qr, 2, GH), ALU.mult)
            dve.tensor_tensor(scr, b1, bc(qi, 2, GH), ALU.mult)
            dve.tensor_tensor(scr2, b0, bc(qi, 2, GH), ALU.mult)
            dve.tensor_scalar(cxn[:], c0, sg[:, 1:2], None, ALU.mult)
            dve.tensor_tensor(dI[0:GH, :, :], bc(dskip[0:GH, :], 2, GH), bc(ident[0:GH, 0:GH], 1, G), ALU.mult)
            dve.drain()
            dve.tensor_tensor(bx, bx, scr, ALU.add)
            dve.tensor_tensor(by, by, scr2, ALU.subtract)
            dve.memset(zin[:], 0.0)
            dve.wait_ge(S["std"], 1)
            dve.reciprocal(rstd5[:], rstd5[:])
            dve.drain().then_inc(S["prologue"], 1)
            H = QG // 2
            with dve.Fori(0, NQ) as q:
                gs = bass.ds(q * QG, QG)
                dve.wait_ge(S["winT_free"], q + 1)
                dve.tensor_tensor(winT[:], bc(pw_re[:, 0:CH, gs].rearrange("p t g -> p g t"), 3, GH),
                                  bc(bx[:, gs, :], 2, CH), ALU.mult)
                for half in range(2):
                    hs = bass.ds(q * QG + half * H, H)
                    o = winT[:, half * H:(half + 1) * H, :, :]
                    dve.tensor_tensor(wtmp[:], bc(pw_ims[:, 0:CH, hs].rearrange("p t g -> p g t"), 3, GH),
                                      bc(by[:, hs, :], 2, CH), ALU.mult)
                    dve.drain()
                    last = dve.tensor_tensor(o, o, wtmp[:], ALU.add)
                    if half == 0:
                        dve.drain()
                last.then_inc(S["winT_ready"], 1)
                dve.wait_ge(S["ang_ready"], q + 1)
                dve.tensor_scalar(ztmp[:], ang[:], ROUND, -ROUND, ALU.add, ALU.add)
                dve.drain()
                dve.tensor_tensor(ang[:], ang[:], ztmp[:], ALU.subtract).then_inc(S["ang_reduced"], 1)
                dve.wait_ge(S["y_done"], q * 4 + 1)
                dve.tensor_tensor(u_q[:], xs[:, gs, :], bc(rstd5[:], 1, QG), ALU.mult)
                dve.drain()
                dve.tensor_tensor(u_q[:], u_q[:], bc(gain5[:, gs], 2, NC), ALU.mult).then_inc(S["u_ready"], 1)
                dve.wait_ge(S["conv_copied"], q + 1)
                dve.tensor_tensor(conv[0:GH, :, :], conv[0:GH, :, :], dI[0:GH, gs, :], ALU.add)
                dve.drain().then_inc(S["conv_ready"], 1)
                dve.wait_ge(S["half_ready"], q + 1)
                dve.tensor_scalar(cos_t[:], cos_t[:], -2.0, 1.0, ALU.mult, ALU.add)
                dve.drain()
                dve.wait_ge(S["w_ready"], q + 1)
                n1 = NC - 1
                wv = ps[:, 3:5, :].rearrange("p b (g c) -> p (b g) c", c=NC)
                wsw = ps[:, 5:7, :].rearrange("p b (g c) -> p (b g) c", c=NC)
                dve.tensor_tensor(zin[:, :, 1:NC], wv[:, :, 0:n1], cos_t[:, :, 1:NC], ALU.mult)
                dve.tensor_tensor(ztmp[:, :, 1:NC], wsw[:, :, 0:n1], sin_t[:, :, 1:NC], ALU.mult).then_inc(S["w_free"], 1)
                dve.drain()
                dve.tensor_tensor(zin[:, :, 1:NC], zin[:, :, 1:NC], ztmp[:, :, 1:NC], ALU.add)
                dve.drain()
                dve.wait_ge(S["decay_ready"], q + 1)
                dve.tensor_tensor_scan(zst[:].rearrange("p g c -> p (g c)"), decay[:].rearrange("p g c -> p (g c)"),
                                       zin[:].rearrange("p g c -> p (g c)"), 0.0, ALU.mult, ALU.add)
                dve.drain()
                dve.tensor_tensor(zin[:], zst[:], cos_t[:], ALU.mult)
                dve.tensor_tensor(ztmp[NS:P, :, :], zst[0:NS, :, :], sin_t[0:NS, :, :], ALU.mult)
                dve.scalar_tensor_tensor(ztmp[0:NS, :, :], zst[NS:P, :, :], -1.0, sin_t[NS:P, :, :], ALU.mult, ALU.mult)\
                    .then_inc(S["decay_free"], 1)
                dve.drain()
                dve.tensor_tensor(zin[:], zin[:], ztmp[:], ALU.add).then_inc(S["s_ready"], 1)
                for m in range(2):
                    dve.wait_ge(S["yhi_ready"], q * 2 + (m + 1))
                    at_ = bass.ds(q * 2 + m, 1)
                    dve.tensor_tensor(h_lo[:, at_, :], t32[m][:].unsqueeze(1), h_hi[:, at_, :].bitcast(F32), ALU.subtract)\
                        .then_inc(S["ylo_ready"], 1)
                dve.drain().then_inc(S["yT_free"], 1)

        def s5_tensor(pe):
            for n in ("winT_free", "win_free", "y_done", "y_evac", "gelu_ready"):
                pe.sem_inc(S[n], 1)
            pe.sem_inc(S["toep_landed"], 16)
            pe.wait_ge(consts_landed, 32)
            pe.wait_ge(S["sumsq"], 1)
            pe.matmul(ps[:, 7, 0:NC], const("same_token"), sumsq[:], start=True, stop=True).then_inc(S["sumps"], 1)
            pe.wait_ge(S["prologue"], 1)
            with pe.Fori(0, NQ) as q:
                pe.wait_ge(S["winT_ready"], q + 1)
                pe.wait_ge(S["y_evac"], q * 4 + 1)
                for b in range(QG // 4):
                    pe.wait_ge(S["psT_free"], q * 4 + (b + 1))
                    for g in range(4 * b, 4 * b + 4):
                        last = pe.transpose(ps[:, b % 2, (g % 4) * P:(g % 4 + 1) * P],
                                            winT[:, g, :, :].rearrange("p t h -> p (t h)"), ident)
                    last.then_inc(S["psT_ready"], 1)
                for g in range(QG):
                    last = pe.matmul(ps[:, 2, g * GH:(g + 1) * GH], winT[:, g, :, :].rearrange("p t h -> p (t h)"),
                                     cxn[:].rearrange("p (g h) -> p g h", h=GH)[:, bass.ds(q * QG + g, 1), :].rearrange("p a h -> p (a h)"),
                                     start=True, stop=True)
                last.then_inc(S["convps"], 1)
                pe.wait_ge(S["u_ready"], q + 1)
                pe.wait_ge(S["w_free"], q + 1)
                pe.wait_ge(S["psT_free"], q * 4 + 6)
                for g in range(QG):
                    for bank, c0 in ((3, 0), (5, NS)):
                        last = pe.matmul(ps[:, bank + g // 8, (g % 8) * NC:(g % 8 + 1) * NC], win[:, g, c0:c0 + P],
                                         u_q[:, g, :], start=True, stop=True)
                last.then_inc(S["w_ready"], 1)
                pe.wait_ge(S["toep_landed"], q * (16 * N_SHIFT) + (16 * N_SHIFT + 16))
                pe.wait_ge(S["wout_ready"], q + 1)
                pe.wait_ge(S["s_ready"], q + 1)
                for b in range(QG // 4):
                    if b >= 2:
                        pe.wait_ge(S["y_evac"], q * 4 + b)
                    for g in range(4 * b, 4 * b + 4):
                        o = ps[0:NC, b % 2, (g % 4) * P:(g % 4 + 1) * P]
                        pe.matmul(o, u_q[:, g, :], toep[:, :, g, :], start=True, stop=False)
                        last = pe.matmul(o, zin[:, g, :], wout[:, g, :, :], start=False, stop=True)
                    last.then_inc(S["y_done"], 1)
                for m in range(2):
                    pe.wait_ge(S["y_evac"], q * 4 + 5)
                    pe.wait_ge(S["gelu_ready"], q * 2 + (m + 1))
                    pe.sem_inc(S["yT_begun"], 1)
                    for t in range(CH):
                        last = pe.transpose(ps[:, 7, t * NC:(t + 1) * NC], y_q[0:NC, t, m * P:(m + 1) * P], ident[0:NC, 0:NC])
                    last.then_inc(S["yT_ready"], 1)
                pe.sem_inc(S["winT_free"], 1)
                pe.sem_inc(S["win_free"], 1)

        def done(number):
            return number + 2

        class Gated:
            gate_done = sem("gate_done")
            pair_done = sem("pair_done")
            part_hi = sem("part_hi")
            out_ready = sem("pair_ready")

            def __init__(self, before, name, pairs, in_ready):
                self.before = before
                self.name, self.pairs, self.in_ready = name, pairs, in_ready

        def gated_tensor(pe, ph):
            with pe.Fori(0, ph.pairs // 2) as it:
                for jj in range(2):
                    pe.wait_ge(ph.pair_done, it * 2 + (ph.before + jj + 1))
                    for half in range(2):
                        slot, number, _ = unit(FIRST[ph.name] + 2 * jj + half, it)
                        pe.wait_ge(lo_ready, number + 1)
                        for kt in range(KT):
                            if jj == 0 and half == 0:
                                pe.wait_ge(*ph.in_ready(kt + 1))
                            cols = slice(kt * P, (kt + 1) * P)
                            last = mm3(pe, ps[:, 2 * jj + half, :], w_hi[slot][:, cols], w_lo[slot][:, cols],
                                       h_hi[:, kt, :], h_lo[:, kt, :], kt == 0, kt == KT - 1)
                        last.then_inc(unit_used, 1)

        def ffn_scalar(act, ph):
            with act.Fori(0, ph.pairs // 2) as it:
                for jj in range(2):
                    k = FIRST[ph.name] + 2 * jj
                    split_hi(act, k + LOOK, it)
                    split_hi(act, k + 1 + LOOK, it)
                    act.wait_ge(ph.pair_done, it * 2 + (ph.before + jj + 1))
                    act.wait_ge(unit_used, done(unit(k, it)[1]))
                    act.activation(sq[jj][:], ps[:, 2 * jj, :], ACT.Silu).then_inc(ph.gate_done, 1)
                    act.wait_ge(ph.pair_done, it * 2 + (ph.before + jj + 3))
                    act.activation(hid_hi[:, bass.ds(it * 2 + jj, 1), :], t32[jj][:].unsqueeze(1), ACT.Copy)\
                        .then_inc(ph.part_hi, 1)

        def ffn_vector(dve, ph):
            with dve.Fori(0, ph.pairs // 2) as it:
                for jj in range(2):
                    k = FIRST[ph.name] + 2 * jj
                    dve.wait_ge(ph.gate_done, it * 2 + (ph.before + jj + 1))
                    dve.wait_ge(unit_used, done(unit(k + 1, it)[1]))
                    dve.tensor_tensor(t32[jj][:], ps[:, 2 * jj + 1, :], sq[jj][:], ALU.mult).then_inc(ph.pair_done, 1)
                    dve.wait_ge(ph.part_hi, it * 2 + (ph.before + jj + 1))
                    at_ = bass.ds(it * 2 + jj, 1)
                    dve.tensor_tensor(hid_lo[:, at_, :], t32[jj][:].unsqueeze(1), hid_hi[:, at_, :].bitcast(F32),
                                      ALU.subtract).then_inc(ph.out_ready, 1)

        def glu_scalar(act, ph):
            with act.Fori(0, ph.pairs // 2) as it:
                for jj in range(2):
                    k = FIRST[ph.name] + 2 * jj
                    split_hi(act, k + LOOK, it)
                    split_hi(act, k + 1 + LOOK, it)
                    act.wait_ge(ph.pair_done, it * 2 + (ph.before + jj + 1))
                    act.wait_ge(unit_used, done(unit(k, it)[1]))
                    act.activation(t32[jj][:], ps[:, 2 * jj, :], ACT.Sigmoid).then_inc(ph.gate_done, 1)
                    act.wait_ge(ph.pair_done, it * 2 + (ph.before + jj + 3))
                    act.activation(sq[jj][:], xT[:, bass.ds(it * 2 + jj, 1), :].rearrange("p a t -> p (a t)"), ACT.Square)\
                        .then_inc(ph.part_hi, 1)

        def glu_vector(dve, ph):
            dve.sem_inc(ph.pair_done, 2)
            dve.memset(acc[:], 0.0)
            dve.wait_ge(S["xT_landed"], 16)
            with dve.Fori(0, ph.pairs // 2) as it:
                for jj in range(2):
                    k = FIRST[ph.name] + 2 * jj
                    tile = xT[:, bass.ds(it * 2 + jj, 1), :].rearrange("p a t -> p (a t)")
                    dve.wait_ge(ph.gate_done, it * 2 + (ph.before + jj + 1))
                    dve.wait_ge(unit_used, done(unit(k + 1, it)[1]))
                    dve.tensor_tensor(t32[jj][:], ps[:, 2 * jj + 1, :], t32[jj][:], ALU.mult)
                    dve.drain()
                    dve.tensor_tensor(tile, tile, t32[jj][:], ALU.add).then_inc(ph.pair_done, 1)
                    dve.wait_ge(ph.part_hi, it * 2 + (ph.before + jj + 1))
                    dve.tensor_tensor(acc[:], acc[:], sq[jj][:], ALU.add).then_inc(ph.out_ready, 1)

        class Rows:

            tile_done = sem("rows_tile_done")
            x_ready = sem("rows_x_ready")
            sq_ready = sem("rows_sq_ready")
            acc_ready = sem("rows_acc_ready")

            def __init__(self, nth, name, k_tiles, src_hi, src_lo, in_ready):
                self.before = nth * KT
                self.name, self.k_tiles, self.src_hi, self.src_lo, self.in_ready = name, k_tiles, src_hi, src_lo, in_ready

        def rows_tensor(pe, ph, banks):
            n0, n = FIRST[ph.name], ph.k_tiles

            def products(k, kt, o, it=None, start=False, stop=False):
                slot = k % R
                cols = slice(o * P, (o + 1) * P)
                if it is None:
                    ah, al = ph.src_hi[:, kt, :], ph.src_lo[:, kt, :]
                else:
                    one = bass.ds(it * R + kt, 1)
                    ah, al = (s[:, one, :].rearrange("p a t -> p (a t)") for s in (ph.src_hi, ph.src_lo))
                return mm3(pe, ps[:, o, :], w_hi[slot][:, cols], w_lo[slot][:, cols], ah, al, start, stop)

            def whole(kt, it=None):
                _, number, _ = unit(n0 + kt, it)
                pe.wait_ge(lo_ready, number + 1)
                pe.wait_ge(*ph.in_ready((kt if it is None else it * R + kt) + 1))
                for o, wait in banks if kt == 0 and it is None else [(o, None) for o in range(KT)]:
                    if wait is not None:
                        pe.wait_ge(*wait)
                    last = products(n0 + kt, kt, o, it, start=(kt == 0 and it is None))
                last.then_inc(unit_used, 1)

            head = (n - R) % R or R
            for kt in range(head):
                whole(kt)
            if n - R > head:
                with pe.Fori(0, (n - R - head) // R) as it:
                    for kt in range(R):
                        whole(head + kt, it)
            pe.wait_ge(lo_ready, n0 + n)
            pe.wait_ge(*ph.in_ready(n))
            for o in range(KT):
                for kt in range(n - R, n):
                    last = products(n0 + kt, kt, o, stop=(kt == n - 1))
                last.then_inc(ph.tile_done, 1)
            pe.sem_inc(unit_used, R)

        def rows_scalar(act, ph):
            n0, n = FIRST[ph.name], ph.k_tiles
            head = (n - R) % R or R
            for kt in range(head):
                split_hi(act, n0 + kt + LOOK)
            if n - R > head:
                with act.Fori(0, (n - R - head) // R) as it:
                    for kt in range(R):
                        split_hi(act, n0 + head + kt + LOOK, it)
            split_hi(act, n0 + n - R + LOOK)
            for o in range(KT):
                act.wait_ge(ph.x_ready, ph.before + o + 1)
                act.activation(sq[o % 2][:], xT[:, o, :], ACT.Square).then_inc(ph.sq_ready, 1)
            for kt in range(n - R + 1, n):
                split_hi(act, n0 + kt + LOOK)

        def rows_vector(dve, ph):
            dve.memset(acc[:], 0.0)
            dve.drain()

            def add_square(o):
                dve.wait_ge(ph.sq_ready, ph.before + o + 1)
                if o:
                    dve.wait_ge(ph.acc_ready, ph.before + o)
                dve.tensor_tensor(acc[:], acc[:], sq[o % 2][:], ALU.add).then_inc(ph.acc_ready, 1)

            for o in range(KT):
                dve.wait_ge(ph.tile_done, ph.before + o + 1)
                dve.tensor_tensor(xT[:, o, :], xT[:, o, :], ps[:, o, :], ALU.add).then_inc(ph.x_ready, 1)
                if o:
                    add_square(o - 1)
            add_square(KT - 1)

        class Norm:
            sum_ready = sem("norm_sum_ready")
            std_ready = sem("norm_std_ready")
            n32_ready = sem("norm_n32_ready")
            hi_done = sem("norm_hi_done")
            h_ready = sem("norm_h_ready")

            def __init__(self, nth, name, acc_ready):
                self.nth, self.before = nth, nth * KT
                self.name, self.acc_ready = name, acc_ready

        def norm_tensor(pe, nm):
            pe.wait_ge(*nm.acc_ready(KT))
            pe.matmul(ps[:, 7, :], ones, acc[:], start=True, stop=True).then_inc(nm.sum_ready, 1)

        def norm_scalar(act, nm, tiles=KT):
            act.wait_ge(nm.sum_ready, nm.nth + 1)
            act.activation(rstd[:], ps[:, 7, :], ACT.Sqrt, bias=eps, scale=1.0 / D).then_inc(nm.std_ready, 1)
            for o in range(tiles):
                act.wait_ge(nm.n32_ready, nm.before + o + 1)
                act.activation(h_hi[:, o, :], t32[o % 2][:], ACT.Copy).then_inc(nm.hi_done, 1)

        def norm_vector(dve, nm):
            dve.wait_ge(nm.std_ready, nm.nth + 1)
            dve.reciprocal(rstd[:], rstd[:])
            dve.drain()
            g0 = VEC_AT[nm.name]

            def low(o):
                dve.wait_ge(nm.hi_done, nm.before + o + 1)
                dve.tensor_tensor(h_lo[:, o, :], t32[o % 2][:], h_hi[:, o, :].bitcast(F32), ALU.subtract).then_inc(nm.h_ready, 1)

            for o in range(KT):
                if o >= 2:
                    dve.wait_ge(nm.h_ready, nm.before + o - 1)
                dve.scalar_tensor_tensor(t32[o % 2][:], xT[:, o, :], vec[:, g0 + o:g0 + o + 1], rstd[:], ALU.mult, ALU.mult)\
                    .then_inc(nm.n32_ready, 1)
                if o:
                    low(o - 1)
            low(KT - 1)

        class Attention:

            def __init__(self, name, heads, qT, kT, val, mask, lg, pr, pt, nmax, den, osb):
                self.heads, self.qT, self.kT, self.val, self.mask = heads, qT, kT, val, mask
                self.lg, self.pr, self.pt, self.nmax, self.den, self.osb = lg, pr, pt, nmax, den, osb
                self.n = TB * heads
                self.L_ready = sem(name + "_L_ready")
                self.masked = sem(name + "_masked")
                self.p_ready = sem(name + "_p_ready")
                self.pT_ready = sem(name + "_pT_ready")
                self.pt_out = sem(name + "_pt_out")
                self.pv_done = sem(name + "_pv_done")
                self.o_out = sem(name + "_o_out")
                self.oT_ready = sem(name + "_oT_ready")
                self.oT_hi = sem(name + "_oT_hi")
                self.oT_done = sem(name + "_oT_done")

        def attn_tensor(pe, a):
            def logits(n):
                tb, h = divmod(n, a.heads)
                rows = slice(HD * (h % 2), HD * (h % 2 + 1))
                if n >= 2:
                    pe.wait_ge(a.masked, n - 1)
                keys = (tb + 1) * P
                pe.matmul(ps[:, n % 2, 0:keys], a.qT[rows, h // 2, tb * P:(tb + 1) * P], a.kT[rows, h // 2, 0:keys],
                          start=True, stop=True).then_inc(a.L_ready, 1)

            def turn(n):
                pe.wait_ge(a.p_ready, n + 1)
                if n >= 2:
                    pe.wait_ge(a.pt_out, n - 1)
                for kb in range(n // a.heads + 1):
                    last = pe.transpose(ps[:, 2 + n % 2, kb * P:(kb + 1) * P], a.pr[n % 2][:, kb * P:(kb + 1) * P], ident)
                last.then_inc(a.pT_ready, 1)

            def values(n):
                tb, h = divmod(n, a.heads)
                pe.wait_ge(a.pt_out, n + 1)
                if h == 0 and tb >= 2:
                    pe.wait_ge(a.o_out, tb - 1)
                for kb in range(tb + 1):
                    last = pe.matmul(ps[:, 4 + 2 * (tb % 2) + h // 8, (h % 8) * HD:(h % 8 + 1) * HD],
                                     a.pt[n % 2][:, kb * P:(kb + 1) * P], a.val[:, kb, h * HD:(h + 1) * HD],
                                     start=(kb == 0), stop=(kb == tb))
                last.then_inc(a.pv_done, 1)

            logits(0)
            logits(1)
            for n in range(a.n):
                turn(n)
                if n + 2 < a.n:
                    logits(n + 2)
                if n:
                    values(n - 1)
            values(a.n - 1)
            pe.wait_ge(a.o_out, TB)
            for c in range(a.heads * HD // P):
                if c >= 4:
                    pe.wait_ge(a.oT_done, c - 3)
                for tb in range(TB):
                    last = pe.transpose(ps[:, c % 4, tb * P:(tb + 1) * P], a.osb[:, tb, c * P:(c + 1) * P], ident)
                last.then_inc(a.oT_ready, 1)

        def attn_scalar(act, a):
            for n in range(a.n):
                keys = (n // a.heads + 1) * P
                act.wait_ge(a.masked, n + 1)
                if n >= 2:
                    act.wait_ge(a.pT_ready, n - 1)
                act.activation(a.pr[n % 2][:, 0:keys], a.lg[n % 2][:, 0:keys], ACT.Exp, bias=a.nmax[:, n:n + 1], scale=-1.0,
                               accum_out=a.den[:, n:n + 1]).then_inc(a.p_ready, 1)

        def attn_vector(dve, a):
            def mask(n):
                tb, h = divmod(n, a.heads)
                keys = (tb + 1) * P
                dve.wait_ge(a.L_ready, n + 1)
                if n >= 2:
                    dve.wait_ge(a.p_ready, n - 1)
                dve.tensor_tensor_reduce(out=a.lg[n % 2][:, 0:keys], in0=ps[:, n % 2, 0:keys], in1=a.mask(tb, h),
                                         scale=-(HD ** -0.5), scalar=3e38, op0=ALU.add, op1=ALU.min,
                                         accum_out=a.nmax[:, n:n + 1]).then_inc(a.masked, 1)

            def probs_out(n):
                keys = (n // a.heads + 1) * P
                dve.wait_ge(a.pT_ready, n + 1)
                if n >= 2:
                    dve.wait_ge(a.pv_done, n - 1)
                dve.tensor_copy(a.pt[n % 2][:, 0:keys], ps[:, 2 + n % 2, 0:keys]).then_inc(a.pt_out, 1)

            def heads_out(tb):
                dve.wait_ge(a.pv_done, a.heads * (tb + 1))
                r = a.den[:, tb * a.heads:(tb + 1) * a.heads]
                dve.reciprocal(r, r)
                dve.drain()
                b0 = 4 + 2 * (tb % 2)
                dve.tensor_tensor(a.osb[:, tb, :].rearrange("p (h d) -> p h d", d=HD),
                                  ps[:, b0:b0 + a.heads // 8, :].rearrange("p b (h d) -> p (b h) d", d=HD),
                                  bc(r, 2, HD), ALU.mult).then_inc(a.o_out, 1)

            mask(0)
            mask(1)
            for n in range(a.n):
                probs_out(n)
                if n + 2 < a.n:
                    mask(n + 2)
                if n >= a.heads and n % a.heads == 1:
                    heads_out(n // a.heads - 1)
            heads_out(TB - 1)

        def heads_hi(act, a, hi):
            for c in range(a.heads * HD // P):
                act.wait_ge(a.oT_ready, c + 1)
                act.activation(hi[:, c, :], ps[:, c % 4, :], ACT.Copy).then_inc(a.oT_hi, 1)

        def heads_lo(dve, a, hi, lo):
            for c in range(a.heads * HD // P):
                dve.wait_ge(a.oT_hi, c + 1)
                dve.tensor_tensor(lo[:, c, :], ps[:, c % 4, :], hi[:, c, :].bitcast(F32), ALU.subtract).then_inc(a.oT_done, 1)

        o6 = [BIGR]

        def dsabuf(name, shape, parts=P):
            off = o6[0]
            o6[0] += -(-4 * int(np.prod(shape)) // 32) * 32
            assert o6[0] <= end, name
            return at(name, shape, off)

        qT = dsabuf("qT", [KT, T])
        kT = dsabuf("kT", [KT, T])
        val = dsabuf("val", [TB, D])
        raw_off = o6[0]
        rawp = [dsabuf(f"rawp{n}", [TB, GROUP]) for n in range(2)]
        rope_off = o6[0]
        rope_a = dsabuf("rope_a", [2, GROUP])
        rope_b = dsabuf("rope_b", [2, GROUP])
        qi_off = o6[0]
        qiT = dsabuf("qiT", [IH // 2, T])
        kiT = dsabuf("kiT", [T])
        kin = dsabuf("kin", [TB, 2 * HD])
        rope = dsabuf("rope", [2, TB, HD])
        hgain = dsabuf("hgain", [2, HD])
        rtab = dsabuf("rtab", [2, 2, TB, HD])
        wi = dsabuf("wi", [TB, IH])
        hsum = dsabuf("hsum", [TB * 8])
        kisum = dsabuf("kisum", [TB])
        nmax = dsabuf("nmax", [TB * NH])
        den = dsabuf("den", [TB * NH])
        top8 = dsabuf("top8", [3, 8])
        hsq = at("hsq", [TB, GROUP], rope_off)
        osb = at("osb", [TB, D], raw_off)
        lg = [at(f"lg{n}", [T], rope_off + 2 * KB * n) for n in range(2)]
        pr = [at(f"pr{n}", [T], rope_off + 4 * KB + 2 * KB * n) for n in range(2)]
        pt = [at(f"pt{n}", [T], qi_off + 2 * KB * n) for n in range(2)]
        score = [None] + [at(f"score{n}", [T], SCR + 2 * KB * (1 + n)) for n in range(3)]
        relu = [at(f"relu{n}", [T], SCR + 8 * KB + 2 * KB * n) for n in range(2)]

        A = {n: sem("dsa_" + n) for n in (
            "par_landed", "raw_ready", "sums_ready", "std_ready", "roped", "tr_ready", "tr_evac", "rem_ready", "ki_sums",
            "ki_std", "ki_ready", "val_ready", "idx_ready", "relu_ready", "relu_used")}
        att1 = Attention("att1", NH, qT, kT, val,
                         lambda tb, h: const("causal") if tb == 0 else score[tb][:, 0:(tb + 1) * P], lg, pr, pt, nmax, den, osb)
        QI, REM, Q0, Q1, K0, K1, V0, V1 = range(8)
        HALF = {QI: 0, REM: 1, Q0: 0, Q1: 1, K0: 0, K1: 1, V0: 0, V1: 1}
        UNIT_OF = {QI: 0, REM: 4, Q0: 5, Q1: 9, K0: 13, K1: 17, V0: 21, V1: 25}
        ROT = [QI, Q0, Q1, K0, K1]
        RAWBUF = {g: n % 2 for n, g in enumerate(ROT)}
        n_dsa = FIRST["dsa"] if "dsa" in FIRST else 0

        def end_of(g):
            return n_dsa + UNIT_OF[g] + (0 if g == REM else 3)

        def project(pe, w0, group_half, units, in_ready=None, width=GROUP, n_kt=2):
            for u in range(units):
                slot, number, _ = unit(w0 + u)
                pe.wait_ge(lo_ready, number + 1)
                for k2 in range(n_kt):
                    kt = u * n_kt + k2
                    if in_ready is not None:
                        pe.wait_ge(*in_ready(kt + 1))
                    step = UNIT // n_kt
                    wh, wl = w_hi[slot][:, k2 * step:k2 * step + width], w_lo[slot][:, k2 * step:k2 * step + width]
                    for tb in range(TB):
                        toks = slice(tb * P, (tb + 1) * P)
                        o = ps[:, 4 * group_half + tb, 0:width]
                        pe.matmul(o, h_hi[:, kt, toks], wh, start=(kt == 0), stop=False)
                        pe.matmul(o, h_hi[:, kt, toks], wl, start=False, stop=False)
                        last = pe.matmul(o, h_lo[:, kt, toks], wh, start=False, stop=(kt == KT - 1))
                last.then_inc(unit_used, 1)

        def dsa_tensor(pe, nm):
            def proj(g, in_ready=None):
                if g == REM:
                    project(pe, n_dsa + UNIT_OF[g], HALF[g], 1, in_ready, HD + IH, KT)
                else:
                    project(pe, n_dsa + UNIT_OF[g], HALF[g], 4, in_ready)

            def transposes(g):
                n = ROT.index(g)
                pe.wait_ge(A["roped"], n + 1)
                for c in range(4):
                    for tb in range(TB):
                        last = pe.transpose(ps[:, 4 * HALF_T[g] + c, tb * P:(tb + 1) * P], rawp[RAWBUF[g]][:, tb, c * P:(c + 1) * P], ident)
                    last.then_inc(A["tr_ready"], 1)

            HALF_T = {QI: 1, Q0: 0, Q1: 1, K0: 0, K1: 1}
            proj(QI, after(nm.h_ready, nm.before))
            proj(REM)
            pe.wait_ge(A["raw_ready"], 1)
            proj(Q0)
            pe.wait_ge(A["rem_ready"], 1)
            transposes(QI)
            pe.wait_ge(A["ki_ready"], 1)
            pe.wait_ge(A["tr_evac"], 1)
            for tb in range(TB):
                last = pe.transpose(ps[:, 4, tb * P:(tb + 1) * P], kin[:, tb, :], ident)
            last.then_inc(A["tr_ready"], 1)
            pe.wait_ge(A["tr_evac"], 5)
            for n in range(3 * IH):
                tb, h = 1 + n // IH, n % IH
                rows = slice(HD * (h % 2), HD * (h % 2 + 1))
                keys = (tb + 1) * P
                if n >= 2:
                    pe.wait_ge(A["relu_ready"], n - 1)
                pe.matmul(ps[:, 4 + n % 2, 0:keys], qiT[rows, h // 2, tb * P:(tb + 1) * P], kiT[rows, 0:keys],
                          start=True, stop=True).then_inc(A["idx_ready"], 1)
            pe.wait_ge(A["relu_ready"], 3 * IH)
            for g, before in ((Q1, Q0), (K0, Q1), (K1, K0), (V0, K1)):
                proj(g)
                if g == V0:
                    break
                pe.wait_ge(A["raw_ready"], ROT.index(before) + 1)
                transposes(before)
                pe.wait_ge(A["tr_evac"], 5 + 4 * ROT.index(before))
            transposes(K1)
            pe.wait_ge(A["tr_evac"], 5 + 4 * 4)
            proj(V1)
            pe.wait_ge(A["val_ready"], 2)
            attn_tensor(pe, att1)

        def dsa_scalar(act):
            def split(g, u):
                split_hi(act, n_dsa + UNIT_OF[g] + u + LOOK)

            def raw_out(g):
                n = ROT.index(g)
                act.wait_ge(unit_used, done(end_of(g)))
                if n >= 2:
                    act.wait_ge(A["tr_ready"], 4 * (n - 1) + (1 if n >= 2 else 0))
                for tb in range(TB):
                    last = act.activation(rawp[RAWBUF[g]][:, tb, :], ps[:, 4 * HALF[g] + tb, :], ACT.Copy)
                if g != QI:
                    act.wait_ge(A["roped"], n)
                    for tb in range(TB):
                        last = act.activation(hsq[:, tb, :], ps[:, 4 * HALF[g] + tb, :], ACT.Square)
                last.then_inc(A["raw_ready"], 1)

            def std(g):
                n = ROT.index(g)
                act.wait_ge(A["sums_ready"], n)
                act.activation(hsum[:], hsum[:], ACT.Sqrt, bias=eps, scale=1.0 / HD).then_inc(A["std_ready"], 1)

            def tr_out(g):
                n = ROT.index(g)
                first = 4 * n + (1 if n else 0)
                for c in range(4):
                    act.wait_ge(A["tr_ready"], first + c + 1)
                    o = {QI: qiT[:, c, :], Q0: qT[:, c, :], Q1: qT[:, 4 + c, :], K0: kT[:, c, :], K1: kT[:, 4 + c, :]}[g]
                    half = {QI: 1, Q0: 0, Q1: 1, K0: 0, K1: 1}[g]
                    act.activation(o, ps[:, 4 * half + c, :], ACT.Copy).then_inc(A["tr_evac"], 1)

            for u in range(4):
                split(QI, u)
            raw_out(QI)
            split(REM, 0)
            act.wait_ge(unit_used, done(end_of(REM)))
            for tb in range(TB):
                act.activation(kin[:, tb, 0:HD], ps[:, 4 + tb, 0:HD], ACT.Copy)
                act.activation(wi[:, tb, :], ps[:, 4 + tb, HD:HD + IH], ACT.Copy, scale=float(np.float32(IH ** -0.5)) * HD ** -0.5)
                last = act.activation(relu[0][:, 0:HD], ps[:, 4 + tb, 0:HD], ACT.Square, accum_out=kisum[:, tb:tb + 1])
                act.drain()
            last = act.activation(kisum[:], kisum[:], ACT.Sqrt, bias=eps, scale=1.0 / HD)
            last.then_inc(A["rem_ready"], 1)
            for u in range(4):
                split(Q0, u)
            tr_out(QI)
            act.wait_ge(A["tr_ready"], 5)
            act.activation(kiT[:], ps[:, 4, :], ACT.Copy).then_inc(A["tr_evac"], 1)
            for n in range(3 * IH):
                tb = 1 + n // IH
                keys = (tb + 1) * P
                act.wait_ge(A["idx_ready"], n + 1)
                if n >= 2:
                    act.wait_ge(A["relu_used"], n - 1)
                act.activation(relu[n % 2][:, 0:keys], ps[:, 4 + n % 2, 0:keys], ACT.Relu).then_inc(A["relu_ready"], 1)
            for g, before in ((Q1, Q0), (K0, Q1), (K1, K0), (V0, K1)):
                split(g, 0)
                raw_out(before)
                split(g, 1)
                std(before)
                split(g, 2)
                split(g, 3)
                tr_out(before)
            for half, g in ((0, V0), (1, V1)):
                if g == V1:
                    for u in range(4):
                        split(V1, u)
                act.wait_ge(unit_used, done(end_of(g)))
                for tb in range(TB):
                    last = act.activation(val[:, tb, half * GROUP:(half + 1) * GROUP], ps[:, 4 * HALF[g] + tb, :], ACT.Copy)
                last.then_inc(A["val_ready"], 1)
            attn_scalar(act, att1)
            heads_hi(act, att1, h_hi)

        def dsa_vector(dve):
            dve.wait_ge(A["par_landed"], 32)
            for which in range(2):
                for part in range(2):
                    dve.tensor_tensor(rtab[:, which, part, :, :], rope[:, part, :, :], bc(hgain[:, which, :], 1, TB), ALU.mult)
            dve.drain()
            HH = HD // 2

            def rotate(g):
                buf = rawp[RAWBUF[g]]
                cs = [rope[:, part, :, :] for part in range(2)] if g == QI else \
                    [rtab[:, 0 if g in (Q0, Q1) else 1, part, :, :] for part in range(2)]
                for half in range(2):
                    tbs = slice(2 * half, 2 * half + 2)
                    x = buf[:, tbs, :].rearrange("p b (h d) -> p b h d", d=HD)
                    a, b = (t[:].rearrange("p b (h d) -> p b h d", d=HD) for t in (rope_a, rope_b))
                    dve.tensor_tensor(a, x, bc(cs[0][:, tbs, :], 2, 8), ALU.mult)
                    dve.tensor_tensor(b, x, bc(cs[1][:, tbs, :], 2, 8), ALU.mult)
                    dve.drain()
                    dve.tensor_tensor(x[:, :, :, 0:HH], a[:, :, :, 0:HH], b[:, :, :, HH:HD], ALU.subtract)
                    last = dve.tensor_tensor(x[:, :, :, HH:HD], a[:, :, :, HH:HD], b[:, :, :, 0:HH], ALU.add)
                    if half == 0:
                        dve.drain()
                last.then_inc(A["roped"], 1)

            def head_sums(g):
                dve.wait_ge(A["raw_ready"], ROT.index(g) + 1)
                dve.tensor_reduce(hsum[:], hsq[:].rearrange("p b (h d) -> p (b h) d", d=HD), AX_X, ALU.add)\
                    .then_inc(A["sums_ready"], 1)

            def head_norm(g):
                dve.wait_ge(A["std_ready"], ROT.index(g))
                dve.reciprocal(hsum[:], hsum[:])
                dve.drain()
                x = rawp[RAWBUF[g]][:].rearrange("p b (h d) -> p (b h) d", d=HD)
                dve.tensor_tensor(x, x, bc(hsum[:], 2, HD), ALU.mult)
                dve.drain()
                rotate(g)

            dve.wait_ge(A["raw_ready"], 1)
            rotate(QI)
            dve.wait_ge(A["rem_ready"], 1)
            dve.reciprocal(kisum[:], kisum[:])
            dve.drain()
            ki = kin[:, :, 0:HD]
            dve.tensor_tensor(ki, ki, bc(kisum[:], 2, HD), ALU.mult)
            dve.drain()
            a, b = (t[:].rearrange("p b n -> p (b n)")[:, 0:TB * HD].rearrange("p (b d) -> p b d", d=HD) for t in (rope_a, rope_b))
            dve.tensor_tensor(a, ki, rope[:, 0, :, :], ALU.mult)
            dve.tensor_tensor(b, ki, rope[:, 1, :, :], ALU.mult)
            dve.drain()
            for copy in range(2):
                o = kin[:, :, copy * HD:(copy + 1) * HD]
                dve.tensor_tensor(o[:, :, 0:HH], a[:, :, 0:HH], b[:, :, HH:HD], ALU.subtract)
                last = dve.tensor_tensor(o[:, :, HH:HD], a[:, :, HH:HD], b[:, :, 0:HH], ALU.add)
            last.then_inc(A["ki_ready"], 1)
            for tb in range(1, TB):
                dve.memset(score[tb][:, 0:tb * P], 0.0)
                dve.tensor_copy(score[tb][:, tb * P:(tb + 1) * P], const("causal"))
            dve.drain()
            for n in range(3 * IH):
                tb, h = 1 + n // IH, n % IH
                keys = (tb + 1) * P
                dve.wait_ge(A["relu_ready"], n + 1)
                if n:
                    dve.wait_ge(A["relu_used"], n)
                dve.scalar_tensor_tensor(score[tb][:, 0:keys], relu[n % 2][:, 0:keys], wi[:, tb, h:h + 1], score[tb][:, 0:keys],
                                         ALU.mult, ALU.add).then_inc(A["relu_used"], 1)
            dve.drain()

            def select(rounds):
                with dve.Fori(0, rounds):
                    for tb in range(1, TB):
                        dve.max(top8[:, tb - 1, :], score[tb][:, 0:(tb + 1) * P])
                    dve.drain()
                    for tb in range(1, TB):
                        s = score[tb][:, 0:(tb + 1) * P]
                        dve.match_replace(s, top8[:, tb - 1, :], s, TAKEN)
                    dve.drain()

            for g in (Q0, Q1, K0, K1):
                head_sums(g)
                select(TOPK // 8 // 4)
                head_norm(g)
            for tb in range(1, TB):
                s = score[tb][:, 0:(tb + 1) * P]
                dve.tensor_scalar(s, s, -1e37, -BIG, ALU.is_gt, ALU.mult)
            dve.drain()

            attn_vector(dve, att1)
            heads_lo(dve, att1, h_hi, h_lo)

        o7 = [BIGR]

        def mixbuf(name, shape, dt=F32):
            off = o7[0]
            o7[0] += -(-4 * int(np.prod(shape)) // 32) * 32
            assert o7[0] <= end, name
            return at(name, shape, off, dt)

        v2 = mixbuf("v2", [TB, GROUP])
        convT = mixbuf("convT", [XT + LT, T])
        gqk_off = o7[0]
        gqkT = mixbuf("gqkT", [12, T])
        z2 = mixbuf("z2", [TB, GROUP])
        bias_off = o7[0]
        abias = mixbuf("abias", [AH, T])
        gates = mixbuf("gates", [LT, 2, P])
        normw = mixbuf("normw", [GROUP])
        convw = mixbuf("convw", [XT + LT, CW + 1])
        lvec = mixbuf("lvec", [3, LT])
        svec = mixbuf("svec", [3, SH])
        sp8 = mixbuf("sp8", [6, LT])
        dts = mixbuf("dts", [6, TB * SH])
        dt_, dtA, acs, tot, eacs, cdec = (mixbuf(n, [TB * SH]) for n in ("dt_", "dtA", "acs", "tot", "eacs", "cdec"))
        dtdec, gsum = mixbuf("dtdec", [TB * SH]), mixbuf("gsum", [2])
        nmax2, den2 = mixbuf("nmax2", [TB * AH]), mixbuf("den2", [TB * AH])
        lmat = mixbuf("lmat", [SH, P])
        r4, i4 = at("r4", [LT, T], bias_off), at("i4", [LT, T], bias_off + 8 * KB)
        a4 = at("a4", [LT, T], SCR)
        asq = [at(f"asq{n}", [T], SCR + 8 * KB + 2 * KB * n) for n in range(2)]
        H2 = HT + 24 * KB
        xdt, xdec, ysk, prev = (at(n, [GROUP], H2 + 2 * KB * m) for m, n in enumerate(("xdt", "xdec", "ysk", "prev")))
        btok = mixbuf("btok", [SG * SN])
        lg2 = [at(f"lg2_{n}", [T], SCR + 2 * KB * n) for n in range(2)]
        pr2 = [at(f"pr2_{n}", [T], SCR + 4 * KB + 2 * KB * n) for n in range(2)]
        pt2 = [at(f"pt2_{n}", [T], SCR + 8 * KB + 2 * KB * n) for n in range(2)]
        mix_hi = at("mix_hi", [12, T], HT, F32R)
        mix_lo = at("mix_lo", [12, T], BIGR, F32R)
        osb2 = at("osb2", [TB, GROUP], gqk_off)
        xT3 = convT[:, XT:XT + LT, :]
        gT = gqkT[:, 0:LT, :]
        q2T, k2T = gqkT[:, 4:8, :], gqkT[:, 8:12, :]

        M = {n: sem("mix_" + n) for n in (
            "par_landed", "bias_landed", "tap_ready", "conv_done", "silu_ready", "copied", "gelu_ready", "z_ready", "v_ready",
            "lru_ps", "lru_gates", "lru_small", "lru_e", "lru_sp", "lru_a", "lru_sq", "lru_u2", "lru_root", "lru_done",
            "dt_e", "dt_sum", "dt_ready", "acs_ps", "acs_out", "dec_in", "dec_out", "dec_ready", "x_ps", "b_ps", "b_out",
            "g_ps", "bc_ps", "x_out", "seg_ready", "L_exp", "S_ready", "yd_ps", "yo_ps", "st_ps", "prev_ready", "y_ready",
            "y_sq", "y_std", "y_done", "yT_ready", "l_hi")}
        att2 = Attention("att2", AH, q2T, k2T, v2, lambda tb, h: abias[:, h, (TB - 1 - tb) * P:T], lg2, pr2, pt2, nmax2, den2, osb2)
        n_mix = FIRST["mix"]
        Z0, VV0, DT0 = 24, 28, 32

        def log1p_series(dve, e, s, s2, p):
            dve.tensor_scalar(s, e, 2.0, None, ALU.add)
            dve.drain()
            dve.reciprocal(s, s)
            dve.drain()
            dve.tensor_tensor(s, s, e, ALU.mult)
            dve.drain()
            dve.tensor_tensor(s2, s, s, ALU.mult)
            dve.drain()
            dve.tensor_scalar(p, s2, 1.0 / 17, None, ALU.mult)
            for k in (15, 13, 11, 9, 7, 5, 3):
                dve.drain()
                dve.scalar_tensor_tensor(p, p, 1.0 / k, s2, ALU.add, ALU.mult)
            dve.drain()
            dve.scalar_tensor_tensor(p, p, 1.0, s, ALU.add, ALU.mult)
            dve.drain()
            dve.tensor_scalar(p, p, 2.0, None, ALU.mult)
            dve.drain()

        def mix_tensor(pe, nm):
            def tile(k, it, bank, in_ready):
                slot, number, _ = unit(k, it)
                pe.wait_ge(lo_ready, number + 1)
                for kt in range(KT):
                    if in_ready is not None:
                        pe.wait_ge(*in_ready(kt + 1))
                    cols = slice(kt * P, (kt + 1) * P)
                    last = mm3(pe, ps[:, bank, :], w_hi[slot][:, cols], w_lo[slot][:, cols], h_hi[:, kt, :], h_lo[:, kt, :],
                               kt == 0, kt == KT - 1)
                last.then_inc(unit_used, 1)

            with pe.Fori(0, 3) as it:
                for b in range(4):
                    pe.wait_ge(M["conv_done"], it * 4 + (b + 1))
                    tile(n_mix + b, it, b, after(nm.h_ready, nm.before) if b == 0 else None)
            pe.wait_ge(M["conv_done"], 12 + 4)
            with pe.Fori(0, 3) as it:
                for b in range(4):
                    pe.wait_ge(M["copied"], it * 4 + (b + 1))
                    tile(n_mix + 12 + b, it, b, None)
            project(pe, n_mix + Z0, 1, 4)
            pe.wait_ge(M["par_landed"], 16 * 5)
            pe.wait_ge(M["copied"], 12 + 4)
            for j in range(LT):
                for which in range(2):
                    if j >= 2:
                        pe.wait_ge(M["lru_gates"], 2 * (j - 2) + which + 1)
                    pe.matmul(ps[:, 2 * (j % 2) + which, :], gates[:, j, which, :], xT3[:, j, :], start=True, stop=True)\
                        .then_inc(M["lru_ps"], 1)
            pe.wait_ge(M["lru_gates"], 2 * LT)
            project(pe, n_mix + VV0, 0, 4)
            pe.wait_ge(M["z_ready"], 1)
            project(pe, n_mix + DT0, 1, 1, None, SH, KT)
            pe.wait_ge(M["dt_ready"], 1)
            pe.wait_ge(M["v_ready"], 1)
            pe.matmul(ps[:, 0, 0:TB * SH], const("tri"), dtA[:], start=True, stop=True)
            pe.matmul(ps[:, 1, 0:TB * SH], ones, dtA[:], start=True, stop=True).then_inc(M["acs_ps"], 1)
            pe.wait_ge(M["acs_out"], 1)
            pe.wait_ge(M["silu_ready"], 1)
            for c in range(TB):
                toks = slice(c * P, (c + 1) * P)
                if c:
                    pe.wait_ge(M["x_out"], c)
                for m in range(4):
                    last = pe.transpose(ps[:, 0, m * P:(m + 1) * P], convT[:, m, toks], ident)
                last.then_inc(M["x_ps"], 1)
                if c:
                    pe.wait_ge(M["b_out"], c)
                for g in range(SG):
                    last = pe.transpose(ps[:, 1, g * SN:(g + 1) * SN], convT[:, 4 + g, toks], ident)
                last.then_inc(M["b_ps"], 1)
                if c:
                    pe.wait_ge(M["seg_ready"], c)
                for h in range(SH):
                    col = dtA[:, c * SH + h:c * SH + h + 1]
                    last = pe.matmul(ps[:, 2 + h // 4, (h % 4) * P:(h % 4 + 1) * P], col.broadcast_to([P, P]), const("tri"),
                                     start=True, stop=True)
                last.then_inc(M["bc_ps"], 1)
                if c:
                    pe.wait_ge(M["S_ready"], c)
                for g in range(SG):
                    last = pe.matmul(ps[:, 4, g * P:(g + 1) * P], convT[:, 4 + g, toks], convT[:, 6 + g, toks], start=True, stop=True)
                last.then_inc(M["g_ps"], 1)
                pe.wait_ge(M["x_out"], c + 1)
                pe.wait_ge(M["b_out"], c + 1)
                if c:
                    pe.wait_ge(M["prev_ready"], c)
                if c < TB - 1:
                    for g in range(SG):
                        last = pe.matmul(ps[:, 5, g * 256:(g + 1) * 256], btok[:, g * SN:(g + 1) * SN], xdec[:, g * 256:(g + 1) * 256],
                                         start=True, stop=True)
                    last.then_inc(M["st_ps"], 1)
                if c:
                    pe.wait_ge(M["y_ready"], c)
                    for g in range(SG):
                        last = pe.matmul(ps[:, 6, g * 256:(g + 1) * 256], convT[:, 6 + g, toks], prev[:, g * 256:(g + 1) * 256],
                                         start=True, stop=True)
                    last.then_inc(M["yo_ps"], 1)
                pe.wait_ge(M["S_ready"], c + 1)
                for h in range(SH):
                    last = pe.matmul(ps[:, 7, h * HD:(h + 1) * HD], lmat[:, h, :], xdt[:, h * HD:(h + 1) * HD], start=True, stop=True)
                last.then_inc(M["yd_ps"], 1)
            pe.wait_ge(M["y_ready"], TB)
            pe.wait_ge(M["bias_landed"], 16)
            attn_tensor(pe, att2)
            for m in range(4):
                pe.wait_ge(M["y_done"], TB)
                for c in range(TB):
                    last = pe.transpose(ps[:, 4 + m, c * P:(c + 1) * P], z2[:, c, m * P:(m + 1) * P], ident)
                last.then_inc(M["yT_ready"], 1)

        def mix_scalar(act):
            with act.Fori(0, 3) as it:
                for b in range(4):
                    k = n_mix + b
                    split_hi(act, k + LOOK, it)
                    if b == 0:
                        act.wait_ge(M["par_landed"], 16 * 5)
                    tile = bass.ds(it * 4 + b, 1)
                    w = convw[:, tile, :].rearrange("p a k -> p (a k)")
                    act.wait_ge(unit_used, done(unit(k, it)[1]))
                    act.activation(convT[:, tile, :].rearrange("p a t -> p (a t)"), ps[:, b, :], ACT.Identity,
                                   bias=w[:, CW:CW + 1], scale=w[:, CW - 1:CW]).then_inc(M["tap_ready"], 1)
            act.wait_ge(M["conv_done"], 12 + 4)
            act.activation(convT[:, 0:XT, :], convT[:, 0:XT, :], ACT.Silu).then_inc(M["silu_ready"], 1)
            act.sem_inc(M["copied"], 4)
            with act.Fori(0, 3) as it:
                for b in range(4):
                    k = n_mix + 12 + b
                    split_hi(act, k + LOOK, it)
                    act.wait_ge(unit_used, done(unit(k, it)[1]))
                    act.activation(gqkT[:, bass.ds(it * 4 + b, 1), :].rearrange("p a t -> p (a t)"), ps[:, b, :], ACT.Copy)\
                        .then_inc(M["copied"], 1)
            split_hi(act, n_mix + Z0 + LOOK)
            act.wait_ge(M["copied"], 12 + 4)
            act.activation(gT, gT, ACT.Gelu_apprx_tanh).then_inc(M["gelu_ready"], 1)
            for u in range(1, 4):
                split_hi(act, n_mix + Z0 + u + LOOK)
            act.wait_ge(unit_used, done(n_mix + Z0 + 3))
            for tb in range(TB):
                last = act.activation(z2[:, tb, :], ps[:, 4 + tb, :], ACT.Silu)
            last.then_inc(M["z_ready"], 1)
            split_hi(act, n_mix + VV0 + LOOK)
            for j in range(LT):
                for which in range(2):
                    act.wait_ge(M["lru_ps"], 2 * j + which + 1)
                    act.activation((r4, i4)[which][:, j, :], ps[:, 2 * (j % 2) + which, :], ACT.Sigmoid,
                                   bias=lvec[:, which, j:j + 1]).then_inc(M["lru_gates"], 1)
            for u in range(1, 3):
                split_hi(act, n_mix + VV0 + u + LOOK)
            act.wait_ge(M["lru_small"], 1)
            act.activation(sp8[:, 0, :], sp8[:, 0, :], ACT.Exp, scale=-1.0).then_inc(M["lru_e"], 1)
            act.activation(svec[:, 1, :], svec[:, 1, :], ACT.Exp).then_inc(M["lru_e"], 1)
            act.wait_ge(M["lru_sp"], 1)
            act.wait_ge(M["lru_gates"], 2 * LT)
            for j in range(LT):
                act.activation(a4[:, j, :], r4[:, j, :], ACT.Exp, scale=sp8[:, 4, j:j + 1])
                last = act.activation(r4[:, j, :], r4[:, j, :], ACT.Tanh, scale=sp8[:, 5, j:j + 1])
            last.then_inc(M["lru_a"], 1)
            act.drain()
            for j in range(LT):
                if j >= 2:
                    act.wait_ge(M["lru_u2"], j - 1)
                act.activation(asq[j % 2][:], a4[:, j, :], ACT.Square).then_inc(M["lru_sq"], 1)
            split_hi(act, n_mix + VV0 + 3 + LOOK)
            act.wait_ge(M["lru_u2"], LT)
            act.activation(r4[:], r4[:], ACT.Sqrt).then_inc(M["lru_root"], 1)
            act.wait_ge(unit_used, done(n_mix + VV0 + 3))
            for tb in range(TB):
                last = act.activation(v2[:, tb, :], ps[:, tb, :], ACT.Copy)
            last.then_inc(M["v_ready"], 1)
            split_hi(act, n_mix + DT0 + LOOK)
            act.wait_ge(M["dt_e"], 1)
            act.activation(dts[:, 2, :], dts[:, 1, :], ACT.Exp, scale=-1.0).then_inc(M["dt_sum"], 1)
            act.wait_ge(M["acs_ps"], 1)
            act.activation(acs[:], ps[:, 0, 0:TB * SH], ACT.Copy)
            act.activation(tot[:], ps[:, 1, 0:TB * SH], ACT.Copy).then_inc(M["acs_out"], 1)
            act.drain()
            act.activation(eacs[:], acs[:], ACT.Exp)
            act.activation(cdec[:], tot[:], ACT.Exp)
            act.wait_ge(M["dec_in"], 1)
            act.activation(dtdec[:], dtdec[:], ACT.Exp).then_inc(M["dec_out"], 1)
            act.wait_ge(M["lru_done"], 1)
            act.dma_start(abias[:], d["abias"]).then_inc(M["bias_landed"], 16)
            for c in range(TB):
                act.wait_ge(M["b_ps"], c + 1)
                if c >= 2:
                    act.wait_ge(M["st_ps"], c)
                elif c == 1:
                    act.wait_ge(M["st_ps"], 1)
                act.activation(btok[:], ps[:, 1, 0:SG * SN], ACT.Copy).then_inc(M["b_out"], 1)
                act.wait_ge(M["seg_ready"], c + 1)
                act.activation(lmat[:], lmat[:], ACT.Exp).then_inc(M["L_exp"], 1)
                act.wait_ge(M["y_ready"], c + 1)
                for g in range(SG):
                    act.activation(ysk[:, g * 256:(g + 1) * 256], z2[:, c, g * 256:(g + 1) * 256], ACT.Square, accum_out=gsum[:, g:g + 1])
                act.drain()
                act.activation(gsum[:], gsum[:], ACT.Sqrt, bias=const("eps_ssd"), scale=1.0 / 256).then_inc(M["y_std"], 1)
            attn_scalar(act, att2)
            heads_hi(act, att2, mix_hi)
            for m in range(4):
                act.wait_ge(M["yT_ready"], m + 1)
                act.activation(mix_hi[:, 4 + m, :], ps[:, 4 + m, :], ACT.Copy).then_inc(M["l_hi"], 1)
            for j in range(LT):
                act.activation(mix_hi[:, 8 + j, :], xT3[:, j, :], ACT.Copy).then_inc(M["l_hi"], 1)

        def mix_vector(dve):
            dve.sem_inc(M["conv_done"], 4)
            with dve.Fori(0, 3) as it:
                for b in range(4):
                    tile = bass.ds(it * 4 + b, 1)
                    w = convw[:, tile, :].rearrange("p a k -> p (a k)")
                    y = convT[:, tile, :].rearrange("p a t -> p (a t)")
                    dve.wait_ge(M["tap_ready"], it * 4 + (b + 1))
                    for back in range(1, CW):
                        last = dve.scalar_tensor_tensor(y[:, back:T], ps[:, b, 0:T - back], w[:, CW - 1 - back:CW - back], y[:, back:T],
                                                        ALU.mult, ALU.add)
                        if back < CW - 1:
                            dve.drain()
                    last.then_inc(M["conv_done"], 1)
            e, m_, s, s2, p, n8 = (sp8[:, k, :] for k in (0, 1, 2, 3, 4, 5))
            lam = lvec[:, 2, :]
            dve.scalar_tensor_tensor(e, lam, -1.0, lam, ALU.mult, ALU.max)
            dve.tensor_scalar(m_, lam, -1.0, 0.0, ALU.mult, ALU.max).then_inc(M["lru_small"], 1)
            dve.wait_ge(M["lru_e"], 1)
            log1p_series(dve, e, s, s2, p)
            dve.tensor_tensor(p, p, m_, ALU.add)
            dve.drain()
            dve.tensor_scalar(n8, p, 8.0, None, ALU.mult)
            dve.drain()
            dve.tensor_scalar(p, n8, -1.0, None, ALU.mult).then_inc(M["lru_sp"], 1)
            dve.wait_ge(M["lru_a"], 1)
            for j in range(LT):
                dve.wait_ge(M["lru_sq"], j + 1)
                dve.scalar_tensor_tensor(r4[:, j, :], asq[j % 2][:], 1.0, r4[:, j, :], ALU.add, ALU.mult).then_inc(M["lru_u2"], 1)
            dve.tensor_tensor(i4[:], i4[:], xT3, ALU.mult)
            dve.drain()
            dve.wait_ge(M["lru_root"], 1)
            dve.tensor_tensor(r4[:], r4[:], i4[:], ALU.mult)
            dve.drain()
            for j in range(LT):
                dve.tensor_tensor_scan(xT3[:, j, :], a4[:, j, :], r4[:, j, :], 0.0, ALU.mult, ALU.add)
            dve.drain()
            dve.wait_ge(M["gelu_ready"], 1)
            dve.tensor_tensor(xT3, xT3, gT, ALU.mult).then_inc(M["lru_done"], 1)
            raw_dt, ab, e, s, s2, p = (dts[:, k, :] for k in range(6))
            dve.wait_ge(unit_used, done(n_mix + DT0))
            dve.tensor_tensor(raw_dt.rearrange("p (c h) -> p c h", h=SH), ps[:, 4:8, 0:SH], bc(svec[:, 0, :], 1, TB), ALU.add)
            dve.drain()
            dve.scalar_tensor_tensor(ab, raw_dt, -1.0, raw_dt, ALU.mult, ALU.max).then_inc(M["dt_e"], 1)
            dve.wait_ge(M["dt_sum"], 1)
            log1p_series(dve, e, s, s2, p)
            dve.scalar_tensor_tensor(dt_[:], raw_dt, 0.0, p, ALU.max, ALU.add)
            dve.drain()
            dve.wait_ge(M["lru_e"], 2)
            dve.tensor_tensor(dtA[:].rearrange("p (c h) -> p c h", h=SH), dt_[:].rearrange("p (c h) -> p c h", h=SH),
                              bc(svec[:, 1, :], 1, TB), ALU.mult)
            dve.drain()
            dve.tensor_scalar(dtA[:], dtA[:], -1.0, None, ALU.mult).then_inc(M["dt_ready"], 1)
            dve.wait_ge(M["acs_out"], 1)
            dve.tensor_tensor(dtdec[:], tot[:], acs[:], ALU.subtract).then_inc(M["dec_in"], 1)
            dve.wait_ge(M["dec_out"], 1)
            dve.tensor_tensor(dtdec[:], dtdec[:], dt_[:], ALU.mult)
            dve.memset(prev[:], 0.0)
            dve.drain()
            heads = lambda ap: ap.rearrange("p (h d) -> p h d", d=HD)
            for c in range(TB):
                hs = slice(c * SH, (c + 1) * SH)
                dve.wait_ge(M["x_ps"], c + 1)
                if c:
                    dve.wait_ge(M["yd_ps"], c)
                x = heads(ps[:, 0, :])
                dve.tensor_tensor(heads(xdt[:]), x, bc(dt_[:, hs], 2, HD), ALU.mult)
                dve.tensor_tensor(heads(xdec[:]), x, bc(dtdec[:, hs], 2, HD), ALU.mult)
                if c:
                    dve.wait_ge(M["y_std"], c)
                dve.tensor_tensor(heads(ysk[:]), x, bc(svec[:, 2, :], 2, HD), ALU.mult).then_inc(M["x_out"], 1)
                dve.wait_ge(M["bc_ps"], c + 1)
                for h in range(SH):
                    last = dve.scalar_tensor_tensor(lmat[:, h, :], ps[:, 2 + h // 4, (h % 4) * P:(h % 4 + 1) * P],
                                                    acs[:, c * SH + h:c * SH + h + 1], const("causal_t"), ALU.subtract, ALU.add)
                last.then_inc(M["seg_ready"], 1)
                dve.wait_ge(M["g_ps"], c + 1)
                dve.wait_ge(M["L_exp"], c + 1)
                lm = lmat[:].rearrange("p (g h) i -> p g h i", g=SG)
                dve.tensor_tensor(lm, lm, bc(ps[:, 4, 0:SG * P].rearrange("p (g i) -> p g i", g=SG), 2, SH // SG), ALU.mult)\
                    .then_inc(M["S_ready"], 1)
                z = z2[:, c, :]
                if c:
                    dve.wait_ge(M["yo_ps"], c)
                    dve.tensor_tensor(heads(xdec[:]), heads(ps[:, 6, :]), bc(eacs[:, hs], 2, HD), ALU.mult)
                    dve.drain()
                    dve.tensor_tensor(ysk[:], ysk[:], xdec[:], ALU.add)
                    dve.drain()
                if c < TB - 1:
                    dve.wait_ge(M["st_ps"], c + 1)
                    dve.tensor_tensor(heads(prev[:]), heads(prev[:]), bc(cdec[:, hs], 2, HD), ALU.mult)
                    dve.drain()
                    dve.tensor_tensor(prev[:], prev[:], ps[:, 5, :], ALU.add).then_inc(M["prev_ready"], 1)
                dve.wait_ge(M["yd_ps"], c + 1)
                dve.tensor_tensor(ysk[:], ysk[:], ps[:, 7, :], ALU.add)
                dve.drain()
                dve.tensor_tensor(z, z, ysk[:], ALU.mult).then_inc(M["y_ready"], 1)
                dve.wait_ge(M["y_std"], c + 1)
                dve.reciprocal(gsum[:], gsum[:])
                dve.drain()
                for g in range(SG):
                    cols = slice(g * 256, (g + 1) * 256)
                    last = dve.scalar_tensor_tensor(z[:, cols], z[:, cols], gsum[:, g:g + 1], normw[:, cols], ALU.mult, ALU.mult)
                last.then_inc(M["y_done"], 1)
            attn_vector(dve, att2)
            for c in range(4):
                dve.wait_ge(att2.oT_hi, c + 1)
                dve.tensor_tensor(mix_lo[:, c, :], ps[:, c, :], mix_hi[:, c, :].bitcast(F32), ALU.subtract)\
                    .then_inc(mix_in, 1)
            for m in range(8):
                dve.wait_ge(M["l_hi"], m + 1)
                src = ps[:, 4 + m, :] if m < 4 else xT3[:, m - 4, :]
                dve.tensor_tensor(mix_lo[:, 4 + m, :], src, mix_hi[:, 4 + m, :].bitcast(F32), ALU.subtract).then_inc(mix_in, 1)

        def final_vector(dve, nm):
            dve.wait_ge(nm.std_ready, nm.nth + 1)
            dve.reciprocal(rstd[:], rstd[:])
            dve.drain()
            g0 = VEC_AT[nm.name]
            for o in range(KT):
                dve.scalar_tensor_tensor(xT[:, o, :], xT[:, o, :], vec[:, g0 + o:g0 + o + 1], rstd[:], ALU.mult, ALU.mult)\
                    .then_inc(out_ready, 1)

        mix_in = sem("mix_parts")
        norms, rows = count(), count()
        glu = Gated(0, "glu", KT, after(S["ylo_ready"]))

        def norm(name, acc_ready):
            return Norm(next(norms), name, acc_ready)

        def rows_of(name, k_tiles, hi, lo, in_ready):
            return Rows(next(rows), name, k_tiles, hi, lo, in_ready)

        def normed(nm):
            return after(nm.h_ready, nm.before)

        def squared(ph):
            return after(ph.acc_ready, ph.before)

        norm_f0 = norm("norm_ffn0", after(glu.out_ready))
        gu0 = Gated(KT + 0 * FT, "gu0", FT, normed(norm_f0))
        down0 = rows_of("down0", FT, hid_hi, hid_lo, after(gu0.out_ready, gu0.before))
        norm_m1 = norm("norm_mix1", squared(down0))
        wo = rows_of("wo", KT, h_hi, h_lo, after(att1.oT_done))
        norm_f1 = norm("norm_ffn1", squared(wo))
        gu1 = Gated(KT + 1 * FT, "gu1", FT, normed(norm_f1))
        down1 = rows_of("down1", FT, hid_hi, hid_lo, after(gu1.out_ready, gu1.before))
        norm_m2 = norm("norm_mix2", squared(down1))
        w_out = rows_of("out", 12, mix_hi, mix_lo, after(mix_in))
        norm_f2 = norm("norm_ffn2", squared(w_out))
        gu2 = Gated(KT + 2 * FT, "gu2", FT, normed(norm_f2))
        down2 = rows_of("down2", FT, hid_hi, hid_lo, after(gu2.out_ready, gu2.before))
        norm_end = norm("norm_final", squared(down2))
        out_ready, out_landed = sem("out_ready"), sem("out_landed")

        def after_pairs(ph):
            n = ph.before + ph.pairs
            return [(o, None) for o in range(4, 8)] + [(0, (ph.pair_done, n + 1)), (1, None), (2, (ph.pair_done, n + 2)), (3, None)]

        block = ctx.enter_context(nc.Block())

        @block.sync
        def _(sp):
            s5_sync(sp)
            load_units(sp, "glu", d["w_glu"])
            load_units(sp, "gu0", d["w_gu0"])
            load_units(sp, "down0", d["w_down0"])
            sp.wait_ge(down0.tile_done, down0.before + KT)
            sp.dma_start(rope[:], d["rope"]).then_inc(A["par_landed"], 16)
            sp.dma_start(hgain[:], d["hgain"]).then_inc(A["par_landed"], 16)
            load_units(sp, "dsa", d["w_dsa"])
            load_units(sp, "wo", d["w_o"])
            load_units(sp, "gu1", d["w_gu1"])
            load_units(sp, "down1", d["w_down1"])
            sp.wait_ge(down1.tile_done, down1.before + KT)
            for buf, name in ((gates, "gates"), (normw, "normw"), (convw, "convw"), (lvec, "lvec"), (svec, "svec")):
                sp.dma_start(buf[:], d[name]).then_inc(M["par_landed"], 16)
            load_units(sp, "mix", d["w_mix"])
            load_units(sp, "out", d["w_out"])
            load_units(sp, "gu2", d["w_gu2"])
            load_units(sp, "down2", d["w_down2"])
            for o in range(KT):
                sp.wait_ge(out_ready, o + 1)
                sp.dma_start(out[:, o, :], xT[:, o, :]).then_inc(out_landed, 16)
            sp.wait_ge(out_landed, 16 * KT)

        @block.gpsimd
        def _(pool):
            s5_gpsimd(pool)
            split_lo_all(pool)

        @block.scalar
        def _(act):
            s5_scalar(act)
            for k in range(LOOK):
                split_hi(act, k)
            glu_scalar(act, glu)
            norm_scalar(act, norm_f0)
            ffn_scalar(act, gu0)
            rows_scalar(act, down0)
            norm_scalar(act, norm_m1)
            dsa_scalar(act)
            rows_scalar(act, wo)
            norm_scalar(act, norm_f1)
            ffn_scalar(act, gu1)
            rows_scalar(act, down1)
            norm_scalar(act, norm_m2)
            mix_scalar(act)
            rows_scalar(act, w_out)
            norm_scalar(act, norm_f2)
            ffn_scalar(act, gu2)
            rows_scalar(act, down2)
            norm_scalar(act, norm_end, 0)

        @block.vector
        def _(dve):
            s5_vector(dve)
            glu_vector(dve, glu)
            norm_vector(dve, norm_f0)
            ffn_vector(dve, gu0)
            rows_vector(dve, down0)
            norm_vector(dve, norm_m1)
            dsa_vector(dve)
            rows_vector(dve, wo)
            norm_vector(dve, norm_f1)
            ffn_vector(dve, gu1)
            rows_vector(dve, down1)
            norm_vector(dve, norm_m2)
            mix_vector(dve)
            rows_vector(dve, w_out)
            norm_vector(dve, norm_f2)
            ffn_vector(dve, gu2)
            rows_vector(dve, down2)
            final_vector(dve, norm_end)

        @block.tensor
        def _(pe):
            pe.sem_inc(unit_used, 1)
            s5_tensor(pe)
            gated_tensor(pe, glu)
            norm_tensor(pe, norm_f0)
            gated_tensor(pe, gu0)
            rows_tensor(pe, down0, after_pairs(gu0))
            norm_tensor(pe, norm_m1)
            dsa_tensor(pe, norm_m1)
            rows_tensor(pe, wo, [(o, None) for o in range(4, 8)] + [(o, (att1.oT_done, o + 5)) for o in range(4)])
            norm_tensor(pe, norm_f1)
            gated_tensor(pe, gu1)
            rows_tensor(pe, down1, after_pairs(gu1))
            norm_tensor(pe, norm_m2)
            mix_tensor(pe, norm_m2)
            rows_tensor(pe, w_out, [(o, (mix_in, o + 1)) for o in range(KT)])
            norm_tensor(pe, norm_f2)
            gated_tensor(pe, gu2)
            rows_tensor(pe, down2, after_pairs(gu2))
            norm_tensor(pe, norm_end)


def kernel(**inputs):
    import concourse.bacc as bacc
    from concourse.bass_utils import run_bass_kernel_spmd

    i = {k: np.asarray(v) for k, v in inputs.items()}
    x = i["x"][0]

    def tiles(w):
        k, n = w.shape
        return w.reshape(k // P, P, n // P, P).transpose(2, 1, 0, 3).reshape(n // P, P, k)

    def pairs(gate, value):
        return np.stack([tiles(gate), tiles(value)], 1).reshape(-1, P, gate.shape[0])

    def token_major(w):
        return w.reshape(KT // 2, 2, P, GROUP).transpose(0, 2, 1, 3).reshape(KT // 2, P, UNIT)

    def narrow(w):
        u = np.zeros((P, KT, P), w.dtype)
        u[:, :, :w.shape[1]] = w.reshape(KT, P, -1).transpose(1, 0, 2)
        return u.reshape(1, P, UNIT)

    def two(name):
        return i[name + "_2"][0]

    def block_diagonal(w):
        o = np.zeros((P, LT, P), w.dtype)
        for b in range(2 * LT):
            at = slice(HD * (b % 2), HD * (b % 2 + 1))
            o[at, b // 2, at] = w[b]
        return o

    w2 = two("w_in")
    w_in = i["dsa_w_in"][0]
    rest = narrow(w_in[:, 3 * D + IH * HD:])

    def states(a):
        return np.moveaxis(a, 1, 0)

    s5 = {k: i["s5_" + k][0] for k in ("lambda_re", "lambda_im", "log_dt", "b_re", "b_im", "c_re", "c_im", "d", "w_glu")}
    twice = lambda a, b: np.concatenate([states(a), states(b)], 0)
    gain = np.tile(i["norm_mix"][0].reshape(G, GH).T, (CH, 1))
    par = np.stack([twice(s5["lambda_re"], s5["lambda_re"]), twice(s5["lambda_im"], s5["lambda_im"]),
                    np.broadcast_to(s5["log_dt"], (P, G)), gain], 1)
    ct = {k: s5[k].transpose(0, 2, 1) for k in ("c_re", "c_im")}
    vecs = {"norm_ffn0": i["norm_ffn"][0], "norm_mix1": i["norm_mix"][1], "norm_ffn1": i["norm_ffn"][1],
            "norm_mix2": i["norm_mix_2"][0], "norm_ffn2": i["norm_ffn_2"][0], "norm_final": i["norm_final_2"]}
    wg = s5["w_glu"]
    arrays = {
        "cst": np.concatenate(list(constant_columns().values()), 1),
        "vec": np.concatenate([vecs[k].reshape(-1, P).T for k in VEC], 1),
        "xT": x.T.reshape(KT, P, T).transpose(1, 0, 2),
        "xs5": x.reshape(NC, CH, G, GH)[:, ::-1].transpose(1, 3, 2, 0).reshape(P, G, NC),
        "s5_par": par,
        "s5_b": np.stack([twice(s5["b_re"], s5["b_im"]), twice(s5["b_im"], s5["b_re"])], 1).reshape(P, 2, G * GH),
        "s5_c": np.stack([twice(ct["c_re"], ct["c_im"]), twice(ct["c_im"], ct["c_re"])], 1).reshape(P, 2, G * GH),
        "s5_d": s5["d"].reshape(G, GH).T,
        "w_glu": pairs(wg[:, D:], wg[:, :D]),
        "w_gu0": pairs(i["ffn_w_gate_up"][0][:, :FF], i["ffn_w_gate_up"][0][:, FF:]),
        "w_down0": i["ffn_w_down"][0].reshape(FT, P, D),
        "rope": rope_tables(),
        "hgain": np.broadcast_to(np.stack([i["dsa_q_norm"][0], i["dsa_k_norm"][0]]), (P, 2, HD)),
        "w_dsa": np.concatenate([token_major(w_in[:, 3 * D:3 * D + IH * HD]), rest]
                                + [token_major(w_in[:, n * GROUP:(n + 1) * GROUP]) for n in range(6)]),
        "w_o": i["dsa_w_o"][0].reshape(KT, P, D),
        "w_gu1": pairs(i["ffn_w_gate_up"][1][:, :FF], i["ffn_w_gate_up"][1][:, FF:]),
        "w_down1": i["ffn_w_down"][1].reshape(FT, P, D),
        "abias": dilated_bias(),
        "gates": np.stack([block_diagonal(two("lru_wa")), block_diagonal(two("lru_wx"))], 2),
        "normw": np.broadcast_to(two("ssd_norm"), (P, GROUP)),
        "convw": np.concatenate([np.concatenate([two(n + "_conv_w").T, two(n + "_conv_b")[:, None]], 1) for n in ("ssd", "lru")])
                 .reshape(XT + LT, P, CW + 1).transpose(1, 0, 2),
        "lvec": np.stack([two(n).reshape(LT, P).T for n in ("lru_ba", "lru_bx", "lru_lambda")], 1),
        "svec": np.broadcast_to(np.stack([two(n) for n in ("ssd_dt_bias", "ssd_a_log", "ssd_d")]), (P, 3, SH)),
        "w_mix": np.concatenate([tiles(w2[:, 2048:3072]), tiles(w2[:, 3592:4104]), tiles(w2[:, 3080:3592]), tiles(w2[:, 0:512]),
                                 tiles(w2[:, 512:1024]), token_major(w2[:, 1536:2048]), token_major(w2[:, 1024:1536]),
                                 narrow(w2[:, 3072:3080])]),
        "w_out": two("w_out").reshape(12, P, D),
        "w_gu2": pairs(two("w_gate"), two("w_up")),
        "w_down2": two("w_down").reshape(FT, P, D),
    }
    arrays = {"in_" + k: np.ascontiguousarray(v) for k, v in arrays.items()}
    nc = bacc.Bacc("TRN2", target_bir_lowering=False, num_devices=1)
    d = {k[3:]: nc.dram_tensor(k, v.shape, mybir.dt.from_np(v.dtype), kind="ExternalInput").ap() for k, v in arrays.items()}
    out = nc.dram_tensor("out_x", (P, KT, T), F32, kind="ExternalOutput").ap()
    build(nc, d, out)
    r = run_bass_kernel_spmd(nc, [arrays], core_ids=[0])
    got = np.asarray(r.results[0]["out_x"])
    return got.transpose(2, 1, 0).reshape(1, T, D)
```

```python
import math
from contextlib import ExitStack
from itertools import count

import numpy as np
import concourse.bass as bass
from concourse import mybir

F32 = mybir.dt.float32
F32R = mybir.dt.float32r
ALU = mybir.AluOpType
ACT = mybir.ActivationFunctionType
AX_X = mybir.AxisListType.X

P = 128
D = 1024
T = 512
KT = D // P
TB = T // P
FF = 2816
FT = FF // P
EPS = 1e-6
BIG = 1e30
TAKEN = -3e38

NH, HD, IH = 16, 64, 8
TOPK = 128
SSD_EPS = 1e-5
AH, SH, SG, SN = 8, 8, 2, 128
XT, LT, CW = 8, 4, 4
RATES = ((128, 1), (512, 4), (2048, 16))
GROUP = 512

G, GH, NS = 64, 16, 64
CH = P // GH
NC = T // CH
QG = P // GH
NQ = G // QG
C1 = 6.28125
C2 = 2 * math.pi - C1
ROUND = 12582912.0
SIN_SCALE = 6.283185

UNIT = 1024
R = 4
LOOK = 3


def bc(ap, axis, n):
    out = ap.unsqueeze(axis)
    shape = list(out.shape)
    shape[axis] = n
    return out.broadcast_to(shape)


def constant_columns():
    i = np.arange(P)
    cols = {
        "ident": np.eye(P),
        "ones": np.ones((P, P)),
        "tri": i[:, None] <= i[None, :],
        "causal": np.where(i[None, :] <= i[:, None], 0.0, -BIG),
        "causal_t": np.where(i[:, None] <= i[None, :], 0.0, -BIG),
        "same_token": (i[:, None] // GH) == (i[None, :] // GH),
        "tau": np.broadcast_to(np.arange(CH + 1), (P, CH + 1)),
        "chunk": np.broadcast_to(np.arange(NC) - 1, (P, NC)),
        "carry": np.broadcast_to(np.arange(NC) > 0, (P, NC)),
        "sign": np.stack([np.where(i < NS, -1, 1), np.where(i < NS, 1, -1)], 1),
        "eps": np.full((P, 1), EPS),
        "eps_ssd": np.full((P, 1), SSD_EPS),
    }
    return {k: np.asarray(v, np.float32) for k, v in cols.items()}


def rope_tables():
    f = np.float32
    inv = f(10000.0) ** (-np.arange(0, HD, 2, dtype=f) / f(HD))
    a = np.arange(T, dtype=f)[:, None] * inv[None, :].astype(f)
    t = np.stack([np.cos(a), np.sin(a)]).astype(f)
    return np.concatenate([t, t], -1).reshape(2, TB, P, HD).transpose(2, 0, 1, 3)


def dilated_bias():
    dist = np.arange(P)[:, None] + (T - P) - np.arange(T)[None, :]
    count = sum(((dist % rate == 0) & (dist <= span)).astype(np.float64) for span, rate in RATES)
    count = np.where(dist >= 0, count, 0)
    slopes = 2.0 ** (-8.0 * np.arange(1, AH + 1) / AH)
    bias = -slopes[:, None, None] * dist + np.log(np.maximum(count, 1))
    return np.where(count > 0, 8 * bias, -BIG).astype(np.float32).transpose(1, 0, 2)


CONST_WIDTH = {k: v.shape[1] for k, v in constant_columns().items()}
CONST_AT = dict(zip(CONST_WIDTH, np.cumsum([0, *CONST_WIDTH.values()]).tolist()))
N_CONST = sum(CONST_WIDTH.values())

VEC = {"norm_ffn0": KT, "norm_mix1": KT, "norm_ffn1": KT, "norm_mix2": KT, "norm_ffn2": KT, "norm_final": KT}
VEC_AT = dict(zip(VEC, np.cumsum([0, *VEC.values()]).tolist()))
N_VEC = sum(VEC.values())

PHASES = {"glu": 2 * KT, "gu0": 2 * FT, "down0": FT, "dsa": 4 * 7 + 1, "wo": KT, "gu1": 2 * FT, "down1": FT,
          "mix": 33, "out": 12, "gu2": 2 * FT, "down2": FT}
FIRST = dict(zip(PHASES, np.cumsum([0, *PHASES.values()]).tolist()))
N_UNITS = sum(PHASES.values())


def build(nc, d, out):
    ctx = ExitStack()
    with ctx:
        def sem(name):
            return ctx.enter_context(nc.semaphore(name))

        base = (nc.sbuf_base + 63) // 64 * 64
        end = nc.sbuf_usable_end

        def at(name, shape, offset, dt=F32):
            return nc.alloc_sbuf_tensor_at(name, [P, *shape], dt, offset=offset)

        KB = 1024
        RAW, HI, LO = base, base + 16 * KB, base + 32 * KB
        X = base + 48 * KB
        CST = X + 16 * KB
        SCR = CST + 4 * KB
        HT = SCR + 12 * KB
        BIGR = HT + 32 * KB
        assert end - BIGR >= 95 * KB, (end - BIGR)

        raw = [at(f"raw{s}", [UNIT], RAW + 4 * KB * s) for s in range(R)]
        w_hi = [at(f"w_hi{s}", [UNIT], HI + 4 * KB * s, F32R) for s in range(R)]
        w_lo = [at(f"w_lo{s}", [UNIT], LO + 4 * KB * s, F32R) for s in range(R)]
        xT = at("xT", [KT, T], X)
        cst = at("cst", [N_CONST], CST)
        vec = at("vec", [N_VEC], CST + 32 * (-(-N_CONST // 8)))
        assert 4 * (N_CONST + N_VEC + 8) <= 4 * KB, (N_CONST, N_VEC)
        acc = at("acc", [T], SCR)
        sq = [at(f"sq{s}", [T], SCR + 2 * KB * (1 + s)) for s in range(2)]
        tok_mean, tok_rstd, tok_tmp = (at(f"tok{n}", [TB], SCR + 6 * KB + 64 * n) for n in range(3))
        t32 = [at(f"t32{s}", [T], SCR + 2 * KB * (4 + s)) for s in range(2)]
        h_hi = at("h_hi", [KT, T], HT, F32R)
        h_lo = at("h_lo", [KT, T], HT + 16 * KB, F32R)
        hid_hi = at("hid_hi", [FT, T], BIGR, F32R)
        hid_lo = at("hid_lo", [FT, T], BIGR + 2 * KB * FT, F32R)
        ps = ctx.enter_context(nc.psum_tensor("ps", [P, 8, T], F32))

        def const(name):
            return cst[:, CONST_AT[name]:CONST_AT[name] + CONST_WIDTH[name]]

        ident, ones, eps = const("ident"), const("ones"), const("eps")

        raw_landed = [sem(f"raw_landed{s}") for s in range(R)]
        hi_ready = sem("w_hi_ready")
        lo_ready = sem("w_lo_ready")
        unit_used = sem("unit_used")
        consts_landed = sem("consts_landed")

        def after(s, before=0):
            return lambda n: (s, n + before)

        def unit(k, it=None, per=R):
            if it is None:
                return k % R, k, k // R + 1
            return k % R, it * per + k, it * (per // R) + (k // R + 1)

        def load_units(sp, phase, view):
            n0, n = FIRST[phase], PHASES[phase]
            head = n % R if n0 else R

            def load(k, src, it=None):
                slot, number, _ = unit(k, it)
                if it is not None or k >= R:
                    sp.wait_ge(lo_ready, number - (R - 1))
                sp.dma_start(raw[slot][:], src).then_inc(raw_landed[slot], 16)

            for u in range(head):
                load(n0 + u, view[u])
            if n - head:
                with sp.Fori(0, (n - head) // R) as it:
                    for u in range(R):
                        load(n0 + head + u, view[bass.ds(it * R + (head + u), 1)].rearrange("a p n -> p (a n)"), it)
            assert (n - head) % R == 0

        def split_hi(act, k, it=None, per=R):
            if it is None and k >= N_UNITS:
                return
            slot, number, use = unit(k, it, per)
            act.wait_ge(raw_landed[slot], use * 16)
            if it is not None or k >= R:
                act.wait_ge(unit_used, number - (R - 2))
            act.activation(w_hi[slot][:], raw[slot][:], ACT.Copy).then_inc(hi_ready, 1)

        def split_lo_all(pool):
            def one(k, it=None):
                slot, number, _ = unit(k, it)
                pool.wait_ge(hi_ready, number + 1)
                pool.tensor_tensor(w_lo[slot][:], raw[slot][:], w_hi[slot][:].bitcast(F32), ALU.subtract)\
                    .then_inc(lo_ready, 1)
            with pool.Fori(0, N_UNITS // R) as it:
                for k in range(R):
                    one(k, it)
            for k in range(N_UNITS // R * R, N_UNITS):
                one(k)

        def mm3(pe, o, wh, wl, ah, al, start, stop):
            pe.matmul(o, wh, ah, start=start, stop=False)
            pe.matmul(o, wh, al, start=False, stop=False)
            return pe.matmul(o, wl, ah, start=False, stop=stop)

        def root_reciprocal(dve, out, m, t):
            dve.reciprocal(out, out)
            dve.drain()
            dve.tensor_tensor(t, out, out, ALU.mult)
            dve.drain()
            dve.tensor_tensor(t, t, m, ALU.mult)
            dve.drain()
            dve.tensor_scalar(t, t, -0.5, 1.5, ALU.mult, ALU.add)
            dve.drain()
            dve.tensor_tensor(out, out, t, ALU.mult)
            dve.drain()

        RING = RAW
        xs = at("s5_x", [G, NC], X)
        s5_par = at("s5_par", [4, G], RING)
        braw = at("s5_b", [2, G * GH], RING + 1 * KB)
        craw = at("s5_c", [2, G * GH], RING + 9 * KB)
        bbar = at("s5_bbar", [2, G * GH], RING + 17 * KB)
        NT9 = (CH + 1) * G * 4
        pw = [at(f"s5_pw{n}", [CH + 1, G], RING + 25 * KB + NT9 * n) for n in range(7)]
        turn, pw_re, pw_im, pw_ims, pw_re2, pw_imn, wave = pw
        small = at("s5_small", [16, G], RING + 25 * KB + NT9 * 7)
        assert 25 * KB + NT9 * 7 + 16 * G * 4 <= 48 * KB
        dskip = at("s5_dskip", [G], BIGR + 94 * KB)
        o5 = [BIGR]

        def s5buf(name, shape):
            off = o5[0]
            o5[0] += 4 * int(np.prod(shape))
            assert o5[0] <= BIGR + 94 * KB, name
            return at(name, shape, off)

        def s5two(name, shape):
            return [s5buf(f"{name}{n}", shape) for n in range(2)]

        winT = s5buf("s5_winT", [QG, CH, GH])
        wtmp = s5buf("s5_wtmp", [QG, CH, GH])
        win = s5two("s5_win", [QG, P + NS])
        wout = s5two("s5_wout", [QG, CH, GH])
        wotmp = s5buf("s5_wotmp", [QG, CH, GH])
        toep = s5two("s5_toep", [CH, QG, GH])
        ang2, ang_lo2, ang_sum2 = (s5two(f"s5_ang{n}_", [QG, NC]) for n in range(3))
        sin_t = s5two("s5_sin", [QG, NC])
        cos_t = s5two("s5_cos", [QG, NC])
        decay = s5two("s5_decay", [QG, NC])
        u_q = s5two("s5_u", [QG, NC])
        zin = s5buf("s5_zin", [QG, NC])
        zst = s5buf("s5_zst", [QG, NC])
        ztmp = s5buf("s5_ztmp", [QG, NC])
        zout = s5two("s5_zout", [QG, NC])
        conv = s5buf("s5_conv", [QG, GH])
        dI = s5buf("s5_dI", [G, GH])
        y_q = s5buf("s5_y", [CH, QG * GH])
        cxn = s5buf("s5_cxn", [G * GH])
        sumsq = at("s5_sumsq", [NC], SCR)
        rstd5, mean5, nt5 = (at(f"s5_rstd{n}", [NC], SCR + 256 * (n + 1)) for n in range(3))
        xsq = at("s5_xsq", [G, NC], BIGR)
        assert 4 * G * NC <= 4 * QG * (2 * CH * GH + 2 * (P + NS))
        lam_re, lam_im, log_dt, gain5 = (s5_par[:, n, :] for n in range(4))

        S = {n: sem("s5_" + n) for n in (
            "par_landed", "bc_landed", "x_landed", "dt", "turn", "mag", "wave", "powers", "ratio", "xsq", "sumsq", "sumps",
            "std", "prologue", "zeroed", "ang_ready", "ang_reduced", "half_ready", "decay_ready", "rot_done", "u_ready", "u_copied",
            "wout_ready", "winT_ready", "psT_ready", "psT_free", "convps", "conv_copied", "conv_ready", "w_ready", "w_free",
            "s_ready", "y_done", "y_evac", "yT_begun", "yT_ready", "gelu_ready", "yhi_ready", "ylo_ready", "xT_landed")}
        toep_landed = [sem(f"s5_toep_landed{n}") for n in range(2)]

        def s5_steps(engine, first, step, last):
            first(0, 0, 1)
            with engine.Fori(0, (NQ - 2) // 2) as it:
                step(it * 2 + 1, 1, it + 1)
                step(it * 2 + 2, 0, it + 2)
            last(NQ - 1, 1, NQ // 2)

        def s5_sync(sp):
            sp.dma_start(s5_par[:], d["s5_par"]).then_inc(S["par_landed"], 16)
            sp.dma_start(cst[:], d["cst"]).then_inc(consts_landed, 16)
            sp.dma_start(vec[:], d["vec"]).then_inc(consts_landed, 16)
            sp.dma_start(xs[:], d["xs5"]).then_inc(S["x_landed"], 16)
            sp.dma_start(braw[:], d["s5_b"]).then_inc(S["bc_landed"], 16)
            sp.dma_start(craw[:], d["s5_c"]).then_inc(S["bc_landed"], 16)
            sp.dma_start(dskip[0:GH, :], d["s5_d"]).then_inc(S["bc_landed"], 16)
            sp.wait_ge(S["zeroed"], 1)

            def shift_taps(e, p, use):
                sp.wait_ge(S["conv_ready"], e + 1)
                sp.wait_ge(S["y_done"], e * 2 + 2)
                for t in range(CH):
                    sp.dma_start(toep[p][GH * (CH - 1 - t):P, t, :, :], conv[0:GH * (t + 1), :, :]).then_inc(toep_landed[p], 16)

            s5_steps(sp, shift_taps, shift_taps, shift_taps)
            sp.wait_ge(S["w_ready"], NQ + 2)
            sp.wait_ge(S["u_copied"], NQ)
            sp.dma_start(xT[:], d["xT"]).then_inc(S["xT_landed"], 16)
            sp.wait_ge(S["winT_ready"], NQ)
            sp.wait_ge(S["wout_ready"], NQ)
            sp.wait_ge(S["ang_ready"], NQ)
            sp.wait_ge(S["decay_ready"], NQ)

        t8_hi, t8_lo = small[:, 13, :], small[:, 14, :]
        b_raw = [braw[:, n, :].rearrange("p (g h) -> p g h", h=GH) for n in range(2)]
        bx, by = (bbar[:, n, :].rearrange("p (g h) -> p g h", h=GH) for n in range(2))
        ratio_re, ratio_im = small[:, 9, :], small[:, 10, :]

        def s5_gpsimd(pool):
            for p in range(2):
                pool.memset(toep[p][:], 0.0)
                pool.memset(decay[p][:], 0.0)
            pool.drain().then_inc(S["zeroed"], 1)
            pool.wait_ge(consts_landed, 32)
            pool.wait_ge(S["bc_landed"], 48)
            pool.tensor_tensor(dI[0:GH, :, :], bc(dskip[0:GH, :], 2, GH), bc(ident[0:GH, 0:GH], 1, G), ALU.mult)
            pool.tensor_tensor(cxn[:], craw[:, 0, :], const("sign")[:, 1:2].broadcast_to([P, G * GH]), ALU.mult)
            scr = y_q[:].rearrange("p t n -> p (t n)").rearrange("p (g h) -> p g h", h=GH)
            pool.wait_ge(S["ratio"], 1)
            pool.tensor_tensor(by, b_raw[1], bc(ratio_re, 2, GH), ALU.mult)
            pool.tensor_tensor(scr, b_raw[0], bc(ratio_im, 2, GH), ALU.mult)
            pool.drain()
            pool.tensor_tensor(by, by, scr, ALU.subtract)
            pool.drain().then_inc(S["prologue"], 1)
            cx = craw[:, 0, :].rearrange("p (g h) -> p g h", h=GH)
            cy = craw[:, 1, :].rearrange("p (g h) -> p g h", h=GH)

            def angles(e, p):
                gs = bass.ds(e * QG, QG)
                pool.wait_ge(S["half_ready"], e + 1)
                pool.tensor_tensor(ang2[p][:], bc(t8_hi[:, gs], 2, NC), bc(const("chunk"), 1, QG), ALU.mult)
                pool.tensor_tensor(ang_lo2[p][:], bc(t8_lo[:, gs], 2, NC), bc(const("chunk"), 1, QG), ALU.mult)
                pool.drain()
                pool.tensor_tensor(ang_sum2[p][:], ang2[p][:], ang_lo2[p][:], ALU.add).then_inc(S["ang_ready"], 1)

            def inputs(e):
                gs = bass.ds(e * QG, QG)
                x = xs[:, gs, :]
                pool.tensor_tensor(x, x, bc(rstd5[:], 1, QG), ALU.mult)
                pool.drain()
                pool.tensor_tensor(x, x, bc(gain5[:, gs], 2, NC), ALU.mult).then_inc(S["u_ready"], 1)

            def states_out(e, p):
                gs = bass.ds(e * QG, QG)
                pool.wait_ge(S["y_done"], e * 2 + 2)
                pool.tensor_tensor(wout[p][:], bc(pw_re2[:, 1:CH + 1, gs].rearrange("p t g -> p g t"), 3, GH),
                                   bc(cx[:, gs, :], 2, CH), ALU.mult)
                pool.tensor_tensor(wotmp[:], bc(pw_imn[:, 1:CH + 1, gs].rearrange("p t g -> p g t"), 3, GH),
                                   bc(cy[:, gs, :], 2, CH), ALU.mult)
                pool.drain()
                pool.tensor_tensor(wout[p][:], wout[p][:], wotmp[:], ALU.add).then_inc(S["wout_ready"], 1)

            def begin(e, p, use):
                angles(e, p)
                pool.wait_ge(S["prologue"], 2)
                step(e, p, use)

            def step(e, p, use):
                inputs(e)
                angles(e + 1, 1 - p)
                states_out(e, p)

            def finish(e, p, use):
                inputs(e)
                states_out(e, p)

            s5_steps(pool, begin, step, finish)

        def s5_scalar(act):
            act.sem_inc(S["psT_free"], 2)
            act.sem_inc(S["y_evac"], 2)
            act.sem_inc(S["half_ready"], 2)
            act.sem_inc(S["conv_copied"], 1)
            act.sem_inc(S["gelu_ready"], 1)
            act.wait_ge(S["par_landed"], 16)
            act.activation(small[:, 0, :], log_dt, ACT.Exp).then_inc(S["dt"], 1)
            act.wait_ge(S["x_landed"], 16)
            act.activation(xsq[:], xs[:], ACT.Square).then_inc(S["xsq"], 1)
            act.wait_ge(S["turn"], 1)
            act.activation(wave[:], wave[:], ACT.Exp).then_inc(S["mag"], 1)
            act.activation(pw_im[:], turn[:], ACT.Sin, scale=SIN_SCALE)
            act.activation(pw_re[:], turn[:], ACT.Sin, scale=SIN_SCALE / 2)
            act.drain()
            act.activation(pw_re[:], pw_re[:], ACT.Square).then_inc(S["wave"], 1)
            act.wait_ge(S["sumps"], 1)
            act.wait_ge(consts_landed, 32)
            act.activation(rstd5[:], ps[:, 7, 0:NC], ACT.Sqrt, bias=eps, scale=1.0 / D).then_inc(S["std"], 1)

            def angles(e, p):
                act.wait_ge(S["rot_done"], e + 1)
                act.wait_ge(S["ang_reduced"], e + 1)
                act.activation(sin_t[p][:], ang2[p][:], ACT.Sin, scale=SIN_SCALE)
                act.activation(cos_t[p][:], ang2[p][:], ACT.Sin, scale=SIN_SCALE / 2)
                act.drain()
                act.activation(cos_t[p][:], cos_t[p][:], ACT.Square).then_inc(S["half_ready"], 1)
                act.activation(decay[p][:, :, 1:NC], bc(wave[:, CH, bass.ds(e * QG, QG)], 2, NC - 1), ACT.Copy)\
                    .then_inc(S["decay_ready"], 1)
                act.wait_ge(S["u_ready"], e + 1)
                act.wait_ge(S["y_done"], e * 2 + 2)
                act.activation(u_q[p][:], xs[:, bass.ds(e * QG, QG), :], ACT.Copy).then_inc(S["u_copied"], 1)

            def gelu(e, p):
                act.wait_ge(S["yT_ready"], e + 2)
                act.wait_ge(S["ylo_ready"], e + 1)
                act.activation(t32[p][:].rearrange("p (c t) -> p t c", t=CH), ps[:, 7, :].rearrange("p (t c) -> p t c", t=CH),
                               ACT.Gelu_apprx_tanh).then_inc(S["gelu_ready"], 1)
                act.drain()
                act.activation(h_hi[:, bass.ds(e, 1), :], t32[p][:].unsqueeze(1), ACT.Copy).then_inc(S["yhi_ready"], 1)

            def matrices_out(e, p, use):
                act.wait_ge(S["w_ready"], e + 1)
                for b in range(QG // 4):
                    act.wait_ge(S["psT_ready"], e * 2 + (b + 1))
                    src = ps[:, b, :].rearrange("p (g n) -> p g n", g=4)
                    act.activation(win[p][:, 4 * b:4 * b + 4, 0:P], src, ACT.Copy)
                    act.activation(win[p][:, 4 * b:4 * b + 4, P:P + NS], src[:, :, 0:NS], ACT.Copy, scale=-1.0)\
                        .then_inc(S["psT_free"], 1)
                act.wait_ge(S["convps"], e + 2)
                before = use if p else use - 1
                if not (isinstance(before, int) and before == 0):
                    act.wait_ge(toep_landed[1 - p], before * (16 * CH))
                act.activation(conv[:], ps[:, 2, 0:QG * GH].rearrange("p (g h) -> p g h", g=QG), ACT.Copy)\
                    .then_inc(S["conv_copied"], 1)

            def outputs(e):
                act.wait_ge(S["yT_ready"], e + 1)
                for b in range(QG // 4):
                    act.wait_ge(S["y_done"], e * 2 + (b + 5))
                    act.activation(y_q[0:NC, :, 64 * b:64 * (b + 1)].rearrange("p t (g h) -> p g t h", g=4),
                                   ps[0:NC, 5 + b, :].rearrange("p (g t h) -> p g t h", g=4, t=CH), ACT.Copy)\
                        .then_inc(S["y_evac"], 1)

            def begin(e, p, use):
                act.wait_ge(S["prologue"], 2)
                angles(e, p)
                matrices_out(e, p, use)
                angles(e + 1, 1 - p)
                matrices_out(e + 1, 1, 1)
                outputs(e)

            def step(e, p, use):
                angles(e + 1, 1 - p)
                matrices_out(e + 1, 1 - p, use + 1 if p else use)
                gelu(e - 1, 1 - p)
                outputs(e)

            def finish(e, p, use):
                gelu(e - 1, 1 - p)
                for k in range(LOOK):
                    split_hi(act, k)
                outputs(e)
                gelu(e, p)

            s5_steps(act, begin, step, finish)

        def s5_vector(dve):
            dve.sem_inc(S["rot_done"], 2)
            dve.sem_inc(S["ylo_ready"], 2)
            dve.sem_inc(S["w_free"], 1)
            rho, phi, f1, k1 = (small[:, n, :] for n in (1, 2, 3, 4))
            dve.wait_ge(S["dt"], 1)
            dve.tensor_tensor(rho, lam_re, small[:, 0, :], ALU.mult)
            dve.tensor_tensor(phi, lam_im, small[:, 0, :], ALU.mult)
            dve.drain()
            dve.wait_ge(consts_landed, 32)
            tau = bc(const("tau"), 2, G)
            dve.tensor_scalar(f1, phi, 1.0 / (2 * math.pi), None, ALU.mult)
            dve.tensor_tensor(wave[:], bc(rho, 1, CH + 1), tau, ALU.mult)
            dve.drain()
            dve.tensor_scalar(k1, f1, ROUND, -ROUND, ALU.add, ALU.add)
            dve.drain()
            dve.scalar_tensor_tensor(f1, k1, -C1, phi, ALU.mult, ALU.add)
            dve.drain()
            dve.scalar_tensor_tensor(f1, k1, -C2, f1, ALU.mult, ALU.add)
            dve.drain()
            dve.tensor_scalar(f1, f1, 1.0 / (2 * math.pi), None, ALU.mult)
            dve.drain()
            dve.tensor_tensor(turn[:], bc(f1, 1, CH + 1), tau, ALU.mult)
            dve.drain()
            dve.tensor_scalar(pw_imn[:], turn[:], ROUND, -ROUND, ALU.add, ALU.add)
            dve.drain()
            dve.tensor_tensor(turn[:], turn[:], pw_imn[:], ALU.subtract)
            dve.drain()
            dve.tensor_scalar(turn[:], turn[:], 0.5, -0.5, ALU.min, ALU.max).then_inc(S["turn"], 1)
            dve.drain()
            dve.tensor_scalar(t8_hi, turn[:, CH, :], ROUND / 4096, -ROUND / 4096, ALU.add, ALU.add)
            dve.drain()
            dve.tensor_tensor(t8_lo, turn[:, CH, :], t8_hi, ALU.subtract)
            dve.wait_ge(S["xsq"], 1)
            dve.tensor_reduce(sumsq[:], xsq[:].rearrange("p g c -> p c g"), AX_X, ALU.add).then_inc(S["sumsq"], 1)
            dve.wait_ge(S["wave"], 1)
            dve.tensor_scalar(pw_re[:], pw_re[:], -2.0, 1.0, ALU.mult, ALU.add)
            dve.tensor_tensor(pw_im[:], pw_im[:], wave[:], ALU.mult)
            dve.drain()
            dve.tensor_tensor(pw_re[:], pw_re[:], wave[:], ALU.mult)
            sg = const("sign")
            dve.tensor_scalar(pw_ims[:], pw_im[:], sg[:, 0:1], None, ALU.mult)
            dve.tensor_scalar(pw_imn[:], pw_im[:], -1.0, None, ALU.mult)
            dve.drain()
            a1, den, t0, t1, qr, qi, t2, t3 = (small[:, n, :] for n in range(5, 13))
            ai = pw_im[:, 1, :]
            dve.tensor_scalar(a1, pw_re[:, 1, :], -1.0, None, ALU.add)
            dve.tensor_tensor(t0, lam_re, lam_re, ALU.mult)
            dve.tensor_tensor(t1, lam_im, lam_im, ALU.mult)
            dve.drain()
            dve.tensor_tensor(den, t0, t1, ALU.add)
            dve.tensor_tensor(t2, ai, lam_re, ALU.mult)
            dve.tensor_tensor(t3, a1, lam_im, ALU.mult)
            dve.drain()
            dve.reciprocal(den, den)
            dve.tensor_tensor(t0, a1, lam_re, ALU.mult)
            dve.tensor_tensor(t1, ai, lam_im, ALU.mult)
            dve.tensor_tensor(qi, t2, t3, ALU.subtract)
            dve.drain()
            dve.tensor_tensor(qr, t0, t1, ALU.add)
            dve.tensor_tensor(qi, qi, den, ALU.mult)
            dve.drain()
            dve.tensor_tensor(qr, qr, den, ALU.mult)
            dve.tensor_scalar(qi, qi, sg[:, 0:1], None, ALU.mult)
            dve.drain().then_inc(S["ratio"], 1)
            scr = wtmp[:].rearrange("p g t h -> p (g t h)").rearrange("p (g h) -> p g h", h=GH)
            dve.wait_ge(S["bc_landed"], 48)
            dve.tensor_tensor(bx, b_raw[0], bc(qr, 2, GH), ALU.mult)
            dve.tensor_tensor(scr, b_raw[1], bc(qi, 2, GH), ALU.mult)
            dve.tensor_scalar(pw_re2[:], pw_re[:], sg[:, 1:2], None, ALU.mult)
            dve.memset(zin[:], 0.0)
            dve.drain()
            dve.tensor_tensor(bx, bx, scr, ALU.add)
            dve.wait_ge(S["std"], 1)
            dve.tensor_scalar(mean5[:], ps[:, 7, 0:NC], 1.0 / D, EPS, ALU.mult, ALU.add)
            dve.drain()
            root_reciprocal(dve, rstd5[:], mean5[:], nt5[:])
            dve.drain().then_inc(S["prologue"], 1)

            def matrices(e, p):
                gs = bass.ds(e * QG, QG)
                ang, ang_lo, ang_sum = ang2[p], ang_lo2[p], ang_sum2[p]
                dve.wait_ge(S["ang_ready"], e + 1)
                dve.tensor_scalar(ang_sum[:], ang_sum[:], ROUND, -ROUND, ALU.add, ALU.add)
                dve.wait_ge(S["convps"], e + 1)
                dve.tensor_tensor(winT[:], bc(pw_re[:, 0:CH, gs].rearrange("p t g -> p g t"), 3, GH),
                                  bc(bx[:, gs, :], 2, CH), ALU.mult)
                dve.drain()
                dve.tensor_tensor(ang[:], ang[:], ang_sum[:], ALU.subtract)
                dve.tensor_tensor(wtmp[:], bc(pw_ims[:, 0:CH, gs].rearrange("p t g -> p g t"), 3, GH),
                                  bc(by[:, gs, :], 2, CH), ALU.mult)
                dve.drain()
                dve.tensor_tensor(ang[:], ang[:], ang_lo[:], ALU.add)
                dve.tensor_tensor(winT[:], winT[:], wtmp[:], ALU.add).then_inc(S["winT_ready"], 1)
                dve.drain()
                dve.tensor_scalar(ang[:], ang[:], 0.5, -0.5, ALU.min, ALU.max).then_inc(S["ang_reduced"], 1)

            def low(e, p):
                dve.wait_ge(S["yhi_ready"], e + 1)
                at_ = bass.ds(e, 1)
                dve.tensor_tensor(h_lo[:, at_, :], t32[p][:].unsqueeze(1), h_hi[:, at_, :].bitcast(F32), ALU.subtract)\
                    .then_inc(S["ylo_ready"], 1)

            def recurrence(e, p):
                dve.wait_ge(S["w_ready"], e + 3)
                n1 = NC - 1
                wv = ps[:, 3, :].rearrange("p (g c) -> p g c", c=NC)
                wsw = ps[:, 4, :].rearrange("p (g c) -> p g c", c=NC)
                dve.tensor_tensor(zin[:, :, 1:NC], wv[:, :, 0:n1], cos_t[p][:, :, 1:NC], ALU.mult)
                dve.tensor_tensor(ztmp[:, :, 1:NC], wsw[:, :, 0:n1], sin_t[p][:, :, 1:NC], ALU.mult).then_inc(S["w_free"], 1)
                dve.drain()
                dve.tensor_tensor(zin[:, :, 1:NC], zin[:, :, 1:NC], ztmp[:, :, 1:NC], ALU.add)
                dve.drain()
                dve.wait_ge(S["decay_ready"], e + 1)
                dve.tensor_tensor_scan(zst[:].rearrange("p g c -> p (g c)"), decay[p][:].rearrange("p g c -> p (g c)"),
                                       zin[:].rearrange("p g c -> p (g c)"), 0.0, ALU.mult, ALU.add)
                dve.drain()
                dve.wait_ge(S["y_done"], e * 2 + 2)
                dve.tensor_tensor(zout[p][:], zst[:], cos_t[p][:], ALU.mult)
                dve.tensor_tensor(ztmp[NS:P, :, :], zst[0:NS, :, :], sin_t[p][0:NS, :, :], ALU.mult)
                dve.scalar_tensor_tensor(ztmp[0:NS, :, :], zst[NS:P, :, :], -1.0, sin_t[p][NS:P, :, :], ALU.mult, ALU.mult)\
                    .then_inc(S["rot_done"], 1)
                dve.drain()
                dve.tensor_tensor(zout[p][:], zout[p][:], ztmp[:], ALU.add).then_inc(S["s_ready"], 1)

            def tables(e, p):
                dve.wait_ge(S["half_ready"], e + 3)
                dve.tensor_scalar(cos_t[p][:], cos_t[p][:], -2.0, 1.0, ALU.mult, ALU.add)
                dve.wait_ge(S["conv_copied"], e + 2)
                dve.tensor_tensor(conv[0:GH, :, :], conv[0:GH, :, :], dI[0:GH, bass.ds(e * QG, QG), :], ALU.add)
                dve.drain().then_inc(S["conv_ready"], 1)

            def begin(e, p, use):
                dve.wait_ge(S["prologue"], 2)
                matrices(e, p)
                tables(e, p)
                matrices(e + 1, 1 - p)
                recurrence(e, p)
                tables(e + 1, 1 - p)

            def step(e, p, use):
                matrices(e + 1, 1 - p)
                recurrence(e, p)
                tables(e + 1, 1 - p)
                low(e - 1, 1 - p)

            def finish(e, p, use):
                low(e - 1, 1 - p)
                recurrence(e, p)
                low(e, p)

            s5_steps(dve, begin, step, finish)

        def s5_tensor(pe):
            for n, credits in (("convps", 1), ("w_ready", 2), ("y_done", 4), ("yT_ready", 1)):
                pe.sem_inc(S[n], credits)
            pe.wait_ge(consts_landed, 32)
            pe.wait_ge(S["sumsq"], 1)
            pe.matmul(ps[:, 7, 0:NC], const("same_token"), sumsq[:], start=True, stop=True).then_inc(S["sumps"], 1)
            pe.wait_ge(S["prologue"], 2)

            def matrices(e):
                pe.wait_ge(S["winT_ready"], e + 1)
                for b in range(QG // 4):
                    pe.wait_ge(S["psT_free"], e * 2 + (b + 1))
                    for g in range(4 * b, 4 * b + 4):
                        last = pe.transpose(ps[:, b, (g % 4) * P:(g % 4 + 1) * P],
                                            winT[:, g, :, :].rearrange("p t h -> p (t h)"), ident)
                    last.then_inc(S["psT_ready"], 1)
                pe.wait_ge(S["conv_copied"], e + 1)
                for g in range(QG):
                    last = pe.matmul(ps[:, 2, g * GH:(g + 1) * GH], winT[:, g, :, :].rearrange("p t h -> p (t h)"),
                                     cxn[:].rearrange("p (g h) -> p g h", h=GH)[:, bass.ds(e * QG + g, 1), :].rearrange("p a h -> p (a h)"),
                                     start=True, stop=True)
                last.then_inc(S["convps"], 1)

            def inputs(e, p):
                pe.wait_ge(S["u_ready"], e + 1)
                pe.wait_ge(S["w_free"], e + 1)
                pe.wait_ge(S["psT_free"], e * 2 + 4)
                for g in range(QG):
                    for bank, c0 in ((3, 0), (4, NS)):
                        last = pe.matmul(ps[:, bank, g * NC:(g + 1) * NC], win[p][:, g, c0:c0 + P],
                                         xs[:, bass.ds(e * QG + g, 1), :].rearrange("p a c -> p (a c)"), start=True, stop=True)
                last.then_inc(S["w_ready"], 1)

            def outputs(e, p, use):
                pe.wait_ge(toep_landed[p], use * (16 * CH))
                pe.wait_ge(S["wout_ready"], e + 1)
                pe.wait_ge(S["u_copied"], e + 1)
                pe.wait_ge(S["s_ready"], e + 1)
                for b in range(QG // 4):
                    pe.wait_ge(S["y_evac"], e * 2 + (b + 1))
                    for g in range(4 * b, 4 * b + 4):
                        o = ps[0:NC, 5 + b, (g % 4) * P:(g % 4 + 1) * P]
                        pe.matmul(o, u_q[p][:, g, :], toep[p][:, :, g, :], start=True, stop=False)
                        last = pe.matmul(o, zout[p][:, g, :], wout[p][:, g, :, :], start=False, stop=True)
                    last.then_inc(S["y_done"], 1)

            def turn_outputs(e):
                pe.wait_ge(S["y_evac"], e * 2 + 4)
                pe.wait_ge(S["gelu_ready"], e + 1)
                pe.sem_inc(S["yT_begun"], 1)
                for t in range(CH):
                    last = pe.transpose(ps[:, 7, t * NC:(t + 1) * NC], y_q[0:NC, t, :], ident[0:NC, 0:NC])
                last.then_inc(S["yT_ready"], 1)

            def begin(e, p, use):
                matrices(e)
                inputs(e, p)
                matrices(e + 1)
                outputs(e, p, use)
                inputs(e + 1, 1 - p)

            def step(e, p, use):
                turn_outputs(e - 1)
                matrices(e + 1)
                outputs(e, p, use)
                inputs(e + 1, 1 - p)

            def finish(e, p, use):
                turn_outputs(e - 1)
                outputs(e, p, use)
                turn_outputs(e)

            s5_steps(pe, begin, step, finish)

        def done(number):
            return number + 2

        class Gated:
            gate_done = sem("gate_done")
            pair_done = sem("pair_done")
            part_hi = sem("part_hi")
            out_ready = sem("pair_ready")

            def __init__(self, before, name, pairs, in_ready):
                self.before = before
                self.name, self.pairs, self.in_ready = name, pairs, in_ready

        def gated_tensor(pe, ph):
            def products(slot, bank, kt):
                cols = slice(kt * P, (kt + 1) * P)
                return mm3(pe, ps[:, bank, :], w_hi[slot][:, cols], w_lo[slot][:, cols], h_hi[:, kt, :], h_lo[:, kt, :],
                           kt == 0, kt == KT - 1)

            def pair(jj, it=None):
                for half in range(2):
                    slot, number, _ = unit(FIRST[ph.name] + 2 * jj + half, it)
                    pe.wait_ge(lo_ready, number + 1)
                    for kt in range(KT):
                        last = products(slot, 2 * jj + half, kt)
                    last.then_inc(unit_used, 1)

            pe.wait_ge(ph.pair_done, ph.before + 2)
            first = [unit(FIRST[ph.name] + half) for half in range(2)]
            pe.wait_ge(lo_ready, first[1][1] + 1)
            for kt in range(KT):
                pe.wait_ge(*ph.in_ready(kt + 1))
                for half in range(2):
                    last = products(first[half][0], half, kt)
                    if kt == KT - 1:
                        last.then_inc(unit_used, 1)
            pair(1)
            with pe.Fori(1, ph.pairs // 2) as it:
                for jj in range(2):
                    pe.wait_ge(ph.pair_done, it * 2 + (ph.before + jj + 1))
                    pair(jj, it)

        def ffn_scalar(act, ph):
            with act.Fori(0, ph.pairs // 2) as it:
                for jj in range(2):
                    k = FIRST[ph.name] + 2 * jj
                    split_hi(act, k + LOOK, it)
                    split_hi(act, k + 1 + LOOK, it)
                    act.wait_ge(ph.pair_done, it * 2 + (ph.before + jj + 1))
                    act.wait_ge(unit_used, done(unit(k, it)[1]))
                    act.activation(sq[jj][:], ps[:, 2 * jj, :], ACT.Silu).then_inc(ph.gate_done, 1)
                    act.wait_ge(ph.pair_done, it * 2 + (ph.before + jj + 3))
                    act.activation(hid_hi[:, bass.ds(it * 2 + jj, 1), :], t32[jj][:].unsqueeze(1), ACT.Copy)\
                        .then_inc(ph.part_hi, 1)

        def ffn_vector(dve, ph):
            with dve.Fori(0, ph.pairs // 2) as it:
                for jj in range(2):
                    k = FIRST[ph.name] + 2 * jj
                    dve.wait_ge(ph.gate_done, it * 2 + (ph.before + jj + 1))
                    dve.wait_ge(unit_used, done(unit(k + 1, it)[1]))
                    dve.tensor_tensor(t32[jj][:], ps[:, 2 * jj + 1, :], sq[jj][:], ALU.mult).then_inc(ph.pair_done, 1)
                    dve.wait_ge(ph.part_hi, it * 2 + (ph.before + jj + 1))
                    at_ = bass.ds(it * 2 + jj, 1)
                    dve.tensor_tensor(hid_lo[:, at_, :], t32[jj][:].unsqueeze(1), hid_hi[:, at_, :].bitcast(F32),
                                      ALU.subtract).then_inc(ph.out_ready, 1)

        def glu_scalar(act, ph):
            with act.Fori(0, ph.pairs // 2) as it:
                for jj in range(2):
                    k = FIRST[ph.name] + 2 * jj
                    split_hi(act, k + LOOK, it)
                    split_hi(act, k + 1 + LOOK, it)
                    act.wait_ge(ph.pair_done, it * 2 + (ph.before + jj + 1))
                    act.wait_ge(unit_used, done(unit(k, it)[1]))
                    act.activation(t32[jj][:], ps[:, 2 * jj, :], ACT.Sigmoid).then_inc(ph.gate_done, 1)
                    act.wait_ge(ph.pair_done, it * 2 + (ph.before + jj + 3))
                    act.activation(sq[jj][:], xT[:, bass.ds(it * 2 + jj, 1), :].rearrange("p a t -> p (a t)"), ACT.Square)\
                        .then_inc(ph.part_hi, 1)

        def glu_vector(dve, ph):
            dve.sem_inc(ph.pair_done, 2)
            dve.memset(acc[:], 0.0)
            dve.wait_ge(S["xT_landed"], 16)
            with dve.Fori(0, ph.pairs // 2) as it:
                for jj in range(2):
                    k = FIRST[ph.name] + 2 * jj
                    tile = xT[:, bass.ds(it * 2 + jj, 1), :].rearrange("p a t -> p (a t)")
                    dve.wait_ge(ph.gate_done, it * 2 + (ph.before + jj + 1))
                    dve.wait_ge(unit_used, done(unit(k + 1, it)[1]))
                    dve.tensor_tensor(t32[jj][:], ps[:, 2 * jj + 1, :], t32[jj][:], ALU.mult)
                    dve.drain()
                    dve.tensor_tensor(tile, tile, t32[jj][:], ALU.add).then_inc(ph.pair_done, 1)
                    dve.wait_ge(ph.part_hi, it * 2 + (ph.before + jj + 1))
                    dve.tensor_tensor(acc[:], acc[:], sq[jj][:], ALU.add).then_inc(ph.out_ready, 1)

        class Rows:

            tile_done = sem("rows_tile_done")
            x_ready = sem("rows_x_ready")
            sq_ready = sem("rows_sq_ready")
            acc_ready = sem("rows_acc_ready")

            def __init__(self, nth, name, k_tiles, src_hi, src_lo, in_ready):
                self.before = nth * KT
                self.name, self.k_tiles, self.src_hi, self.src_lo, self.in_ready = name, k_tiles, src_hi, src_lo, in_ready

        LAST = 2

        def rows_tensor(pe, ph, banks):
            n0, n = FIRST[ph.name], ph.k_tiles

            def products(k, kt, o, it=None, start=False, stop=False):
                slot = k % R
                cols = slice(o * P, (o + 1) * P)
                if it is None:
                    ah, al = ph.src_hi[:, kt, :], ph.src_lo[:, kt, :]
                else:
                    one = bass.ds(it * R + kt, 1)
                    ah, al = (s[:, one, :].rearrange("p a t -> p (a t)") for s in (ph.src_hi, ph.src_lo))
                return mm3(pe, ps[:, o, :], w_hi[slot][:, cols], w_lo[slot][:, cols], ah, al, start, stop)

            def whole(kt, it=None):
                _, number, _ = unit(n0 + kt, it)
                pe.wait_ge(lo_ready, number + 1)
                pe.wait_ge(*ph.in_ready((kt if it is None else it * R + kt) + 1))
                for o, wait in banks if kt == 0 and it is None else [(o, None) for o in range(KT)]:
                    if wait is not None:
                        pe.wait_ge(*wait)
                    last = products(n0 + kt, kt, o, it, start=(kt == 0 and it is None))
                last.then_inc(unit_used, 1)

            head = (n - R) % R or R
            for kt in range(head):
                whole(kt)
            if n - R > head:
                with pe.Fori(0, (n - R - head) // R) as it:
                    for kt in range(R):
                        whole(head + kt, it)
            for kt in range(n - R, n - LAST):
                whole(kt)
            pe.wait_ge(lo_ready, n0 + n)
            pe.wait_ge(*ph.in_ready(n))
            for o in range(KT):
                for kt in range(n - LAST, n):
                    last = products(n0 + kt, kt, o, stop=(kt == n - 1))
                last.then_inc(ph.tile_done, 1)
            pe.drain().then_inc(unit_used, LAST)

        def rows_scalar(act, ph):
            n0, n = FIRST[ph.name], ph.k_tiles
            head = (n - R) % R or R
            for kt in range(head):
                split_hi(act, n0 + kt + LOOK)
            if n - R > head:
                with act.Fori(0, (n - R - head) // R) as it:
                    for kt in range(R):
                        split_hi(act, n0 + head + kt + LOOK, it)
            for kt in range(n - R, n - LAST + 1):
                split_hi(act, n0 + kt + LOOK)
            for o in range(KT):
                act.wait_ge(ph.x_ready, ph.before + o + 1)
                act.activation(sq[o % 2][:], xT[:, o, :], ACT.Square).then_inc(ph.sq_ready, 1)
            for kt in range(n - LAST + 1, n):
                split_hi(act, n0 + kt + LOOK)

        def rows_vector(dve, ph):
            dve.memset(acc[:], 0.0)
            dve.drain()

            def add_square(o):
                dve.wait_ge(ph.sq_ready, ph.before + o + 1)
                if o:
                    dve.wait_ge(ph.acc_ready, ph.before + o)
                dve.tensor_tensor(acc[:], acc[:], sq[o % 2][:], ALU.add).then_inc(ph.acc_ready, 1)

            for o in range(KT):
                dve.wait_ge(ph.tile_done, ph.before + o + 1)
                dve.tensor_tensor(xT[:, o, :], xT[:, o, :], ps[:, o, :], ALU.add).then_inc(ph.x_ready, 1)
                if o:
                    add_square(o - 1)
            add_square(KT - 1)

        class Norm:
            sum_ready = sem("norm_sum_ready")
            mean_ready = sem("norm_mean_ready")
            std_ready = sem("norm_std_ready")
            rstd_ready = sem("norm_rstd_ready")
            rstd_spread = sem("norm_spread")
            n32_ready = sem("norm_n32_ready")
            hi_done = sem("norm_hi_done")
            h_ready = sem("norm_h_ready")

            def __init__(self, nth, name, acc_ready):
                self.nth, self.before = nth, nth * KT
                self.name, self.acc_ready = name, acc_ready

        def norm_tensor(pe, nm):
            pe.wait_ge(*nm.acc_ready(KT))
            for tb in range(TB):
                last = pe.matmul(ps[:, 7, tb:tb + 1], acc[:, tb * P:(tb + 1) * P], ones[:, 0:1], start=True, stop=True)
            last.then_inc(nm.sum_ready, 1)
            pe.wait_ge(nm.rstd_ready, nm.nth + 1)
            for tb in range(TB):
                last = pe.matmul(ps[:, 7, tb * P:(tb + 1) * P], tok_rstd[:, tb:tb + 1].broadcast_to([P, P]), ident, start=True, stop=True)
            last.then_inc(nm.rstd_spread, 1)

        def norm_scalar(act, nm, tiles=KT):
            act.wait_ge(nm.mean_ready, nm.nth + 1)
            act.activation(tok_rstd[:], tok_mean[:], ACT.Sqrt).then_inc(nm.std_ready, 1)
            for o in range(tiles):
                act.wait_ge(nm.n32_ready, nm.before + o + 1)
                act.activation(h_hi[:, o, :], t32[o % 2][:], ACT.Copy).then_inc(nm.hi_done, 1)

        def token_factors(dve, nm):
            dve.wait_ge(nm.sum_ready, nm.nth + 1)
            dve.tensor_scalar(tok_mean[:], ps[:, 7, 0:TB], 1.0 / D, EPS, ALU.mult, ALU.add).then_inc(nm.mean_ready, 1)
            dve.wait_ge(nm.std_ready, nm.nth + 1)
            root_reciprocal(dve, tok_rstd[:], tok_mean[:], tok_tmp[:])
            dve.sem_inc(nm.rstd_ready, 1)
            dve.wait_ge(nm.rstd_spread, nm.nth + 1)

        def norm_vector(dve, nm):
            token_factors(dve, nm)
            g0 = VEC_AT[nm.name]

            def low(o):
                dve.wait_ge(nm.hi_done, nm.before + o + 1)
                dve.tensor_tensor(h_lo[:, o, :], t32[o % 2][:], h_hi[:, o, :].bitcast(F32), ALU.subtract).then_inc(nm.h_ready, 1)

            for o in range(KT):
                if o >= 2:
                    dve.wait_ge(nm.h_ready, nm.before + o - 1)
                dve.scalar_tensor_tensor(t32[o % 2][:], xT[:, o, :], vec[:, g0 + o:g0 + o + 1], ps[:, 7, :], ALU.mult, ALU.mult)\
                    .then_inc(nm.n32_ready, 1)
                if o:
                    low(o - 1)
            low(KT - 1)

        BLOCKS = [3, 2, 0, 1]
        P_AT = {3: 0, 2: 4 * P, 0: 7 * P, 1: 8 * P}
        L_AT = {3: (0, 0), 2: (1, 0), 0: (1, 3 * P), 1: (2, 0)}
        T_AT = {0: (3, 0), 1: (4, 0), 3: (4, 3 * P), 2: (5, 0)}
        PT_AT = {kb: (bank - 3) * T + c for kb, (bank, c) in T_AT.items()}
        N_P = P * TB * (TB + 1) // 2
        PR_BUFS, PT_BUFS = 3, 2

        class Attention:

            def __init__(self, name, heads, qT, kT, val, mask, pr, pt, nmax, den, hi, lo):
                self.heads, self.qT, self.kT, self.val, self.mask = heads, qT, kT, val, mask
                self.pr, self.pt, self.nmax, self.den, self.hi, self.lo = pr, pt, nmax, den, hi, lo
                self.L_ready = sem(name + "_L_ready")
                self.masked = sem(name + "_masked")
                self.p_ready = sem(name + "_p_ready")
                self.r_ready = sem(name + "_r_ready")
                self.scaled = sem(name + "_scaled")
                self.pT_ready = sem(name + "_pT_ready")
                self.pt_out = sem(name + "_pt_out")
                self.pv_done = sem(name + "_pv_done")
                self.o_hi = sem(name + "_o_hi")
                self.o_done = sem(name + "_o_done")

            def tiles_ready(self, n):
                return self.o_done, 2 * n

        def attn_tensor(pe, a):
            def logits(h):
                rows = slice(HD * (h % 2), HD * (h % 2 + 1))
                for k, tb in enumerate(BLOCKS):
                    bank, c = L_AT[tb]
                    if h and tb != 0:
                        pe.wait_ge(a.masked, TB * (h - 1) + {3: 1, 2: 3, 1: 4}[tb])
                    keys = (tb + 1) * P
                    last = pe.matmul(ps[:, bank, c:c + keys], a.qT[rows, h // 2, tb * P:(tb + 1) * P], a.kT[rows, h // 2, 0:keys],
                                     start=True, stop=True)
                    if tb != 2:
                        last.then_inc(a.L_ready, 1)

            def turn(h):
                pe.wait_ge(a.scaled, h + 1)
                for bank, kbs in ((3, (0,)), (4, (1, 3)), (5, (2,))):
                    if h:
                        pe.wait_ge(a.pt_out, 3 * (h - 1) + bank - 2)
                    for kb in kbs:
                        for tb in range(kb, TB):
                            c = T_AT[kb][1] + (tb - kb) * P
                            p = P_AT[tb] + kb * P
                            last = pe.transpose(ps[:, bank, c:c + P], a.pr[h % PR_BUFS][:, p:p + P], ident)
                    last.then_inc(a.pT_ready, 1)

            def values(h):
                pe.wait_ge(a.pt_out, 3 * (h + 1))
                if h >= 2:
                    pe.wait_ge(a.o_done, h - 1)
                for kb in range(TB):
                    n = T - kb * P
                    last = pe.matmul(ps[:, 6 + h % 2, kb * P:T], a.val[:, kb, (h // 2) * P:(h // 2 + 1) * P],
                                     a.pt[h % PT_BUFS][:, PT_AT[kb]:PT_AT[kb] + n], start=(kb == 0), stop=(kb == TB - 1))
                last.then_inc(a.pv_done, 1)

            logits(0)
            logits(1)
            for h in range(a.heads):
                turn(h)
                if h + 2 < a.heads:
                    logits(h + 2)
                if h:
                    values(h - 1)
            values(a.heads - 1)

        def attn_scalar(act, a):
            def block(tb):
                return slice(P_AT[tb], P_AT[tb] + (tb + 1) * P)

            def exps(h):
                for k, tb in enumerate(BLOCKS):
                    act.wait_ge(a.masked, TB * h + k + 1)
                    p, n = a.pr[h % PR_BUFS][:, block(tb)], h * TB + tb
                    last = act.activation(p, p, ACT.Exp, bias=a.nmax[:, n:n + 1], scale=-1.0, accum_out=a.den[:, n:n + 1])
                last.then_inc(a.p_ready, 1)

            def scale(h):
                act.wait_ge(a.r_ready, h + 1)
                for tb in BLOCKS:
                    p, n = a.pr[h % PR_BUFS][:, block(tb)], h * TB + tb
                    last = act.activation(p, p, ACT.Copy, scale=a.den[:, n:n + 1])
                last.then_inc(a.scaled, 1)

            def high(h):
                act.wait_ge(a.pv_done, h + 1)
                rows = slice(HD * (h % 2), HD * (h % 2 + 1))
                act.activation(a.hi[rows, h // 2, :], ps[rows, 6 + h % 2, :], ACT.Copy).then_inc(a.o_hi, 1)

            exps(0)
            scale(0)
            exps(1)
            for h in range(a.heads):
                if h + 1 < a.heads:
                    scale(h + 1)
                if h >= 2:
                    high(h - 2)
                if h + 2 < a.heads:
                    exps(h + 2)
            high(a.heads - 2)
            high(a.heads - 1)

        def attn_vector(dve, a):
            def masks(h):
                if h >= PR_BUFS:
                    dve.wait_ge(a.pT_ready, 3 * (h - PR_BUFS + 1))
                for tb in BLOCKS:
                    bank, c = L_AT[tb]
                    keys, n = (tb + 1) * P, h * TB + tb
                    dve.wait_ge(a.L_ready, 3 * h + bank + 1)
                    dve.tensor_tensor_reduce(out=a.pr[h % PR_BUFS][:, P_AT[tb]:P_AT[tb] + keys], in0=ps[:, bank, c:c + keys],
                                             in1=a.mask(tb, h), scale=-(HD ** -0.5), scalar=3e38, op0=ALU.add, op1=ALU.min,
                                             accum_out=a.nmax[:, n:n + 1]).then_inc(a.masked, 1)

            def reciprocals(h):
                dve.wait_ge(a.p_ready, h + 1)
                r = a.den[:, h * TB:(h + 1) * TB]
                dve.reciprocal(r, r).then_inc(a.r_ready, 1)

            def turned_out(h):
                if h >= PT_BUFS:
                    dve.wait_ge(a.pv_done, h - PT_BUFS + 1)
                for k in range(3):
                    n = T if k < 2 else N_P - 2 * T
                    dve.wait_ge(a.pT_ready, 3 * h + k + 1)
                    dve.tensor_copy(a.pt[h % PT_BUFS][:, k * T:k * T + n], ps[:, 3 + k, 0:n]).then_inc(a.pt_out, 1)

            def low(h):
                dve.wait_ge(a.o_hi, h + 1)
                rows = slice(HD * (h % 2), HD * (h % 2 + 1))
                dve.tensor_tensor(a.lo[rows, h // 2, :], ps[rows, 6 + h % 2, :], a.hi[rows, h // 2, :].bitcast(F32), ALU.subtract)\
                    .then_inc(a.o_done, 1)

            masks(0)
            reciprocals(0)
            masks(1)
            for h in range(a.heads):
                if h + 1 < a.heads:
                    reciprocals(h + 1)
                turned_out(h)
                if h + 2 < a.heads:
                    masks(h + 2)
                if h >= 2:
                    low(h - 2)
            low(a.heads - 2)
            low(a.heads - 1)

        o6 = [BIGR]

        def dsabuf(name, shape, parts=P):
            off = o6[0]
            o6[0] += -(-4 * int(np.prod(shape)) // 32) * 32
            assert o6[0] <= end, name
            return at(name, shape, off)

        qT = dsabuf("qT", [KT, T])
        kT = dsabuf("kT", [KT, T])
        val = dsabuf("val", [TB, D])
        raw_off = o6[0]
        rawp = [dsabuf(f"rawp{n}", [TB, GROUP]) for n in range(2)]
        rope_off = o6[0]
        rope_a = dsabuf("rope_a", [2, GROUP])
        rope_b = dsabuf("rope_b", [2, GROUP])
        qi_off = o6[0]
        qiT = dsabuf("qiT", [IH // 2, T])
        kiT = dsabuf("kiT", [T])
        kin = dsabuf("kin", [TB, 2 * HD])
        rope = dsabuf("rope", [2, TB, HD])
        hgain = dsabuf("hgain", [2, HD])
        rtab = dsabuf("rtab", [2, 2, TB, HD])
        wi = dsabuf("wi", [TB, IH])
        hsum, hstd, htmp = (dsabuf(n, [TB * 8]) for n in ("hsum", "hstd", "htmp"))
        kisum, kistd, kitmp = (dsabuf(n, [TB]) for n in ("kisum", "kistd", "kitmp"))
        nmax = dsabuf("nmax", [TB * NH])
        den = dsabuf("den", [TB * NH])
        top8 = dsabuf("top8", [3, 8])
        hsq = at("hsq", [TB, GROUP], rope_off)
        pr = [at(f"pr{n}", [N_P], raw_off + 4 * N_P * n) for n in range(PR_BUFS)]
        pt = [at(f"pt{n}", [N_P], raw_off + 4 * N_P * (PR_BUFS + n)) for n in range(PT_BUFS)]
        assert raw_off + 4 * N_P * (PR_BUFS + PT_BUFS) <= qi_off + 8 * KB
        score = [None] + [at(f"score{n}", [T], SCR + 2 * KB * (1 + n)) for n in range(3)]
        relu = [at(f"relu{n}", [T], SCR + 8 * KB + 2 * KB * n) for n in range(2)]

        A = {n: sem("dsa_" + n) for n in (
            "par_landed", "raw_ready", "sums_ready", "std_ready", "roped", "tr_ready", "tr_evac", "rem_copied", "rem_turned", "rem_ready", "ki_sums",
            "ki_std", "ki_ready", "val_ready", "idx_ready", "relu_ready", "relu_used")}
        att1 = Attention("att1", NH, qT, kT, val,
                         lambda tb, h: const("causal") if tb == 0 else score[tb][:, 0:(tb + 1) * P], pr, pt, nmax, den, h_hi, h_lo)
        QI, REM, Q0, Q1, K0, K1, V0, V1 = range(8)
        HALF = {QI: 0, REM: 1, Q0: 0, Q1: 1, K0: 0, K1: 1, V0: 0, V1: 1}
        UNIT_OF = {QI: 0, REM: 4, Q0: 5, Q1: 9, K0: 13, K1: 17, V0: 21, V1: 25}
        ROT = [QI, Q0, Q1, K0, K1]
        RAWBUF = {g: n % 2 for n, g in enumerate(ROT)}
        n_dsa = FIRST["dsa"] if "dsa" in FIRST else 0

        def end_of(g):
            return n_dsa + UNIT_OF[g] + (0 if g == REM else 3)

        def project_narrow(pe, w0, width, copied, buf):
            slot, number, _ = unit(w0)
            pe.wait_ge(lo_ready, number + 1)
            for kt in range(KT):
                cols = slice(kt * P, kt * P + width)
                last = mm3(pe, ps[0:width, 4, :], w_hi[slot][:, cols], w_lo[slot][:, cols], h_hi[:, kt, :], h_lo[:, kt, :],
                           kt == 0, kt == KT - 1)
            last.then_inc(unit_used, 1)
            pe.wait_ge(copied, 1)
            for tb in range(TB):
                last = pe.transpose(ps[:, 4 + tb, 0:width], buf[0:width, tb * P:(tb + 1) * P], ident[0:width, 0:width])
            return last

        def project(pe, w0, group_half, units, in_ready=None, width=GROUP, n_kt=2):
            for u in range(units):
                slot, number, _ = unit(w0 + u)
                pe.wait_ge(lo_ready, number + 1)
                for k2 in range(n_kt):
                    kt = u * n_kt + k2
                    if in_ready is not None:
                        pe.wait_ge(*in_ready(kt + 1))
                    step = UNIT // n_kt
                    wh, wl = w_hi[slot][:, k2 * step:k2 * step + width], w_lo[slot][:, k2 * step:k2 * step + width]
                    for tb in range(TB):
                        toks = slice(tb * P, (tb + 1) * P)
                        o = ps[:, 4 * group_half + tb, 0:width]
                        pe.matmul(o, h_hi[:, kt, toks], wh, start=(kt == 0), stop=False)
                        pe.matmul(o, h_hi[:, kt, toks], wl, start=False, stop=False)
                        last = pe.matmul(o, h_lo[:, kt, toks], wh, start=False, stop=(kt == KT - 1))
                last.then_inc(unit_used, 1)

        def dsa_tensor(pe, nm):
            def proj(g, in_ready=None):
                if g == REM:
                    project_narrow(pe, n_dsa + UNIT_OF[g], HD + IH, A["rem_copied"], relu[1]).then_inc(A["rem_turned"], 1)
                else:
                    project(pe, n_dsa + UNIT_OF[g], HALF[g], 4, in_ready)

            def transposes(g):
                n = ROT.index(g)
                pe.wait_ge(A["roped"], n + 1)
                for c in range(4):
                    for tb in range(TB):
                        last = pe.transpose(ps[:, 4 * HALF_T[g] + c, tb * P:(tb + 1) * P], rawp[RAWBUF[g]][:, tb, c * P:(c + 1) * P], ident)
                    last.then_inc(A["tr_ready"], 1)

            HALF_T = {QI: 1, Q0: 0, Q1: 1, K0: 0, K1: 1}
            proj(QI, after(nm.h_ready, nm.before))
            proj(REM)
            pe.wait_ge(A["raw_ready"], 1)
            proj(Q0)
            pe.wait_ge(A["rem_ready"], 1)
            transposes(QI)
            pe.wait_ge(A["ki_ready"], 1)
            pe.wait_ge(A["tr_evac"], 1)
            for tb in range(TB):
                last = pe.transpose(ps[:, 4, tb * P:(tb + 1) * P], kin[:, tb, :], ident)
            last.then_inc(A["tr_ready"], 1)
            pe.wait_ge(A["tr_evac"], 5)
            for n in range(3 * IH):
                tb, h = 1 + n // IH, n % IH
                rows = slice(HD * (h % 2), HD * (h % 2 + 1))
                keys = (tb + 1) * P
                if n >= 2:
                    pe.wait_ge(A["relu_ready"], n - 1)
                pe.matmul(ps[:, 4 + n % 2, 0:keys], qiT[rows, h // 2, tb * P:(tb + 1) * P], kiT[rows, 0:keys],
                          start=True, stop=True).then_inc(A["idx_ready"], 1)
            pe.wait_ge(A["relu_ready"], 3 * IH)
            for g, before in ((Q1, Q0), (K0, Q1), (K1, K0), (V0, K1)):
                proj(g)
                if g == V0:
                    break
                pe.wait_ge(A["raw_ready"], ROT.index(before) + 1)
                transposes(before)
                pe.wait_ge(A["tr_evac"], 5 + 4 * ROT.index(before))
            transposes(K1)
            pe.wait_ge(A["tr_evac"], 5 + 4 * 4)
            proj(V1)
            pe.wait_ge(A["val_ready"], 2)
            attn_tensor(pe, att1)

        def dsa_scalar(act):
            def split(g, u):
                split_hi(act, n_dsa + UNIT_OF[g] + u + LOOK)

            def raw_out(g):
                n = ROT.index(g)
                act.wait_ge(unit_used, done(end_of(g)))
                if n >= 2:
                    act.wait_ge(A["tr_ready"], 4 * (n - 1) + (1 if n >= 2 else 0))
                for tb in range(TB):
                    last = act.activation(rawp[RAWBUF[g]][:, tb, :], ps[:, 4 * HALF[g] + tb, :], ACT.Copy)
                if g != QI:
                    act.wait_ge(A["roped"], n)
                    for tb in range(TB):
                        last = act.activation(hsq[:, tb, :], ps[:, 4 * HALF[g] + tb, :], ACT.Square)
                last.then_inc(A["raw_ready"], 1)

            def std(g):
                n = ROT.index(g)
                act.wait_ge(A["sums_ready"], n)
                act.activation(hstd[:], hsum[:], ACT.Sqrt).then_inc(A["std_ready"], 1)

            def tr_out(g):
                n = ROT.index(g)
                first = 4 * n + (1 if n else 0)
                for c in range(4):
                    act.wait_ge(A["tr_ready"], first + c + 1)
                    o = {QI: qiT[:, c, :], Q0: qT[:, c, :], Q1: qT[:, 4 + c, :], K0: kT[:, c, :], K1: kT[:, 4 + c, :]}[g]
                    half = {QI: 1, Q0: 0, Q1: 1, K0: 0, K1: 1}[g]
                    act.activation(o, ps[:, 4 * half + c, :], ACT.Copy).then_inc(A["tr_evac"], 1)

            for u in range(4):
                split(QI, u)
            raw_out(QI)
            split(REM, 0)
            act.wait_ge(unit_used, done(end_of(REM)))
            act.activation(relu[1][0:HD + IH, :], ps[0:HD + IH, 4, :], ACT.Copy).then_inc(A["rem_copied"], 1)
            act.wait_ge(A["rem_turned"], 1)
            for tb in range(TB):
                act.activation(kin[:, tb, 0:HD], ps[:, 4 + tb, 0:HD], ACT.Copy)
                act.activation(wi[:, tb, :], ps[:, 4 + tb, HD:HD + IH], ACT.Copy, scale=float(np.float32(IH ** -0.5)) * HD ** -0.5)
                last = act.activation(relu[0][:, 0:HD], ps[:, 4 + tb, 0:HD], ACT.Square, accum_out=kisum[:, tb:tb + 1])
                act.drain()
            last = act.activation(kistd[:], kisum[:], ACT.Sqrt, bias=eps, scale=1.0 / HD)
            last.then_inc(A["rem_ready"], 1)
            for u in range(4):
                split(Q0, u)
            tr_out(QI)
            act.wait_ge(A["tr_ready"], 5)
            act.activation(kiT[:], ps[:, 4, :], ACT.Copy).then_inc(A["tr_evac"], 1)
            for n in range(3 * IH):
                tb = 1 + n // IH
                keys = (tb + 1) * P
                act.wait_ge(A["idx_ready"], n + 1)
                if n >= 2:
                    act.wait_ge(A["relu_used"], n - 1)
                act.activation(relu[n % 2][:, 0:keys], ps[:, 4 + n % 2, 0:keys], ACT.Relu).then_inc(A["relu_ready"], 1)
            for g, before in ((Q1, Q0), (K0, Q1), (K1, K0), (V0, K1)):
                split(g, 0)
                raw_out(before)
                split(g, 1)
                std(before)
                split(g, 2)
                split(g, 3)
                tr_out(before)
            for half, g in ((0, V0), (1, V1)):
                if g == V1:
                    for u in range(4):
                        split(V1, u)
                act.wait_ge(unit_used, done(end_of(g)))
                for tb in range(TB):
                    last = act.activation(val[:, tb, half * GROUP:(half + 1) * GROUP], ps[:, 4 * HALF[g] + tb, :], ACT.Copy)
                last.then_inc(A["val_ready"], 1)
            attn_scalar(act, att1)

        def dsa_vector(dve):
            dve.wait_ge(A["par_landed"], 32)
            for which in range(2):
                for part in range(2):
                    dve.tensor_tensor(rtab[:, which, part, :, :], rope[:, part, :, :], bc(hgain[:, which, :], 1, TB), ALU.mult)
            dve.drain()
            HH = HD // 2

            def rotate(g):
                buf = rawp[RAWBUF[g]]
                cs = [rope[:, part, :, :] for part in range(2)] if g == QI else \
                    [rtab[:, 0 if g in (Q0, Q1) else 1, part, :, :] for part in range(2)]
                for half in range(2):
                    tbs = slice(2 * half, 2 * half + 2)
                    x = buf[:, tbs, :].rearrange("p b (h d) -> p b h d", d=HD)
                    a, b = (t[:].rearrange("p b (h d) -> p b h d", d=HD) for t in (rope_a, rope_b))
                    dve.tensor_tensor(a, x, bc(cs[0][:, tbs, :], 2, 8), ALU.mult)
                    dve.tensor_tensor(b, x, bc(cs[1][:, tbs, :], 2, 8), ALU.mult)
                    dve.drain()
                    dve.tensor_tensor(x[:, :, :, 0:HH], a[:, :, :, 0:HH], b[:, :, :, HH:HD], ALU.subtract)
                    last = dve.tensor_tensor(x[:, :, :, HH:HD], a[:, :, :, HH:HD], b[:, :, :, 0:HH], ALU.add)
                    if half == 0:
                        dve.drain()
                last.then_inc(A["roped"], 1)

            def head_sums(g):
                dve.wait_ge(A["raw_ready"], ROT.index(g) + 1)
                dve.tensor_reduce(hsum[:], hsq[:].rearrange("p b (h d) -> p (b h) d", d=HD), AX_X, ALU.add)
                dve.drain()
                dve.tensor_scalar(hsum[:], hsum[:], 1.0 / HD, EPS, ALU.mult, ALU.add).then_inc(A["sums_ready"], 1)

            def head_norm(g):
                dve.wait_ge(A["std_ready"], ROT.index(g))
                root_reciprocal(dve, hstd[:], hsum[:], htmp[:])
                x = rawp[RAWBUF[g]][:].rearrange("p b (h d) -> p (b h) d", d=HD)
                dve.tensor_tensor(x, x, bc(hstd[:], 2, HD), ALU.mult)
                dve.drain()
                rotate(g)

            dve.wait_ge(A["raw_ready"], 1)
            rotate(QI)
            dve.wait_ge(A["rem_ready"], 1)
            dve.tensor_scalar(kisum[:], kisum[:], 1.0 / HD, EPS, ALU.mult, ALU.add)
            dve.drain()
            root_reciprocal(dve, kistd[:], kisum[:], kitmp[:])
            ki = kin[:, :, 0:HD]
            dve.tensor_tensor(ki, ki, bc(kistd[:], 2, HD), ALU.mult)
            dve.drain()
            a, b = (t[:].rearrange("p b n -> p (b n)")[:, 0:TB * HD].rearrange("p (b d) -> p b d", d=HD) for t in (rope_a, rope_b))
            dve.tensor_tensor(a, ki, rope[:, 0, :, :], ALU.mult)
            dve.tensor_tensor(b, ki, rope[:, 1, :, :], ALU.mult)
            dve.drain()
            for copy in range(2):
                o = kin[:, :, copy * HD:(copy + 1) * HD]
                dve.tensor_tensor(o[:, :, 0:HH], a[:, :, 0:HH], b[:, :, HH:HD], ALU.subtract)
                last = dve.tensor_tensor(o[:, :, HH:HD], a[:, :, HH:HD], b[:, :, 0:HH], ALU.add)
            last.then_inc(A["ki_ready"], 1)
            for tb in range(1, TB):
                dve.memset(score[tb][:, 0:tb * P], 0.0)
                dve.tensor_copy(score[tb][:, tb * P:(tb + 1) * P], const("causal"))
            dve.drain()
            for n in range(3 * IH):
                tb, h = 1 + n // IH, n % IH
                keys = (tb + 1) * P
                dve.wait_ge(A["relu_ready"], n + 1)
                if n:
                    dve.wait_ge(A["relu_used"], n)
                dve.scalar_tensor_tensor(score[tb][:, 0:keys], relu[n % 2][:, 0:keys], wi[:, tb, h:h + 1], score[tb][:, 0:keys],
                                         ALU.mult, ALU.add).then_inc(A["relu_used"], 1)
            dve.drain()

            def select(rounds):
                with dve.Fori(0, rounds):
                    for tb in range(1, TB):
                        dve.max(top8[:, tb - 1, :], score[tb][:, 0:(tb + 1) * P])
                    dve.drain()
                    for tb in range(1, TB):
                        s = score[tb][:, 0:(tb + 1) * P]
                        dve.match_replace(s, top8[:, tb - 1, :], s, TAKEN)
                    dve.drain()

            for g in (Q0, Q1, K0, K1):
                head_sums(g)
                select(1)
                head_norm(g)
                select(1)
            select(TOPK // 8 - 8)
            for tb in range(1, TB):
                s = score[tb][:, 0:(tb + 1) * P]
                dve.tensor_scalar(s, s, -1e37, -BIG, ALU.is_gt, ALU.mult)
            dve.drain()

            attn_vector(dve, att1)

        o7 = [BIGR]

        def mixbuf(name, shape, dt=F32):
            off = o7[0]
            o7[0] += -(-4 * int(np.prod(shape)) // 32) * 32
            assert o7[0] <= end, name
            return at(name, shape, off, dt)

        v2 = mixbuf("v2", [TB, GROUP])
        conv_off = o7[0]
        convT = mixbuf("convT", [XT + LT, T])
        gqk_off = o7[0]
        gqkT = mixbuf("gqkT", [12, T])
        z2 = mixbuf("z2", [TB, GROUP])
        bias_off = o7[0]
        abias = mixbuf("abias", [AH, T])
        gates = mixbuf("gates", [LT, 2, P])
        normw = mixbuf("normw", [GROUP])
        convw = mixbuf("convw", [XT + LT, CW + 1])
        lvec = mixbuf("lvec", [3, LT])
        svec = mixbuf("svec", [3, SH])
        sp8 = mixbuf("sp8", [6, LT])
        dts = mixbuf("dts", [6, TB * SH])
        dt_, dtA, acs, tot, eacs, cdec = (mixbuf(n, [TB * SH]) for n in ("dt_", "dtA", "acs", "tot", "eacs", "cdec"))
        dtdec, gsum, gstd, gtmp = mixbuf("dtdec", [TB * SH]), *(mixbuf(n, [2]) for n in ("gsum", "gstd", "gtmp"))
        nmax2, den2 = mixbuf("nmax2", [TB * AH]), mixbuf("den2", [TB * AH])
        lmat_off = o7[0]
        lmat = mixbuf("lmat", [SH, P])
        r4, i4 = at("r4", [LT, T], bias_off), at("i4", [LT, T], bias_off + 8 * KB)
        a4 = at("a4", [LT, T], SCR)
        asq = [at(f"asq{n}", [T], SCR + 8 * KB + 2 * KB * n) for n in range(2)]
        H2 = HT + 24 * KB
        xdt, xdec, ysk0, ysk1, prev, junk = (at(n, [GROUP], SCR + 2 * KB * m)
                                             for m, n in enumerate(("xdt", "xdec", "ysk0", "ysk1", "prev", "junk")))
        ysk = [ysk0, ysk1]
        btok_off = o7[0]
        btok = mixbuf("btok", [SG * SN])
        assert btok_off == lmat_off + 4 * KB
        pr2 = [at(f"pr2_{n}", [N_P], o) for n, o in enumerate((SCR, SCR + 4 * N_P, H2))]
        pt2 = [at(f"pt2_{n}", [N_P], o) for n, o in enumerate((gqk_off, lmat_off))]
        mix_hi = at("mix_hi", [12, T], HT, F32R)
        mix_lo = at("mix_lo", [12, T], conv_off, F32R)
        xT3 = convT[:, XT:XT + LT, :]
        gT = gqkT[:, 0:LT, :]
        q2T, k2T = gqkT[:, 4:8, :], gqkT[:, 8:12, :]

        M = {n: sem("mix_" + n) for n in (
            "par_landed", "bias_landed", "tap_ready", "conv_done", "silu_ready", "copied", "gelu_ready", "z_ready", "v_ready",
            "lru_ps", "lru_gates", "lru_small", "lru_e", "lru_sp", "lru_a", "lru_sq", "lru_u2", "lru_root", "lru_scan", "lru_done", "yo_out",
            "dt_copied", "dt_turned", "dt_e", "dt_sum", "dt_ready", "acs_ps", "acs_out", "dec_in", "dec_out", "x_ps", "b_ps", "b_out",
            "g_ps", "bc_ps", "x_out", "seg_ready", "L_exp", "S_ready", "yd_ps", "yo_ps", "st_ps", "prev_ready", "y_ready",
            "y_sq", "y_std", "y_done", "yT_ready", "l_hi")}
        att2 = Attention("att2", AH, q2T, k2T, v2, lambda tb, h: abias[:, h, (TB - 1 - tb) * P:T], pr2, pt2, nmax2, den2, mix_hi, mix_lo)
        n_mix = FIRST["mix"]
        DT0, Z0, VV0, TILE0 = 12, 13, 17, 21
        PER_CHUNK = (PHASES["mix"] - TILE0) // TB

        def log1p_series(dve, e, s, s2, p):
            dve.tensor_scalar(s, e, 2.0, None, ALU.add)
            dve.drain()
            dve.reciprocal(s, s)
            dve.drain()
            dve.tensor_tensor(s, s, e, ALU.mult)
            dve.drain()
            dve.tensor_tensor(s2, s, s, ALU.mult)
            dve.drain()
            dve.tensor_scalar(p, s2, 1.0 / 17, None, ALU.mult)
            for k in (15, 13, 11, 9, 7, 5, 3):
                dve.drain()
                dve.scalar_tensor_tensor(p, p, 1.0 / k, s2, ALU.add, ALU.mult)
            dve.drain()
            dve.scalar_tensor_tensor(p, p, 1.0, s, ALU.add, ALU.mult)
            dve.drain()
            dve.tensor_scalar(p, p, 2.0, None, ALU.mult)
            dve.drain()

        def mix_tensor(pe, nm):
            def tile(k, it, bank, in_ready):
                slot, number, _ = unit(k, it)
                pe.wait_ge(lo_ready, number + 1)
                for kt in range(KT):
                    if in_ready is not None:
                        pe.wait_ge(*in_ready(kt + 1))
                    cols = slice(kt * P, (kt + 1) * P)
                    last = mm3(pe, ps[:, bank, :], w_hi[slot][:, cols], w_lo[slot][:, cols], h_hi[:, kt, :], h_lo[:, kt, :],
                               kt == 0, kt == KT - 1)
                last.then_inc(unit_used, 1)

            first = [unit(n_mix + b) for b in range(2)]
            pe.wait_ge(lo_ready, first[1][1] + 1)
            for kt in range(KT):
                pe.wait_ge(nm.h_ready, nm.before + kt + 1)
                for b in range(2):
                    cols = slice(kt * P, (kt + 1) * P)
                    slot = first[b][0]
                    last = mm3(pe, ps[:, b, :], w_hi[slot][:, cols], w_lo[slot][:, cols], h_hi[:, kt, :], h_lo[:, kt, :],
                               kt == 0, kt == KT - 1)
                    if kt == KT - 1:
                        last.then_inc(unit_used, 1)
            for b in range(2, 4):
                tile(n_mix + b, None, b, None)
            with pe.Fori(1, 3) as it:
                for b in range(4):
                    pe.wait_ge(M["conv_done"], it * 4 + (b + 1))
                    tile(n_mix + b, it, b, None)
            pe.wait_ge(M["par_landed"], 16 * 5)
            pe.wait_ge(M["conv_done"], 12 + 4)
            for j in range(LT):
                for which in range(2):
                    if j >= 2:
                        pe.wait_ge(M["lru_gates"], 2 * (j - 2) + which + 1)
                    pe.matmul(ps[:, 4 + 2 * (j % 2) + which, :], gates[:, j, which, :], xT3[:, j, :], start=True, stop=True)\
                        .then_inc(M["lru_ps"], 1)
            pe.wait_ge(M["lru_gates"], 2 * LT)
            project_narrow(pe, n_mix + DT0, SH, M["dt_copied"], junk).then_inc(M["dt_turned"], 1)
            project(pe, n_mix + Z0, 0, 4)
            pe.wait_ge(M["dt_ready"], 1)
            pe.matmul(ps[:, 4, 0:TB * SH], const("tri"), dtA[:], start=True, stop=True)
            pe.matmul(ps[:, 5, 0:TB * SH], ones, dtA[:], start=True, stop=True).then_inc(M["acs_ps"], 1)
            pe.wait_ge(M["acs_out"], 1)
            project(pe, n_mix + VV0, 1, 4)
            pe.wait_ge(M["silu_ready"], 1)
            pe.wait_ge(M["z_ready"], 1)
            pe.wait_ge(M["v_ready"], 1)

            def plain(j):
                if j >= 2:
                    pe.wait_ge(M["copied"], j - 1)
                tile(n_mix + TILE0 + j, None, 5 + j % 2, None)

            for c in range(TB):
                toks = slice(c * P, (c + 1) * P)
                plain(PER_CHUNK * c)
                if c:
                    pe.wait_ge(M["prev_ready"], c)
                for m in range(4):
                    last = pe.transpose(ps[:, 0, m * P:(m + 1) * P], convT[:, m, toks], ident)
                last.then_inc(M["x_ps"], 1)
                if c:
                    pe.wait_ge(M["b_out"], c)
                if c >= 2:
                    pe.wait_ge(M["yo_out"], c - 1)
                for g in range(SG):
                    last = pe.transpose(ps[:, 1, g * SN:(g + 1) * SN], convT[:, 4 + g, toks], ident)
                last.then_inc(M["b_ps"], 1)
                if c:
                    pe.wait_ge(M["seg_ready"], c)
                for h in range(SH):
                    col = dtA[:, c * SH + h:c * SH + h + 1]
                    last = pe.matmul(ps[:, 2 + h // 4, (h % 4) * P:(h % 4 + 1) * P], col.broadcast_to([P, P]), const("tri"),
                                     start=True, stop=True)
                last.then_inc(M["bc_ps"], 1)
                if c:
                    pe.wait_ge(M["S_ready"], c)
                for g in range(SG):
                    last = pe.matmul(ps[:, 4, g * P:(g + 1) * P], convT[:, 4 + g, toks], convT[:, 6 + g, toks], start=True, stop=True)
                last.then_inc(M["g_ps"], 1)
                plain(PER_CHUNK * c + 1)
                pe.wait_ge(M["x_out"], c + 1)
                pe.wait_ge(M["b_out"], c + 1)
                if c < TB - 1:
                    for g in range(SG):
                        last = pe.matmul(ps[:, 0, g * 256:(g + 1) * 256], btok[:, g * SN:(g + 1) * SN], xdec[:, g * 256:(g + 1) * 256],
                                         start=True, stop=True)
                    last.then_inc(M["st_ps"], 1)
                if c:
                    for g in range(SG):
                        last = pe.matmul(ps[:, 1, g * 256:(g + 1) * 256], convT[:, 6 + g, toks], prev[:, g * 256:(g + 1) * 256],
                                         start=True, stop=True)
                    last.then_inc(M["yo_ps"], 1)
                plain(PER_CHUNK * c + 2)
                pe.wait_ge(M["S_ready"], c + 1)
                if c:
                    pe.wait_ge(M["y_ready"], c)
                for h in range(SH):
                    last = pe.matmul(ps[:, 7, h * HD:(h + 1) * HD], lmat[:, h, :], xdt[:, h * HD:(h + 1) * HD], start=True, stop=True)
                last.then_inc(M["yd_ps"], 1)
            pe.wait_ge(M["y_ready"], TB)
            pe.wait_ge(M["copied"], PER_CHUNK * TB)
            pe.wait_ge(M["lru_done"], 1)
            attn_tensor(pe, att2)
            pe.wait_ge(att2.o_done, AH)
            for m in range(4):
                pe.wait_ge(M["y_done"], TB)
                for c in range(TB):
                    last = pe.transpose(ps[:, 4 + m, c * P:(c + 1) * P], z2[:, c, m * P:(m + 1) * P], ident)
                last.then_inc(M["yT_ready"], 1)

        def mix_scalar(act):
            def tap(index, k, it=None):
                w = convw[:, index, :].rearrange("p a k -> p (a k)")
                act.wait_ge(unit_used, done(unit(k, it)[1]))
                act.activation(convT[:, index, :].rearrange("p a t -> p (a t)"), ps[:, (k - n_mix) % 4, :], ACT.Identity,
                               bias=w[:, CW:CW + 1], scale=w[:, CW - 1:CW]).then_inc(M["tap_ready"], 1)

            def split(u):
                split_hi(act, n_mix + u + LOOK)

            act.wait_ge(M["par_landed"], 16 * 5)
            for b in range(4):
                split(b)
                tap(bass.ds(XT + b, 1), n_mix + b)
            with act.Fori(0, 2) as it:
                for b in range(4):
                    split_hi(act, n_mix + 4 + b + LOOK, it)
                    tap(bass.ds(it * 4 + b, 1), n_mix + 4 + b, it)
            act.wait_ge(M["conv_done"], 12 + 4)
            act.activation(convT[:, 0:XT, :], convT[:, 0:XT, :], ACT.Silu).then_inc(M["silu_ready"], 1)
            for j in range(LT):
                for which in range(2):
                    act.wait_ge(M["lru_ps"], 2 * j + which + 1)
                    act.activation((r4, i4)[which][:, j, :], ps[:, 4 + 2 * (j % 2) + which, :], ACT.Sigmoid,
                                   bias=lvec[:, which, j:j + 1]).then_inc(M["lru_gates"], 1)
            split(DT0)
            act.wait_ge(M["lru_small"], 1)
            act.activation(sp8[:, 0, :], sp8[:, 0, :], ACT.Exp, scale=-1.0).then_inc(M["lru_e"], 1)
            act.activation(svec[:, 1, :], svec[:, 1, :], ACT.Exp).then_inc(M["lru_e"], 1)
            split(Z0)
            act.activation(junk[0:SH, :], ps[0:SH, 4, :], ACT.Copy).then_inc(M["dt_copied"], 1)
            act.wait_ge(M["lru_sp"], 1)
            for j in range(LT):
                act.activation(a4[:, j, :], r4[:, j, :], ACT.Exp, scale=sp8[:, 4, j:j + 1])
            act.wait_ge(M["dt_e"], 1)
            act.activation(dts[:, 2, :], dts[:, 1, :], ACT.Exp, scale=-1.0).then_inc(M["dt_sum"], 1)
            split(Z0 + 1)
            for j in range(LT):
                last = act.activation(r4[:, j, :], r4[:, j, :], ACT.Tanh, scale=sp8[:, 5, j:j + 1])
            last.then_inc(M["lru_a"], 1)
            act.drain()
            for j in range(LT):
                if j >= 2:
                    act.wait_ge(M["lru_u2"], j - 1)
                act.activation(asq[j % 2][:], a4[:, j, :], ACT.Square).then_inc(M["lru_sq"], 1)
            split(Z0 + 2)
            act.wait_ge(M["lru_u2"], LT)
            act.activation(r4[:], r4[:], ACT.Sqrt).then_inc(M["lru_root"], 1)
            split(Z0 + 3)
            act.wait_ge(unit_used, done(n_mix + Z0 + 3))
            for tb in range(TB):
                last = act.activation(z2[:, tb, :], ps[:, tb, :], ACT.Silu)
            last.then_inc(M["z_ready"], 1)
            split(VV0)
            act.wait_ge(M["acs_ps"], 1)
            act.activation(acs[:], ps[:, 4, 0:TB * SH], ACT.Copy)
            act.activation(tot[:], ps[:, 5, 0:TB * SH], ACT.Copy).then_inc(M["acs_out"], 1)
            act.drain()
            act.activation(eacs[:], acs[:], ACT.Exp)
            act.activation(cdec[:], tot[:], ACT.Exp)
            act.wait_ge(M["dec_in"], 1)
            act.activation(dtdec[:], dtdec[:], ACT.Exp).then_inc(M["dec_out"], 1)
            for u in range(1, 4):
                split(VV0 + u)
            act.wait_ge(M["lru_scan"], 1)
            act.dma_start(abias[:], d["abias"]).then_inc(M["bias_landed"], 16)
            act.wait_ge(unit_used, done(n_mix + VV0 + 3))
            for tb in range(TB):
                last = act.activation(v2[:, tb, :], ps[:, 4 + tb, :], ACT.Copy)
            last.then_inc(M["v_ready"], 1)

            def plain(j):
                act.wait_ge(unit_used, done(n_mix + TILE0 + j))
                act.activation(gqkT[:, j, :], ps[:, 5 + j % 2, :], ACT.Copy).then_inc(M["copied"], 1)

            def group_roots(c):
                act.wait_ge(M["y_ready"], c + 1)
                if c:
                    act.wait_ge(M["y_done"], c)
                for g in range(SG):
                    act.activation(junk[:, g * 256:(g + 1) * 256], z2[:, c, g * 256:(g + 1) * 256], ACT.Square, accum_out=gsum[:, g:g + 1])
                act.drain()
                act.activation(gstd[:], gsum[:], ACT.Sqrt, bias=const("eps_ssd"), scale=1.0 / 256).then_inc(M["y_std"], 1)

            for c in range(TB):
                j = PER_CHUNK * c
                split(TILE0 + j)
                plain(j)
                act.wait_ge(M["b_ps"], c + 1)
                if c:
                    act.wait_ge(M["st_ps"], c)
                act.activation(btok[:], ps[:, 1, 0:SG * SN], ACT.Copy).then_inc(M["b_out"], 1)
                split(TILE0 + j + 1)
                act.wait_ge(M["seg_ready"], c + 1)
                act.activation(lmat[:], lmat[:], ACT.Exp).then_inc(M["L_exp"], 1)
                plain(j + 1)
                split(TILE0 + j + 2)
                if c:
                    group_roots(c - 1)
                plain(j + 2)
                if c == 1:
                    act.activation(gT, gT, ACT.Gelu_apprx_tanh).then_inc(M["gelu_ready"], 1)
            group_roots(TB - 1)
            attn_scalar(act, att2)
            for m in range(4):
                act.wait_ge(M["yT_ready"], m + 1)
                act.activation(mix_hi[:, 4 + m, :], ps[:, 4 + m, :], ACT.Copy).then_inc(M["l_hi"], 1)
            for j in range(LT):
                act.activation(mix_hi[:, 8 + j, :], xT3[:, j, :], ACT.Copy).then_inc(M["l_hi"], 1)

        def mix_vector(dve):
            dve.sem_inc(M["conv_done"], 4)

            def taps(index, bank, n):
                w = convw[:, index, :].rearrange("p a k -> p (a k)")
                y = convT[:, index, :].rearrange("p a t -> p (a t)")
                dve.wait_ge(M["tap_ready"], n)
                for back in range(1, CW):
                    last = dve.scalar_tensor_tensor(y[:, back:T], ps[:, bank, 0:T - back], w[:, CW - 1 - back:CW - back], y[:, back:T],
                                                    ALU.mult, ALU.add)
                    if back < CW - 1:
                        dve.drain()
                last.then_inc(M["conv_done"], 1)

            for b in range(4):
                taps(bass.ds(XT + b, 1), b, b + 1)
            with dve.Fori(0, 2) as it:
                for b in range(4):
                    taps(bass.ds(it * 4 + b, 1), b, it * 4 + (b + 5))
            e, m_, s, s2, p, n8 = (sp8[:, k, :] for k in (0, 1, 2, 3, 4, 5))
            lam = lvec[:, 2, :]
            dve.scalar_tensor_tensor(e, lam, -1.0, lam, ALU.mult, ALU.max)
            dve.tensor_scalar(m_, lam, -1.0, 0.0, ALU.mult, ALU.max).then_inc(M["lru_small"], 1)
            dve.wait_ge(M["lru_e"], 1)
            log1p_series(dve, e, s, s2, p)
            dve.tensor_tensor(p, p, m_, ALU.add)
            dve.drain()
            dve.tensor_scalar(n8, p, 8.0, None, ALU.mult)
            dve.drain()
            dve.tensor_scalar(p, n8, -1.0, None, ALU.mult).then_inc(M["lru_sp"], 1)
            raw_dt, ab, e, s, s2, p = (dts[:, k, :] for k in range(6))
            dve.wait_ge(M["dt_turned"], 1)
            dve.tensor_tensor(raw_dt.rearrange("p (c h) -> p c h", h=SH), ps[:, 4:8, 0:SH], bc(svec[:, 0, :], 1, TB), ALU.add)
            dve.drain()
            dve.scalar_tensor_tensor(ab, raw_dt, -1.0, raw_dt, ALU.mult, ALU.max).then_inc(M["dt_e"], 1)
            dve.tensor_tensor(i4[:], i4[:], xT3, ALU.mult)
            dve.wait_ge(M["dt_sum"], 1)
            log1p_series(dve, e, s, s2, p)
            dve.scalar_tensor_tensor(dt_[:], raw_dt, 0.0, p, ALU.max, ALU.add)
            dve.drain()
            dve.wait_ge(M["lru_e"], 2)
            dve.tensor_tensor(dtA[:].rearrange("p (c h) -> p c h", h=SH), dt_[:].rearrange("p (c h) -> p c h", h=SH),
                              bc(svec[:, 1, :], 1, TB), ALU.mult)
            dve.drain()
            dve.tensor_scalar(dtA[:], dtA[:], -1.0, None, ALU.mult).then_inc(M["dt_ready"], 1)
            dve.wait_ge(M["lru_a"], 1)
            for j in range(LT):
                dve.wait_ge(M["lru_sq"], j + 1)
                dve.scalar_tensor_tensor(r4[:, j, :], asq[j % 2][:], 1.0, r4[:, j, :], ALU.add, ALU.mult).then_inc(M["lru_u2"], 1)
            dve.wait_ge(M["lru_root"], 1)
            dve.tensor_tensor(r4[:], r4[:], i4[:], ALU.mult)
            dve.drain()
            for j in range(LT):
                last = dve.tensor_tensor_scan(xT3[:, j, :], a4[:, j, :], r4[:, j, :], 0.0, ALU.mult, ALU.add)
            last.then_inc(M["lru_scan"], 1)
            dve.wait_ge(M["acs_out"], 1)
            dve.tensor_tensor(dtdec[:], tot[:], acs[:], ALU.subtract).then_inc(M["dec_in"], 1)
            dve.wait_ge(M["dec_out"], 1)
            dve.tensor_tensor(dtdec[:], dtdec[:], dt_[:], ALU.mult)
            dve.memset(prev[:], 0.0)
            dve.drain()

            def heads(ap):
                return ap.rearrange("p (h d) -> p h d", d=HD)

            def gated(c):
                y = ysk[c % 2]
                dve.wait_ge(M["yd_ps"], c + 1)
                dve.tensor_tensor(y[:], y[:], ps[:, 7, :], ALU.add)
                dve.drain()
                dve.tensor_tensor(z2[:, c, :], z2[:, c, :], y[:], ALU.mult).then_inc(M["y_ready"], 1)

            def group_norm(c):
                dve.wait_ge(M["y_std"], c + 1)
                dve.tensor_scalar(gsum[:], gsum[:], 1.0 / 256, SSD_EPS, ALU.mult, ALU.add)
                dve.drain()
                root_reciprocal(dve, gstd[:], gsum[:], gtmp[:])
                for g in range(SG):
                    cols = slice(g * 256, (g + 1) * 256)
                    z = z2[:, c, cols]
                    last = dve.scalar_tensor_tensor(z, z, gstd[:, g:g + 1], normw[:, cols], ALU.mult, ALU.mult)
                last.then_inc(M["y_done"], 1)

            for c in range(TB):
                hs = slice(c * SH, (c + 1) * SH)
                if c:
                    gated(c - 1)
                dve.wait_ge(M["x_ps"], c + 1)
                x = heads(ps[:, 0, :])
                dve.tensor_tensor(heads(xdt[:]), x, bc(dt_[:, hs], 2, HD), ALU.mult)
                dve.tensor_tensor(heads(xdec[:]), x, bc(dtdec[:, hs], 2, HD), ALU.mult)
                dve.tensor_tensor(heads(ysk[c % 2][:]), x, bc(svec[:, 2, :], 2, HD), ALU.mult).then_inc(M["x_out"], 1)
                dve.wait_ge(M["bc_ps"], c + 1)
                for h in range(SH):
                    last = dve.scalar_tensor_tensor(lmat[:, h, :], ps[:, 2 + h // 4, (h % 4) * P:(h % 4 + 1) * P],
                                                    acs[:, c * SH + h:c * SH + h + 1], const("causal_t"), ALU.subtract, ALU.add)
                last.then_inc(M["seg_ready"], 1)
                dve.wait_ge(M["g_ps"], c + 1)
                dve.wait_ge(M["L_exp"], c + 1)
                lm = lmat[:].rearrange("p (g h) i -> p g h i", g=SG)
                dve.tensor_tensor(lm, lm, bc(ps[:, 4, 0:SG * P].rearrange("p (g i) -> p g i", g=SG), 2, SH // SG), ALU.mult)\
                    .then_inc(M["S_ready"], 1)
                if c:
                    dve.wait_ge(M["yo_ps"], c)
                    dve.tensor_tensor(heads(xdec[:]), heads(ps[:, 1, :]), bc(eacs[:, hs], 2, HD), ALU.mult).then_inc(M["yo_out"], 1)
                    dve.drain()
                    dve.tensor_tensor(ysk[c % 2][:], ysk[c % 2][:], xdec[:], ALU.add)
                    dve.drain()
                if c < TB - 1:
                    dve.wait_ge(M["st_ps"], c + 1)
                    dve.tensor_tensor(heads(prev[:]), heads(prev[:]), bc(cdec[:, hs], 2, HD), ALU.mult)
                    dve.drain()
                    dve.tensor_tensor(prev[:], prev[:], ps[:, 0, :], ALU.add).then_inc(M["prev_ready"], 1)
                if c:
                    group_norm(c - 1)
                if c == 2:
                    dve.wait_ge(M["gelu_ready"], 1)
                    dve.tensor_tensor(xT3, xT3, gT, ALU.mult).then_inc(M["lru_done"], 1)
            gated(TB - 1)
            group_norm(TB - 1)
            dve.wait_ge(M["bias_landed"], 16)
            attn_vector(dve, att2)
            for m in range(8):
                dve.wait_ge(M["l_hi"], m + 1)
                src = ps[:, 4 + m, :] if m < 4 else xT3[:, m - 4, :]
                dve.tensor_tensor(mix_lo[:, 4 + m, :], src, mix_hi[:, 4 + m, :].bitcast(F32), ALU.subtract).then_inc(mix_in, 1)

        def final_vector(dve, nm):
            token_factors(dve, nm)
            g0 = VEC_AT[nm.name]
            for o in range(KT):
                dve.scalar_tensor_tensor(xT[:, o, :], xT[:, o, :], vec[:, g0 + o:g0 + o + 1], ps[:, 7, :], ALU.mult, ALU.mult)\
                    .then_inc(out_ready, 1)

        mix_in = sem("mix_parts")
        norms, rows = count(), count()
        glu = Gated(0, "glu", KT, after(S["ylo_ready"], 2))

        def norm(name, acc_ready):
            return Norm(next(norms), name, acc_ready)

        def rows_of(name, k_tiles, hi, lo, in_ready):
            return Rows(next(rows), name, k_tiles, hi, lo, in_ready)

        def normed(nm):
            return after(nm.h_ready, nm.before)

        def mixed(n):
            return att2.tiles_ready(n) if isinstance(n, int) and n <= 4 else (mix_in, n - 4)

        def squared(ph):
            return after(ph.acc_ready, ph.before)

        norm_f0 = norm("norm_ffn0", after(glu.out_ready))
        gu0 = Gated(KT + 0 * FT, "gu0", FT, normed(norm_f0))
        down0 = rows_of("down0", FT, hid_hi, hid_lo, after(gu0.out_ready, gu0.before))
        norm_m1 = norm("norm_mix1", squared(down0))
        wo = rows_of("wo", KT, h_hi, h_lo, att1.tiles_ready)
        norm_f1 = norm("norm_ffn1", squared(wo))
        gu1 = Gated(KT + 1 * FT, "gu1", FT, normed(norm_f1))
        down1 = rows_of("down1", FT, hid_hi, hid_lo, after(gu1.out_ready, gu1.before))
        norm_m2 = norm("norm_mix2", squared(down1))
        w_out = rows_of("out", 12, mix_hi, mix_lo, mixed)
        norm_f2 = norm("norm_ffn2", squared(w_out))
        gu2 = Gated(KT + 2 * FT, "gu2", FT, normed(norm_f2))
        down2 = rows_of("down2", FT, hid_hi, hid_lo, after(gu2.out_ready, gu2.before))
        norm_end = norm("norm_final", squared(down2))
        out_ready, out_landed = sem("out_ready"), sem("out_landed")

        def after_pairs(ph):
            n = ph.before + ph.pairs
            return [(o, None) for o in range(4, 8)] + [(0, (ph.pair_done, n + 1)), (1, None), (2, (ph.pair_done, n + 2)), (3, None)]

        block = ctx.enter_context(nc.Block())

        @block.sync
        def _(sp):
            s5_sync(sp)
            load_units(sp, "glu", d["w_glu"])
            load_units(sp, "gu0", d["w_gu0"])
            load_units(sp, "down0", d["w_down0"])
            load_units(sp, "dsa", d["w_dsa"])
            load_units(sp, "wo", d["w_o"])
            load_units(sp, "gu1", d["w_gu1"])
            load_units(sp, "down1", d["w_down1"])
            load_units(sp, "mix", d["w_mix"])
            load_units(sp, "out", d["w_out"])
            load_units(sp, "gu2", d["w_gu2"])
            load_units(sp, "down2", d["w_down2"])
            for o in range(KT):
                sp.wait_ge(out_ready, o + 1)
                sp.dma_start(out[:, o, :], xT[:, o, :]).then_inc(out_landed, 16)
            sp.wait_ge(out_landed, 16 * KT)

        @block.gpsimd
        def _(pool):
            s5_gpsimd(pool)
            split_lo_all(pool)

        @block.scalar
        def _(act):
            s5_scalar(act)
            glu_scalar(act, glu)
            norm_scalar(act, norm_f0)
            ffn_scalar(act, gu0)
            rows_scalar(act, down0)
            act.wait_ge(down0.tile_done, down0.before + KT)
            act.dma_start(rope[:], d["rope"]).then_inc(A["par_landed"], 16)
            act.dma_start(hgain[:], d["hgain"]).then_inc(A["par_landed"], 16)
            norm_scalar(act, norm_m1)
            dsa_scalar(act)
            rows_scalar(act, wo)
            norm_scalar(act, norm_f1)
            ffn_scalar(act, gu1)
            rows_scalar(act, down1)
            act.wait_ge(down1.tile_done, down1.before + KT)
            for buf, name in ((convw, "convw"), (gates, "gates"), (lvec, "lvec"), (svec, "svec"), (normw, "normw")):
                act.dma_start(buf[:], d[name]).then_inc(M["par_landed"], 16)
            norm_scalar(act, norm_m2)
            mix_scalar(act)
            rows_scalar(act, w_out)
            norm_scalar(act, norm_f2)
            ffn_scalar(act, gu2)
            rows_scalar(act, down2)
            norm_scalar(act, norm_end, 0)

        @block.vector
        def _(dve):
            s5_vector(dve)
            glu_vector(dve, glu)
            norm_vector(dve, norm_f0)
            ffn_vector(dve, gu0)
            rows_vector(dve, down0)
            norm_vector(dve, norm_m1)
            dsa_vector(dve)
            rows_vector(dve, wo)
            norm_vector(dve, norm_f1)
            ffn_vector(dve, gu1)
            rows_vector(dve, down1)
            norm_vector(dve, norm_m2)
            mix_vector(dve)
            rows_vector(dve, w_out)
            norm_vector(dve, norm_f2)
            ffn_vector(dve, gu2)
            rows_vector(dve, down2)
            final_vector(dve, norm_end)

        @block.tensor
        def _(pe):
            pe.sem_inc(unit_used, 1)
            s5_tensor(pe)
            gated_tensor(pe, glu)
            norm_tensor(pe, norm_f0)
            gated_tensor(pe, gu0)
            rows_tensor(pe, down0, after_pairs(gu0))
            norm_tensor(pe, norm_m1)
            dsa_tensor(pe, norm_m1)
            rows_tensor(pe, wo, [(o, None) for o in range(6)] + [(o, (att1.o_done, NH - 7 + o)) for o in (6, 7)])
            norm_tensor(pe, norm_f1)
            gated_tensor(pe, gu1)
            rows_tensor(pe, down1, after_pairs(gu1))
            norm_tensor(pe, norm_m2)
            mix_tensor(pe, norm_m2)
            rows_tensor(pe, w_out, [(o, None) for o in range(4)] + [(o, (mix_in, o - 3)) for o in range(4, KT)])
            norm_tensor(pe, norm_f2)
            gated_tensor(pe, gu2)
            rows_tensor(pe, down2, after_pairs(gu2))
            norm_tensor(pe, norm_end)


def kernel(**inputs):
    import concourse.bacc as bacc
    from concourse.bass_utils import run_bass_kernel_spmd

    i = {k: np.asarray(v) for k, v in inputs.items()}
    x = i["x"][0]

    def tiles(w):
        k, n = w.shape
        return w.reshape(k // P, P, n // P, P).transpose(2, 1, 0, 3).reshape(n // P, P, k)

    def pairs(gate, value):
        return np.stack([tiles(gate), tiles(value)], 1).reshape(-1, P, gate.shape[0])

    def token_major(w):
        return w.reshape(KT // 2, 2, P, GROUP).transpose(0, 2, 1, 3).reshape(KT // 2, P, UNIT)

    def narrow(w):
        u = np.zeros((P, KT, P), w.dtype)
        u[:, :, :w.shape[1]] = w.reshape(KT, P, -1).transpose(1, 0, 2)
        return u.reshape(1, P, UNIT)

    def two(name):
        return i[name + "_2"][0]

    def block_diagonal(w):
        o = np.zeros((P, LT, P), w.dtype)
        for b in range(2 * LT):
            at = slice(HD * (b % 2), HD * (b % 2 + 1))
            o[at, b // 2, at] = w[b]
        return o

    w2 = two("w_in")
    w_in = i["dsa_w_in"][0]
    rest = narrow(w_in[:, 3 * D + IH * HD:])

    def states(a):
        return np.moveaxis(a, 1, 0)

    s5 = {k: i["s5_" + k][0] for k in ("lambda_re", "lambda_im", "log_dt", "b_re", "b_im", "c_re", "c_im", "d", "w_glu")}
    twice = lambda a, b: np.concatenate([states(a), states(b)], 0)
    gain = np.tile(i["norm_mix"][0].reshape(G, GH).T, (CH, 1))
    par = np.stack([twice(s5["lambda_re"], s5["lambda_re"]), twice(s5["lambda_im"], s5["lambda_im"]),
                    np.broadcast_to(s5["log_dt"], (P, G)), gain], 1)
    ct = {k: s5[k].transpose(0, 2, 1) for k in ("c_re", "c_im")}
    vecs = {"norm_ffn0": i["norm_ffn"][0], "norm_mix1": i["norm_mix"][1], "norm_ffn1": i["norm_ffn"][1],
            "norm_mix2": i["norm_mix_2"][0], "norm_ffn2": i["norm_ffn_2"][0], "norm_final": i["norm_final_2"]}
    wg = s5["w_glu"]
    arrays = {
        "cst": np.concatenate(list(constant_columns().values()), 1),
        "vec": np.concatenate([vecs[k].reshape(-1, P).T for k in VEC], 1),
        "xT": x.T.reshape(KT, P, T).transpose(1, 0, 2),
        "xs5": x.reshape(NC, CH, G, GH)[:, ::-1].transpose(1, 3, 2, 0).reshape(P, G, NC),
        "s5_par": par,
        "s5_b": np.stack([twice(s5["b_re"], s5["b_im"]), twice(s5["b_im"], s5["b_re"])], 1).reshape(P, 2, G * GH),
        "s5_c": np.stack([twice(ct["c_re"], ct["c_im"]), twice(ct["c_im"], ct["c_re"])], 1).reshape(P, 2, G * GH),
        "s5_d": s5["d"].reshape(G, GH).T,
        "w_glu": pairs(wg[:, D:], wg[:, :D]),
        "w_gu0": pairs(i["ffn_w_gate_up"][0][:, :FF], i["ffn_w_gate_up"][0][:, FF:]),
        "w_down0": i["ffn_w_down"][0].reshape(FT, P, D),
        "rope": rope_tables(),
        "hgain": np.broadcast_to(np.stack([i["dsa_q_norm"][0], i["dsa_k_norm"][0]]), (P, 2, HD)),
        "w_dsa": np.concatenate([token_major(w_in[:, 3 * D:3 * D + IH * HD]), rest]
                                + [token_major(w_in[:, n * GROUP:(n + 1) * GROUP]) for n in range(6)]),
        "w_o": i["dsa_w_o"][0].reshape(KT, P, D),
        "w_gu1": pairs(i["ffn_w_gate_up"][1][:, :FF], i["ffn_w_gate_up"][1][:, FF:]),
        "w_down1": i["ffn_w_down"][1].reshape(FT, P, D),
        "abias": dilated_bias(),
        "gates": np.stack([block_diagonal(two("lru_wa")), block_diagonal(two("lru_wx"))], 2),
        "normw": np.broadcast_to(two("ssd_norm"), (P, GROUP)),
        "convw": np.concatenate([np.concatenate([two(n + "_conv_w").T, two(n + "_conv_b")[:, None]], 1) for n in ("ssd", "lru")])
                 .reshape(XT + LT, P, CW + 1).transpose(1, 0, 2),
        "lvec": np.stack([two(n).reshape(LT, P).T for n in ("lru_ba", "lru_bx", "lru_lambda")], 1),
        "svec": np.broadcast_to(np.stack([two(n) for n in ("ssd_dt_bias", "ssd_a_log", "ssd_d")]), (P, 3, SH)),
        "w_mix": np.concatenate([tiles(w2[:, 3592:4104]), tiles(w2[:, 2048:3072]), narrow(w2[:, 3072:3080]),
                                 token_major(w2[:, 1536:2048]), token_major(w2[:, 1024:1536]), tiles(w2[:, 3080:3592]),
                                 tiles(w2[:, 0:1024])]),
        "w_out": two("w_out").reshape(12, P, D),
        "w_gu2": pairs(two("w_gate"), two("w_up")),
        "w_down2": two("w_down").reshape(FT, P, D),
    }
    arrays = {"in_" + k: np.ascontiguousarray(v) for k, v in arrays.items()}
    nc = bacc.Bacc("TRN2", target_bir_lowering=False, num_devices=1)
    d = {k[3:]: nc.dram_tensor(k, v.shape, mybir.dt.from_np(v.dtype), kind="ExternalInput").ap() for k, v in arrays.items()}
    out = nc.dram_tensor("out_x", (P, KT, T), F32, kind="ExternalOutput").ap()
    build(nc, d, out)
    r = run_bass_kernel_spmd(nc, [arrays], core_ids=[0])
    got = np.asarray(r.results[0]["out_x"])
    return got.transpose(2, 1, 0).reshape(1, T, D)
```

```python
import math
from contextlib import ExitStack
from itertools import count

import numpy as np
import concourse.bass as bass
from concourse import mybir

F32 = mybir.dt.float32
F32R = mybir.dt.float32r
ALU = mybir.AluOpType
ACT = mybir.ActivationFunctionType
AX_X = mybir.AxisListType.X

P = 128
D = 1024
T = 512
KT = D // P
TB = T // P
FF = 2816
FT = FF // P
EPS = 1e-6
BIG = 1e30
TAKEN = -3e38

NH, HD, IH = 16, 64, 8
TOPK = 128
SSD_EPS = 1e-5
AH, SH, SG, SN = 8, 8, 2, 128
XT, LT, CW = 8, 4, 4
RATES = ((128, 1), (512, 4), (2048, 16))
GROUP = 512

G, GH, NS = 64, 16, 64
CH = P // GH
NC = T // CH
QG = P // GH
NQ = G // QG
C1 = 6.28125
C2 = 2 * math.pi - C1
ROUND = 12582912.0
SIN_SCALE = 6.283185

UNIT = 1024
R = 4
LOOK = 3


def bc(ap, axis, n):
    out = ap.unsqueeze(axis)
    shape = list(out.shape)
    shape[axis] = n
    return out.broadcast_to(shape)


def constant_columns():
    i = np.arange(P)
    cols = {
        "ident": np.eye(P),
        "ones": np.ones((P, P)),
        "tri": i[:, None] <= i[None, :],
        "causal": np.where(i[None, :] <= i[:, None], 0.0, -BIG),
        "causal_t": np.where(i[:, None] <= i[None, :], 0.0, -BIG),
        "same_token": (i[:, None] // GH) == (i[None, :] // GH),
        "tau": np.broadcast_to(np.arange(CH + 1), (P, CH + 1)),
        "chunk": np.broadcast_to(np.arange(NC) - 1, (P, NC)),
        "carry": np.broadcast_to(np.arange(NC) > 0, (P, NC)),
        "sign": np.stack([np.where(i < NS, -1, 1), np.where(i < NS, 1, -1)], 1),
        "eps": np.full((P, 1), EPS),
        "eps_ssd": np.full((P, 1), SSD_EPS),
    }
    return {k: np.asarray(v, np.float32) for k, v in cols.items()}


def rope_tables():
    f = np.float32
    inv = f(10000.0) ** (-np.arange(0, HD, 2, dtype=f) / f(HD))
    a = np.arange(T, dtype=f)[:, None] * inv[None, :].astype(f)
    t = np.stack([np.cos(a), np.sin(a)]).astype(f)
    return np.concatenate([t, t], -1).reshape(2, TB, P, HD).transpose(2, 0, 1, 3)


def dilated_bias():
    dist = np.arange(P)[:, None] + (T - P) - np.arange(T)[None, :]
    count = sum(((dist % rate == 0) & (dist <= span)).astype(np.float64) for span, rate in RATES)
    count = np.where(dist >= 0, count, 0)
    slopes = 2.0 ** (-8.0 * np.arange(1, AH + 1) / AH)
    bias = -slopes[:, None, None] * dist + np.log(np.maximum(count, 1))
    return np.where(count > 0, 8 * bias, -BIG).astype(np.float32).transpose(1, 0, 2)


CONST_WIDTH = {k: v.shape[1] for k, v in constant_columns().items()}
CONST_AT = dict(zip(CONST_WIDTH, np.cumsum([0, *CONST_WIDTH.values()]).tolist()))
N_CONST = sum(CONST_WIDTH.values())

VEC = {"norm_ffn0": KT, "norm_mix1": KT, "norm_ffn1": KT, "norm_mix2": KT, "norm_ffn2": KT, "norm_final": KT}
VEC_AT = dict(zip(VEC, np.cumsum([0, *VEC.values()]).tolist()))
N_VEC = sum(VEC.values())

PHASES = {"glu": 2 * KT, "gu0": 2 * FT, "down0": FT, "dsa": 4 * 7 + 1, "wo": KT, "gu1": 2 * FT, "down1": FT,
          "mix": 33, "out": 12, "gu2": 2 * FT, "down2": FT}
FIRST = dict(zip(PHASES, np.cumsum([0, *PHASES.values()]).tolist()))
N_UNITS = sum(PHASES.values())


def build(nc, d, out):
    ctx = ExitStack()
    with ctx:
        def sem(name):
            return ctx.enter_context(nc.semaphore(name))

        base = (nc.sbuf_base + 63) // 64 * 64
        end = nc.sbuf_usable_end

        def at(name, shape, offset, dt=F32):
            return nc.alloc_sbuf_tensor_at(name, [P, *shape], dt, offset=offset)

        KB = 1024
        RAW, HI, LO = base, base + 16 * KB, base + 32 * KB
        X = base + 48 * KB
        CST = X + 16 * KB
        SCR = CST + 4 * KB
        HT = SCR + 12 * KB
        BIGR = HT + 32 * KB
        assert end - BIGR >= 95 * KB, (end - BIGR)

        raw = [at(f"raw{s}", [UNIT], RAW + 4 * KB * s) for s in range(R)]
        w_hi = [at(f"w_hi{s}", [UNIT], HI + 4 * KB * s, F32R) for s in range(R)]
        w_lo = [at(f"w_lo{s}", [UNIT], LO + 4 * KB * s, F32R) for s in range(R)]
        xT = at("xT", [KT, T], X)
        cst = at("cst", [N_CONST], CST)
        vec = at("vec", [N_VEC], CST + 32 * (-(-N_CONST // 8)))
        assert 4 * (N_CONST + N_VEC + 8 + 32) <= 4 * KB, (N_CONST, N_VEC)
        acc = at("acc", [T], SCR)
        sq = [at(f"sq{s}", [T], SCR + 2 * KB * (1 + s)) for s in range(2)]
        tok_mean, tok_rstd, tok_tmp, tok_wi = (at(f"tok{n}", [TB], CST + 4 * KB - 32 * (n + 1)) for n in range(4))
        spread = at("spread", [T], SCR + 6 * KB)
        t32 = [at(f"t32{s}", [T], SCR + 2 * KB * (4 + s)) for s in range(2)]
        h_hi = at("h_hi", [KT, T], HT, F32R)
        h_lo = at("h_lo", [KT, T], HT + 16 * KB, F32R)
        hid_hi = at("hid_hi", [FT, T], BIGR, F32R)
        hid_lo = at("hid_lo", [FT, T], BIGR + 2 * KB * FT, F32R)
        ps = ctx.enter_context(nc.psum_tensor("ps", [P, 8, T], F32))

        def const(name):
            return cst[:, CONST_AT[name]:CONST_AT[name] + CONST_WIDTH[name]]

        ident, ones, eps = const("ident"), const("ones"), const("eps")

        raw_landed = [sem(f"raw_landed{s}") for s in range(R)]
        hi_ready = sem("w_hi_ready")
        lo_ready = sem("w_lo_ready")
        unit_used = sem("unit_used")
        consts_landed = sem("consts_landed")

        def after(s, before=0):
            return lambda n: (s, n + before)

        def unit(k, it=None, per=R):
            if it is None:
                return k % R, k, k // R + 1
            return k % R, it * per + k, it * (per // R) + (k // R + 1)

        def load_units(sp, phase, view, after_head=None):
            n0, n = FIRST[phase], PHASES[phase]
            head = n % R if n0 else R

            def load(k, src, it=None):
                slot, number, _ = unit(k, it)
                if it is not None or k >= R:
                    sp.wait_ge(lo_ready, number - (R - 1))
                sp.dma_start(raw[slot][:], src).then_inc(raw_landed[slot], 16)

            for u in range(head):
                load(n0 + u, view[u])
            if after_head:
                after_head(sp)
            if n - head:
                with sp.Fori(0, (n - head) // R) as it:
                    for u in range(R):
                        load(n0 + head + u, view[bass.ds(it * R + (head + u), 1)].rearrange("a p n -> p (a n)"), it)
            assert (n - head) % R == 0

        def split_hi(act, k, it=None, per=R):
            if it is None and k >= N_UNITS:
                return
            slot, number, use = unit(k, it, per)
            act.wait_ge(raw_landed[slot], use * 16)
            if it is not None or k >= R:
                act.wait_ge(unit_used, number - (R - 2))
            act.activation(w_hi[slot][:], raw[slot][:], ACT.Copy).then_inc(hi_ready, 1)

        def split_lo_all(pool):
            def one(k, it=None):
                slot, number, _ = unit(k, it)
                pool.wait_ge(hi_ready, number + 1)
                pool.tensor_tensor(w_lo[slot][:], raw[slot][:], w_hi[slot][:].bitcast(F32), ALU.subtract)\
                    .then_inc(lo_ready, 1)
            with pool.Fori(0, N_UNITS // R) as it:
                for k in range(R):
                    one(k, it)
            for k in range(N_UNITS // R * R, N_UNITS):
                one(k)

        def mm3(pe, o, wh, wl, ah, al, start, stop):
            pe.matmul(o, wh, ah, start=start, stop=False)
            pe.matmul(o, wh, al, start=False, stop=False)
            return pe.matmul(o, wl, ah, start=False, stop=stop)

        def root_reciprocal(dve, out, m, t):
            dve.reciprocal(out, out)
            dve.drain()
            dve.tensor_tensor(t, out, out, ALU.mult)
            dve.drain()
            dve.tensor_tensor(t, t, m, ALU.mult)
            dve.drain()
            dve.tensor_scalar(t, t, -0.5, 1.5, ALU.mult, ALU.add)
            dve.drain()
            dve.tensor_tensor(out, out, t, ALU.mult)
            dve.drain()

        RING = RAW
        xs = at("s5_x", [G, NC], X)
        s5_par = at("s5_par", [4, G], RING)
        braw = at("s5_b", [2, G * GH], RING + 1 * KB)
        craw = at("s5_c", [2, G * GH], RING + 9 * KB)
        bbar = at("s5_bbar", [2, G * GH], RING + 17 * KB)
        NT9 = (CH + 1) * G * 4
        pw = [at(f"s5_pw{n}", [CH + 1, G], RING + 25 * KB + NT9 * n) for n in range(7)]
        turn, pw_re, pw_im, pw_ims, pw_re2, pw_imn, wave = pw
        small = at("s5_small", [16, G], RING + 25 * KB + NT9 * 7)
        assert 25 * KB + NT9 * 7 + 16 * G * 4 <= 48 * KB
        dskip = at("s5_dskip", [G], BIGR + 94 * KB)
        o5 = [BIGR]

        def s5buf(name, shape):
            off = o5[0]
            o5[0] += 4 * int(np.prod(shape))
            assert o5[0] <= BIGR + 94 * KB, name
            return at(name, shape, off)

        def s5two(name, shape):
            return [s5buf(f"{name}{n}", shape) for n in range(2)]

        winT = s5buf("s5_winT", [QG, CH, GH])
        wtmp = s5buf("s5_wtmp", [QG, CH, GH])
        win = s5two("s5_win", [QG, P + NS])
        wout = s5two("s5_wout", [QG, CH, GH])
        wotmp = s5buf("s5_wotmp", [QG, CH, GH])
        toep = s5two("s5_toep", [CH, QG, GH])
        ang2, ang_lo2, ang_sum2 = (s5two(f"s5_ang{n}_", [QG, NC]) for n in range(3))
        sin_t = s5two("s5_sin", [QG, NC])
        cos_t = s5two("s5_cos", [QG, NC])
        decay = s5two("s5_decay", [QG, NC])
        u_q = s5two("s5_u", [QG, NC])
        zin = s5buf("s5_zin", [QG, NC])
        zst = s5buf("s5_zst", [QG, NC])
        ztmp = s5buf("s5_ztmp", [QG, NC])
        zout = s5two("s5_zout", [QG, NC])
        conv = s5buf("s5_conv", [QG, GH])
        dI = s5buf("s5_dI", [G, GH])
        y_q = s5buf("s5_y", [CH, QG * GH])
        cxn = s5buf("s5_cxn", [G * GH])
        sumsq = at("s5_sumsq", [NC], SCR)
        rstd5, mean5, nt5 = (at(f"s5_rstd{n}", [NC], SCR + 256 * (n + 1)) for n in range(3))
        xsq = at("s5_xsq", [G, NC], BIGR)
        assert 4 * G * NC <= 4 * QG * (2 * CH * GH + 2 * (P + NS))
        lam_re, lam_im, log_dt, gain5 = (s5_par[:, n, :] for n in range(4))

        S = {n: sem("s5_" + n) for n in (
            "par_landed", "bc_landed", "x_landed", "dt", "turn", "wave", "ratio", "xsq", "sumsq", "sumps",
            "std", "prologue", "zeroed", "ang_ready", "ang_reduced", "half_ready", "decay_ready", "rot_done", "u_ready", "u_copied",
            "wout_ready", "winT_ready", "psT_ready", "psT_free", "convps", "conv_copied", "conv_ready", "w_ready", "w_free",
            "s_ready", "y_done", "y_evac", "yT_begun", "yT_ready", "gelu_ready", "yhi_ready", "ylo_ready", "xT_landed")}
        toep_landed = [sem(f"s5_toep_landed{n}") for n in range(2)]

        def s5_steps(engine, first, step, last):
            first(0, 0, 1)
            with engine.Fori(0, (NQ - 2) // 2) as it:
                step(it * 2 + 1, 1, it + 1)
                step(it * 2 + 2, 0, it + 2)
            last(NQ - 1, 1, NQ // 2)

        def s5_sync(sp):
            sp.dma_start(s5_par[:], d["s5_par"]).then_inc(S["par_landed"], 16)
            sp.dma_start(cst[:], d["cst"]).then_inc(consts_landed, 16)
            sp.dma_start(vec[:], d["vec"]).then_inc(consts_landed, 16)
            sp.dma_start(xs[:], d["xs5"]).then_inc(S["x_landed"], 16)
            sp.dma_start(braw[:], d["s5_b"]).then_inc(S["bc_landed"], 16)
            sp.dma_start(craw[:], d["s5_c"]).then_inc(S["bc_landed"], 16)
            sp.dma_start(dskip[0:GH, :], d["s5_d"]).then_inc(S["bc_landed"], 16)
            sp.wait_ge(S["zeroed"], 1)

            def shift_taps(e, p, use):
                sp.wait_ge(S["conv_ready"], e + 1)
                sp.wait_ge(S["y_done"], e * 2 + 2)
                for t in range(CH):
                    sp.dma_start(toep[p][GH * (CH - 1 - t):P, t, :, :], conv[0:GH * (t + 1), :, :]).then_inc(toep_landed[p], 16)

            s5_steps(sp, shift_taps, shift_taps, shift_taps)
            sp.wait_ge(S["winT_ready"], NQ)
            sp.wait_ge(S["wout_ready"], NQ)
            sp.wait_ge(S["ang_ready"], NQ)
            sp.wait_ge(S["decay_ready"], NQ)

        def residual(sp):
            sp.wait_ge(S["w_ready"], NQ + 2)
            sp.wait_ge(S["u_copied"], NQ)
            sp.dma_start(xT[:], d["xT"]).then_inc(S["xT_landed"], 16)

        t8_hi, t8_lo = small[:, 13, :], small[:, 14, :]
        b_raw = [braw[:, n, :].rearrange("p (g h) -> p g h", h=GH) for n in range(2)]
        bx, by = (bbar[:, n, :].rearrange("p (g h) -> p g h", h=GH) for n in range(2))
        ratio_re, ratio_im = small[:, 9, :], small[:, 10, :]

        def s5_gpsimd(pool):
            for p in range(2):
                pool.memset(toep[p][:], 0.0)
                pool.memset(decay[p][:], 0.0)
            pool.drain().then_inc(S["zeroed"], 1)
            pool.wait_ge(consts_landed, 32)
            for n in range(NQ // 2):
                pool.wait_ge(S["xsq"], n + 1)
                x = xs[:, n * QG:(n + 1) * QG, :]
                pool.tensor_tensor(x, x, bc(gain5[:, n * QG:(n + 1) * QG], 2, NC), ALU.mult)
            pool.wait_ge(S["bc_landed"], 48)
            pool.tensor_tensor(dI[0:GH, :, :], bc(dskip[0:GH, :], 2, GH), bc(ident[0:GH, 0:GH], 1, G), ALU.mult)
            scr = y_q[:].rearrange("p t n -> p (t n)").rearrange("p (g h) -> p g h", h=GH)
            pool.wait_ge(S["ratio"], 1)
            pool.tensor_tensor(by, b_raw[1], bc(ratio_re, 2, GH), ALU.mult)
            pool.tensor_tensor(scr, b_raw[0], bc(ratio_im, 2, GH), ALU.mult)
            pool.drain()
            pool.tensor_tensor(by, by, scr, ALU.subtract)
            pool.drain().then_inc(S["prologue"], 1)
            cx = craw[:, 0, :].rearrange("p (g h) -> p g h", h=GH)
            cy = craw[:, 1, :].rearrange("p (g h) -> p g h", h=GH)

            def angles(e, p):
                gs = bass.ds(e * QG, QG)
                pool.wait_ge(S["half_ready"], e + 1)
                pool.tensor_tensor(ang2[p][:], bc(t8_hi[:, gs], 2, NC), bc(const("chunk"), 1, QG), ALU.mult)
                pool.tensor_tensor(ang_lo2[p][:], bc(t8_lo[:, gs], 2, NC), bc(const("chunk"), 1, QG), ALU.mult)
                pool.drain()
                pool.tensor_tensor(ang_sum2[p][:], ang2[p][:], ang_lo2[p][:], ALU.add).then_inc(S["ang_ready"], 1)

            def inputs(e):
                gs = bass.ds(e * QG, QG)
                x = xs[:, gs, :]
                pool.tensor_tensor(x, x, bc(rstd5[:], 1, QG), ALU.mult).then_inc(S["u_ready"], 1)

            def states_out(e, p):
                gs = bass.ds(e * QG, QG)
                pool.wait_ge(S["y_done"], e * 2 + 2)
                pool.tensor_tensor(wout[p][:], bc(pw_re2[:, 1:CH + 1, gs].rearrange("p t g -> p g t"), 3, GH),
                                   bc(cx[:, gs, :], 2, CH), ALU.mult)
                pool.tensor_tensor(wotmp[:], bc(pw_imn[:, 1:CH + 1, gs].rearrange("p t g -> p g t"), 3, GH),
                                   bc(cy[:, gs, :], 2, CH), ALU.mult)
                pool.drain()
                pool.tensor_tensor(wout[p][:], wout[p][:], wotmp[:], ALU.add).then_inc(S["wout_ready"], 1)

            def begin(e, p, use):
                angles(e, p)
                pool.wait_ge(S["prologue"], 3)
                inputs(e)
                step(e, p, use)

            def step(e, p, use):
                inputs(e + 1)
                angles(e + 1, 1 - p)
                states_out(e, p)

            def finish(e, p, use):
                pool.drain()
                states_out(e, p)

            s5_steps(pool, begin, step, finish)

        def s5_scalar(act):
            act.sem_inc(S["psT_free"], 2)
            act.sem_inc(S["y_evac"], 2)
            act.sem_inc(S["half_ready"], 2)
            act.sem_inc(S["conv_copied"], 1)
            act.sem_inc(S["gelu_ready"], 1)
            act.wait_ge(S["par_landed"], 16)
            act.activation(small[:, 0, :], log_dt, ACT.Exp).then_inc(S["dt"], 1)
            act.wait_ge(S["turn"], 1)
            act.activation(wave[:], wave[:], ACT.Exp)
            act.activation(pw_im[:], turn[:], ACT.Sin, scale=SIN_SCALE)
            act.activation(pw_re[:], turn[:], ACT.Sin, scale=SIN_SCALE / 2)
            act.drain()
            act.activation(pw_re[:], pw_re[:], ACT.Square).then_inc(S["wave"], 1)
            act.wait_ge(S["x_landed"], 16)
            for g in range(0, G, QG):
                act.activation(xsq[:, g:g + QG, :], xs[:, g:g + QG, :], ACT.Square).then_inc(S["xsq"], 1)
            act.wait_ge(consts_landed, 32)
            act.wait_ge(S["bc_landed"], 48)
            act.activation(cxn[:], craw[:, 0, :], ACT.Copy, scale=const("sign")[:, 1:2])
            act.drain()

            def gains(g0, g1):
                for g in range(g0, g1):
                    act.activation(xs[:, g, :], xs[:, g, :], ACT.Copy, scale=gain5[:, g:g + 1])

            gains(G // 2, G)
            act.wait_ge(S["sumsq"], 1)
            act.activation(rstd5[:], sumsq[:], ACT.Sqrt, bias=eps, scale=1.0 / D).then_inc(S["std"], 1)
            act.drain().then_inc(S["prologue"], 1)

            def angles(e, p):
                act.wait_ge(S["rot_done"], e + 1)
                act.wait_ge(S["ang_reduced"], e + 1)
                act.activation(sin_t[p][:], ang2[p][:], ACT.Sin, scale=SIN_SCALE)
                act.activation(cos_t[p][:], ang2[p][:], ACT.Sin, scale=SIN_SCALE / 2)
                act.drain()
                act.activation(cos_t[p][:], cos_t[p][:], ACT.Square)
                act.drain()
                act.activation(cos_t[p][:], cos_t[p][:], ACT.Copy, scale=-2.0, bias=1.0).then_inc(S["half_ready"], 1)
                act.activation(decay[p][:, :, 1:NC], bc(wave[:, CH, bass.ds(e * QG, QG)], 2, NC - 1), ACT.Copy)\
                    .then_inc(S["decay_ready"], 1)
                act.wait_ge(S["u_ready"], e + 1)
                act.wait_ge(S["y_done"], e * 2 + 2)
                act.activation(u_q[p][:], xs[:, bass.ds(e * QG, QG), :], ACT.Copy).then_inc(S["u_copied"], 1)

            def gelu(e, p):
                act.wait_ge(S["yT_ready"], e + 2)
                act.wait_ge(S["ylo_ready"], e + 1)
                act.activation(t32[p][:].rearrange("p (c t) -> p t c", t=CH), ps[:, 7, :].rearrange("p (t c) -> p t c", t=CH),
                               ACT.Gelu_apprx_tanh).then_inc(S["gelu_ready"], 1)
                act.drain()
                act.activation(h_hi[:, bass.ds(e, 1), :], t32[p][:].unsqueeze(1), ACT.Copy).then_inc(S["yhi_ready"], 1)

            def matrices_out(e, p, use):
                act.wait_ge(S["w_ready"], e + 1)
                for b in range(QG // 4):
                    act.wait_ge(S["psT_ready"], e * 2 + (b + 1))
                    src = ps[:, b, :].rearrange("p (g n) -> p g n", g=4)
                    act.activation(win[p][:, 4 * b:4 * b + 4, 0:P], src, ACT.Copy)
                    act.activation(win[p][:, 4 * b:4 * b + 4, P:P + NS], src[:, :, 0:NS], ACT.Copy, scale=-1.0)\
                        .then_inc(S["psT_free"], 1)
                act.wait_ge(S["convps"], e + 2)
                before = use if p else use - 1
                if not (isinstance(before, int) and before == 0):
                    act.wait_ge(toep_landed[1 - p], before * (16 * CH))
                act.activation(conv[:], ps[:, 2, 0:QG * GH].rearrange("p (g h) -> p g h", g=QG), ACT.Copy)\
                    .then_inc(S["conv_copied"], 1)

            def outputs(e):
                act.wait_ge(S["yT_ready"], e + 1)
                for b in range(QG // 4):
                    act.wait_ge(S["y_done"], e * 2 + (b + 5))
                    act.activation(y_q[0:NC, :, 64 * b:64 * (b + 1)].rearrange("p t (g h) -> p g t h", g=4),
                                   ps[0:NC, 5 + b, :].rearrange("p (g t h) -> p g t h", g=4, t=CH), ACT.Copy)\
                        .then_inc(S["y_evac"], 1)

            def begin(e, p, use):
                act.wait_ge(S["prologue"], 3)
                angles(e, p)
                matrices_out(e, p, use)
                angles(e + 1, 1 - p)
                matrices_out(e + 1, 1, 1)
                outputs(e)

            def step(e, p, use):
                matrices_out(e + 1, 1 - p, use + 1 if p else use)
                gelu(e - 1, 1 - p)
                angles(e + 1, 1 - p)
                outputs(e)

            def finish(e, p, use):
                gelu(e - 1, 1 - p)
                for k in range(LOOK):
                    split_hi(act, k)
                outputs(e)
                gelu(e, p)

            s5_steps(act, begin, step, finish)

        def s5_vector(dve):
            dve.sem_inc(S["rot_done"], 2)
            dve.sem_inc(S["ylo_ready"], 2)
            dve.sem_inc(S["w_free"], 1)
            rho, phi, f1, k1 = (small[:, n, :] for n in (1, 2, 3, 4))
            dve.wait_ge(S["dt"], 1)
            dve.tensor_tensor(rho, lam_re, small[:, 0, :], ALU.mult)
            dve.tensor_tensor(phi, lam_im, small[:, 0, :], ALU.mult)
            dve.drain()
            dve.wait_ge(consts_landed, 32)
            tau = bc(const("tau"), 2, G)
            dve.tensor_scalar(f1, phi, 1.0 / (2 * math.pi), None, ALU.mult)
            dve.tensor_tensor(wave[:], bc(rho, 1, CH + 1), tau, ALU.mult)
            dve.drain()
            dve.tensor_scalar(k1, f1, ROUND, -ROUND, ALU.add, ALU.add)
            dve.drain()
            dve.scalar_tensor_tensor(f1, k1, -C1, phi, ALU.mult, ALU.add)
            dve.drain()
            dve.scalar_tensor_tensor(f1, k1, -C2, f1, ALU.mult, ALU.add)
            dve.drain()
            dve.tensor_scalar(f1, f1, 1.0 / (2 * math.pi), None, ALU.mult)
            dve.drain()
            dve.tensor_tensor(turn[:], bc(f1, 1, CH + 1), tau, ALU.mult)
            dve.drain()
            dve.tensor_scalar(pw_imn[:], turn[:], ROUND, -ROUND, ALU.add, ALU.add)
            dve.drain()
            dve.tensor_tensor(turn[:], turn[:], pw_imn[:], ALU.subtract)
            dve.drain()
            dve.tensor_scalar(turn[:], turn[:], 0.5, -0.5, ALU.min, ALU.max).then_inc(S["turn"], 1)
            dve.drain()
            dve.tensor_scalar(t8_hi, turn[:, CH, :], ROUND / 4096, -ROUND / 4096, ALU.add, ALU.add)
            dve.drain()
            dve.tensor_tensor(t8_lo, turn[:, CH, :], t8_hi, ALU.subtract)
            dve.wait_ge(S["wave"], 1)
            dve.tensor_scalar(pw_re[:], pw_re[:], -2.0, 1.0, ALU.mult, ALU.add)
            dve.tensor_tensor(pw_im[:], pw_im[:], wave[:], ALU.mult)
            dve.drain()
            dve.tensor_tensor(pw_re[:], pw_re[:], wave[:], ALU.mult)
            sg = const("sign")
            dve.tensor_scalar(pw_ims[:], pw_im[:], sg[:, 0:1], None, ALU.mult)
            dve.tensor_scalar(pw_imn[:], pw_im[:], -1.0, None, ALU.mult)
            dve.drain()
            a1, den, t0, t1, qr, qi, t2, t3 = (small[:, n, :] for n in range(5, 13))
            ai = pw_im[:, 1, :]
            dve.tensor_scalar(a1, pw_re[:, 1, :], -1.0, None, ALU.add)
            dve.tensor_tensor(t0, lam_re, lam_re, ALU.mult)
            dve.tensor_tensor(t1, lam_im, lam_im, ALU.mult)
            dve.drain()
            dve.tensor_tensor(den, t0, t1, ALU.add)
            dve.tensor_tensor(t2, ai, lam_re, ALU.mult)
            dve.tensor_tensor(t3, a1, lam_im, ALU.mult)
            dve.drain()
            dve.reciprocal(den, den)
            dve.tensor_tensor(t0, a1, lam_re, ALU.mult)
            dve.tensor_tensor(t1, ai, lam_im, ALU.mult)
            dve.tensor_tensor(qi, t2, t3, ALU.subtract)
            dve.drain()
            dve.tensor_tensor(qr, t0, t1, ALU.add)
            dve.tensor_tensor(qi, qi, den, ALU.mult)
            dve.drain()
            dve.tensor_tensor(qr, qr, den, ALU.mult)
            dve.tensor_scalar(qi, qi, sg[:, 0:1], None, ALU.mult)
            dve.drain().then_inc(S["ratio"], 1)
            scr = wotmp[:].rearrange("p g t h -> p (g t h)").rearrange("p (g h) -> p g h", h=GH)
            dve.wait_ge(S["bc_landed"], 48)
            dve.tensor_tensor(bx, b_raw[0], bc(qr, 2, GH), ALU.mult)
            dve.tensor_tensor(scr, b_raw[1], bc(qi, 2, GH), ALU.mult)
            dve.tensor_scalar(pw_re2[:], pw_re[:], sg[:, 1:2], None, ALU.mult)
            dve.memset(zin[:], 0.0)
            dve.drain()
            dve.tensor_tensor(bx, bx, scr, ALU.add)
            dve.wait_ge(S["sumps"], 1)
            dve.tensor_reduce(sumsq[:], ps[:, 7, :].rearrange("p (g c) -> p c g", c=NC), AX_X, ALU.add).then_inc(S["sumsq"], 1)
            dve.wait_ge(S["std"], 1)
            dve.tensor_scalar(mean5[:], sumsq[:], 1.0 / D, EPS, ALU.mult, ALU.add)
            dve.drain()
            root_reciprocal(dve, rstd5[:], mean5[:], nt5[:])
            dve.drain().then_inc(S["prologue"], 1)

            def matrices(e, p):
                gs = bass.ds(e * QG, QG)
                ang, ang_lo, ang_sum = ang2[p], ang_lo2[p], ang_sum2[p]
                dve.wait_ge(S["ang_ready"], e + 1)
                dve.tensor_scalar(ang_sum[:], ang_sum[:], ROUND, -ROUND, ALU.add, ALU.add)
                dve.wait_ge(S["convps"], e + 1)
                dve.tensor_tensor(winT[:], bc(pw_re[:, 0:CH, gs].rearrange("p t g -> p g t"), 3, GH),
                                  bc(bx[:, gs, :], 2, CH), ALU.mult)
                dve.drain()
                dve.tensor_tensor(ang[:], ang[:], ang_sum[:], ALU.subtract)
                dve.tensor_tensor(wtmp[:], bc(pw_ims[:, 0:CH, gs].rearrange("p t g -> p g t"), 3, GH),
                                  bc(by[:, gs, :], 2, CH), ALU.mult)
                dve.drain()
                dve.tensor_tensor(ang[:], ang[:], ang_lo[:], ALU.add)
                dve.tensor_tensor(winT[:], winT[:], wtmp[:], ALU.add).then_inc(S["winT_ready"], 1)
                dve.drain()
                dve.tensor_scalar(ang[:], ang[:], 0.5, -0.5, ALU.min, ALU.max).then_inc(S["ang_reduced"], 1)

            def low(e, p):
                dve.wait_ge(S["yhi_ready"], e + 1)
                at_ = bass.ds(e, 1)
                dve.tensor_tensor(h_lo[:, at_, :], t32[p][:].unsqueeze(1), h_hi[:, at_, :].bitcast(F32), ALU.subtract)\
                    .then_inc(S["ylo_ready"], 1)

            def recurrence(e, p):
                dve.wait_ge(S["half_ready"], e + 3)
                dve.wait_ge(S["w_ready"], e + 3)
                n1 = NC - 1
                wv = ps[:, 3, :].rearrange("p (g c) -> p g c", c=NC)
                wsw = ps[:, 4, :].rearrange("p (g c) -> p g c", c=NC)
                dve.tensor_tensor(zin[:, :, 1:NC], wv[:, :, 0:n1], cos_t[p][:, :, 1:NC], ALU.mult)
                dve.tensor_tensor(ztmp[:, :, 1:NC], wsw[:, :, 0:n1], sin_t[p][:, :, 1:NC], ALU.mult).then_inc(S["w_free"], 1)
                dve.drain()
                dve.tensor_tensor(zin[:, :, 1:NC], zin[:, :, 1:NC], ztmp[:, :, 1:NC], ALU.add)
                dve.drain()
                dve.wait_ge(S["decay_ready"], e + 1)
                dve.tensor_tensor_scan(zst[:].rearrange("p g c -> p (g c)"), decay[p][:].rearrange("p g c -> p (g c)"),
                                       zin[:].rearrange("p g c -> p (g c)"), 0.0, ALU.mult, ALU.add)
                dve.drain()
                dve.wait_ge(S["y_done"], e * 2 + 2)
                dve.tensor_tensor(zout[p][:], zst[:], cos_t[p][:], ALU.mult)
                dve.tensor_tensor(ztmp[NS:P, :, :], zst[0:NS, :, :], sin_t[p][0:NS, :, :], ALU.mult)
                dve.scalar_tensor_tensor(ztmp[0:NS, :, :], zst[NS:P, :, :], -1.0, sin_t[p][NS:P, :, :], ALU.mult, ALU.mult)\
                    .then_inc(S["rot_done"], 1)
                dve.drain()
                dve.tensor_tensor(zout[p][:], zout[p][:], ztmp[:], ALU.add).then_inc(S["s_ready"], 1)

            def tables(e, p):
                dve.wait_ge(S["conv_copied"], e + 2)
                dve.tensor_tensor(conv[0:GH, :, :], conv[0:GH, :, :], dI[0:GH, bass.ds(e * QG, QG), :], ALU.add)
                dve.drain().then_inc(S["conv_ready"], 1)

            def begin(e, p, use):
                dve.wait_ge(S["prologue"], 3)
                matrices(e, p)
                tables(e, p)
                matrices(e + 1, 1 - p)
                recurrence(e, p)
                tables(e + 1, 1 - p)

            def step(e, p, use):
                matrices(e + 1, 1 - p)
                recurrence(e, p)
                tables(e + 1, 1 - p)
                low(e - 1, 1 - p)

            def finish(e, p, use):
                recurrence(e, p)
                low(e - 1, 1 - p)
                low(e, p)

            s5_steps(dve, begin, step, finish)

        def s5_tensor(pe):
            for n, credits in (("convps", 1), ("w_ready", 2), ("y_done", 4), ("yT_ready", 1)):
                pe.sem_inc(S[n], credits)
            pe.wait_ge(consts_landed, 32)
            for n in range(NQ):
                pe.wait_ge(S["xsq"], n + 1)
                last = pe.matmul(ps[:, 7, :], const("same_token"), xsq[:, n * QG:(n + 1) * QG, :], start=n == 0, stop=n == NQ - 1)
            last.then_inc(S["sumps"], 1)
            pe.wait_ge(S["prologue"], 3)

            def matrices(e):
                pe.wait_ge(S["winT_ready"], e + 1)
                for b in range(QG // 4):
                    pe.wait_ge(S["psT_free"], e * 2 + (b + 1))
                    for g in range(4 * b, 4 * b + 4):
                        last = pe.transpose(ps[:, b, (g % 4) * P:(g % 4 + 1) * P],
                                            winT[:, g, :, :].rearrange("p t h -> p (t h)"), ident)
                    last.then_inc(S["psT_ready"], 1)
                pe.wait_ge(S["conv_copied"], e + 1)
                for g in range(QG):
                    last = pe.matmul(ps[:, 2, g * GH:(g + 1) * GH], winT[:, g, :, :].rearrange("p t h -> p (t h)"),
                                     cxn[:].rearrange("p (g h) -> p g h", h=GH)[:, bass.ds(e * QG + g, 1), :].rearrange("p a h -> p (a h)"),
                                     start=True, stop=True)
                last.then_inc(S["convps"], 1)

            def inputs(e, p):
                pe.wait_ge(S["u_ready"], e + 1)
                pe.wait_ge(S["w_free"], e + 1)
                pe.wait_ge(S["psT_free"], e * 2 + 4)
                for g in range(QG):
                    for bank, c0 in ((3, 0), (4, NS)):
                        last = pe.matmul(ps[:, bank, g * NC:(g + 1) * NC], win[p][:, g, c0:c0 + P],
                                         xs[:, bass.ds(e * QG + g, 1), :].rearrange("p a c -> p (a c)"), start=True, stop=True)
                last.then_inc(S["w_ready"], 1)

            def outputs(e, p, use, between=None):
                pe.wait_ge(toep_landed[p], use * (16 * CH))
                pe.wait_ge(S["u_copied"], e + 1)
                def out_of(g):
                    return ps[0:NC, 5 + g // 4, (g % 4) * P:(g % 4 + 1) * P]

                for g in range(QG):
                    if g % 4 == 0:
                        pe.wait_ge(S["y_evac"], e * 2 + (g // 4 + 1))
                    pe.matmul(out_of(g), u_q[p][:, g, :], toep[p][:, :, g, :], start=g % 4 == 0, stop=False)
                if between:
                    between()
                pe.wait_ge(S["wout_ready"], e + 1)
                pe.wait_ge(S["s_ready"], e + 1)
                for g in range(QG):
                    last = pe.matmul(out_of(g), zout[p][:, g, :], wout[p][:, g, :, :], start=False, stop=g % 4 == 3)
                    if g % 4 == 3:
                        last.then_inc(S["y_done"], 1)

            def turn_outputs(e):
                pe.wait_ge(S["y_evac"], e * 2 + 4)
                pe.wait_ge(S["gelu_ready"], e + 1)
                pe.sem_inc(S["yT_begun"], 1)
                for t in range(CH):
                    last = pe.transpose(ps[:, 7, t * NC:(t + 1) * NC], y_q[0:NC, t, :], ident[0:NC, 0:NC])
                last.then_inc(S["yT_ready"], 1)

            def begin(e, p, use):
                matrices(e)
                inputs(e, p)
                matrices(e + 1)
                outputs(e, p, use, between=lambda: inputs(e + 1, 1 - p))

            def step(e, p, use):
                turn_outputs(e - 1)
                matrices(e + 1)
                outputs(e, p, use, between=lambda: inputs(e + 1, 1 - p))

            def finish(e, p, use):
                turn_outputs(e - 1)
                outputs(e, p, use)
                turn_outputs(e)

            s5_steps(pe, begin, step, finish)

        def done(number):
            return number + 2

        class Gated:
            scaled = sem("gate_scaled")
            gate_done = sem("gate_done")
            pair_done = sem("pair_done")
            part_hi = sem("part_hi")
            out_ready = sem("pair_ready")

            def __init__(self, before, name, pairs, in_ready):
                self.before = before
                self.name, self.pairs, self.in_ready = name, pairs, in_ready

        def gated_tensor(pe, ph, nm=None, free=None):
            def products(slot, bank, kt):
                cols = slice(kt * P, (kt + 1) * P)
                return mm3(pe, ps[:, bank, :], w_hi[slot][:, cols], w_lo[slot][:, cols], h_hi[:, kt, :], h_lo[:, kt, :],
                           kt == 0, kt == KT - 1)

            def pair(jj, it=None, halves=(0, 1)):
                for half in halves:
                    slot, number, _ = unit(FIRST[ph.name] + 2 * jj + half, it)
                    pe.wait_ge(lo_ready, number + 1)
                    for kt in range(KT):
                        last = products(slot, 2 * jj + half, kt)
                    last.then_inc(unit_used, 1)

            pe.wait_ge(ph.pair_done, ph.before + 2)
            if free is not None:
                pe.wait_ge(*free)
            first = [unit(FIRST[ph.name] + half) for half in range(2)]
            pe.wait_ge(lo_ready, first[1][1] + 1)
            for kt in range(KT):
                pe.wait_ge(*ph.in_ready(kt + 1))
                for half in range(2):
                    last = products(first[half][0], half, kt)
                    if kt == KT - 1:
                        last.then_inc(unit_used, 1)
            if nm is not None:
                norm_sums(pe, nm)
            pair(1, None, (0,))
            if nm is not None:
                norm_spread(pe, nm)
            pair(1, None, (1,))
            with pe.Fori(1, ph.pairs // 2) as it:
                for jj in range(2):
                    pe.wait_ge(ph.pair_done, it * 2 + (ph.before + jj + 1))
                    pair(jj, it)

        def ffn_scalar(act, ph):
            with act.Fori(0, ph.pairs // 2) as it:
                for jj in range(2):
                    k = FIRST[ph.name] + 2 * jj
                    split_hi(act, k + LOOK, it)
                    split_hi(act, k + 1 + LOOK, it)
                    act.wait_ge(ph.scaled, it * 2 + (ph.before - KT + jj + 1))
                    act.activation(sq[jj][:], sq[jj][:], ACT.Silu).then_inc(ph.gate_done, 1)
                    act.wait_ge(ph.pair_done, it * 2 + (ph.before + jj + 3))
                    act.activation(hid_hi[:, bass.ds(it * 2 + jj, 1), :], t32[jj][:].unsqueeze(1), ACT.Copy)\
                        .then_inc(ph.part_hi, 1)

        def ffn_vector(dve, ph):
            with dve.Fori(0, ph.pairs // 2) as it:
                for jj in range(2):
                    k = FIRST[ph.name] + 2 * jj
                    dve.wait_ge(unit_used, done(unit(k, it)[1]))
                    dve.tensor_tensor(sq[jj][:], ps[:, 2 * jj, :], spread[:], ALU.mult).then_inc(ph.scaled, 1)
                    dve.wait_ge(unit_used, done(unit(k + 1, it)[1]))
                    dve.tensor_tensor(t32[jj][:], ps[:, 2 * jj + 1, :], spread[:], ALU.mult)
                    dve.drain()
                    dve.wait_ge(ph.gate_done, it * 2 + (ph.before + jj + 1))
                    dve.tensor_tensor(t32[jj][:], t32[jj][:], sq[jj][:], ALU.mult).then_inc(ph.pair_done, 1)
                    dve.wait_ge(ph.part_hi, it * 2 + (ph.before + jj + 1))
                    at_ = bass.ds(it * 2 + jj, 1)
                    dve.tensor_tensor(hid_lo[:, at_, :], t32[jj][:].unsqueeze(1), hid_hi[:, at_, :].bitcast(F32),
                                      ALU.subtract).then_inc(ph.out_ready, 1)

        def glu_scalar(act, ph):
            with act.Fori(0, ph.pairs // 2) as it:
                for jj in range(2):
                    k = FIRST[ph.name] + 2 * jj
                    split_hi(act, k + LOOK, it)
                    split_hi(act, k + 1 + LOOK, it)
                    act.wait_ge(ph.pair_done, it * 2 + (ph.before + jj + 1))
                    act.wait_ge(unit_used, done(unit(k, it)[1]))
                    act.activation(t32[jj][:], ps[:, 2 * jj, :], ACT.Sigmoid).then_inc(ph.gate_done, 1)
                    act.wait_ge(ph.pair_done, it * 2 + (ph.before + jj + 3))
                    act.activation(sq[jj][:], xT[:, bass.ds(it * 2 + jj, 1), :].rearrange("p a t -> p (a t)"), ACT.Square)\
                        .then_inc(ph.part_hi, 1)

        def glu_vector(dve, ph):
            dve.sem_inc(ph.pair_done, 2)
            dve.memset(acc[:], 0.0)
            dve.wait_ge(S["xT_landed"], 16)
            with dve.Fori(0, ph.pairs // 2) as it:
                for jj in range(2):
                    k = FIRST[ph.name] + 2 * jj
                    tile = xT[:, bass.ds(it * 2 + jj, 1), :].rearrange("p a t -> p (a t)")
                    dve.wait_ge(ph.gate_done, it * 2 + (ph.before + jj + 1))
                    dve.wait_ge(unit_used, done(unit(k + 1, it)[1]))
                    dve.tensor_tensor(t32[jj][:], ps[:, 2 * jj + 1, :], t32[jj][:], ALU.mult)
                    dve.drain()
                    dve.tensor_tensor(tile, tile, t32[jj][:], ALU.add).then_inc(ph.pair_done, 1)
                    dve.wait_ge(ph.part_hi, it * 2 + (ph.before + jj + 1))
                    dve.tensor_tensor(acc[:], acc[:], sq[jj][:], ALU.add).then_inc(ph.out_ready, 1)

        class Rows:

            tile_done = sem("rows_tile_done")
            x_ready = sem("rows_x_ready")
            sq_ready = sem("rows_sq_ready")
            acc_ready = sem("rows_acc_ready")

            def __init__(self, nth, name, k_tiles, src_hi, src_lo, in_ready, hi_early=KT, lo_early=KT - 1):
                self.before = nth * KT
                self.hi_early, self.lo_early = hi_early, lo_early
                self.name, self.k_tiles, self.src_hi, self.src_lo, self.in_ready = name, k_tiles, src_hi, src_lo, in_ready

        LAST = 2

        def rows_tensor(pe, ph, banks):
            n0, n = FIRST[ph.name], ph.k_tiles

            def products(k, kt, o, it=None, start=False, stop=False):
                slot = k % R
                cols = slice(o * P, (o + 1) * P)
                if it is None:
                    ah, al = ph.src_hi[:, kt, :], ph.src_lo[:, kt, :]
                else:
                    one = bass.ds(it * R + kt, 1)
                    ah, al = (s[:, one, :].rearrange("p a t -> p (a t)") for s in (ph.src_hi, ph.src_lo))
                return mm3(pe, ps[:, o, :], w_hi[slot][:, cols], w_lo[slot][:, cols], ah, al, start, stop)

            def whole(kt, it=None):
                _, number, _ = unit(n0 + kt, it)
                pe.wait_ge(lo_ready, number + 1)
                pe.wait_ge(*ph.in_ready((kt if it is None else it * R + kt) + 1))
                for o, wait in banks if kt == 0 and it is None else [(o, None) for o in range(KT)]:
                    if wait is not None:
                        pe.wait_ge(*wait)
                    last = products(n0 + kt, kt, o, it, start=(kt == 0 and it is None))
                last.then_inc(unit_used, 1)

            head = (n - R) % R or R
            for kt in range(head):
                whole(kt)
            if n - R > head:
                with pe.Fori(0, (n - R - head) // R) as it:
                    for kt in range(R):
                        whole(head + kt, it)
            for kt in range(n - R, n - LAST):
                whole(kt)
            pe.wait_ge(lo_ready, n0 + n)
            pe.wait_ge(*ph.in_ready(n))
            for o in range(KT):
                for kt in range(n - LAST, n):
                    last = products(n0 + kt, kt, o, stop=(kt == n - 1))
                last.then_inc(ph.tile_done, 1)
            pe.drain().then_inc(unit_used, LAST)

        def rows_scalar(act, ph, nm=None):
            n0, n = FIRST[ph.name], ph.k_tiles
            head = (n - R) % R or R
            for kt in range(head):
                split_hi(act, n0 + kt + LOOK)
            if n - R > head:
                with act.Fori(0, (n - R - head) // R) as it:
                    for kt in range(R):
                        split_hi(act, n0 + head + kt + LOOK, it)
            for kt in range(n - R, n - LAST + 1):
                split_hi(act, n0 + kt + LOOK)

            def square(o):
                act.wait_ge(ph.x_ready, ph.before + o + 1)
                if o >= 2:
                    act.wait_ge(ph.acc_ready, ph.before + o - 1)
                act.activation(sq[o % 2][:], xT[:, o, :], ACT.Square).then_inc(ph.sq_ready, 1)

            for o in range(KT):
                if nm is None:
                    square(o)
                else:
                    act.wait_ge(ph.x_ready, ph.before + o + 1)
                    if o == ph.hi_early:
                        act.wait_ge(ph.tile_done, ph.before + KT)
                    norm_high(act, nm, o)
            for kt in range(n - LAST + 1, n):
                split_hi(act, n0 + kt + LOOK)
            if nm is not None:
                for o in range(KT):
                    square(o)

        def rows_vector(dve, ph, nm=None):
            dve.memset(acc[:], 0.0)
            dve.drain()

            def add_square(o):
                dve.wait_ge(ph.sq_ready, ph.before + o + 1)
                if o:
                    dve.wait_ge(ph.acc_ready, ph.before + o)
                dve.tensor_tensor(acc[:], acc[:], sq[o % 2][:], ALU.add).then_inc(ph.acc_ready, 1)

            for o in range(KT):
                dve.wait_ge(ph.tile_done, ph.before + o + 1)
                dve.tensor_tensor(xT[:, o, :], xT[:, o, :], ps[:, o, :], ALU.add).then_inc(ph.x_ready, 1)
                if o and nm is None:
                    add_square(o - 1)
                elif o and o <= ph.lo_early:
                    norm_low(dve, nm, o - 1)
            if nm is None:
                add_square(KT - 1)
            else:
                for o in range(ph.lo_early, KT):
                    norm_low(dve, nm, o)
                for o in range(KT):
                    add_square(o)

        class Norm:
            sum_ready = sem("norm_sum_ready")
            mean_ready = sem("norm_mean_ready")
            std_ready = sem("norm_std_ready")
            rstd_ready = sem("norm_rstd_ready")
            rstd_spread = sem("norm_spread")
            hi_done = sem("norm_hi_done")
            h_ready = sem("norm_h_ready")

            def __init__(self, nth, spreads, name, acc_ready):
                self.nth, self.before = nth, nth * KT
                self.spreads = spreads
                self.name, self.acc_ready = name, acc_ready

        def norm_sums(pe, nm):
            pe.wait_ge(*nm.acc_ready(KT))
            for tb in range(TB):
                last = pe.matmul(ps[:, 7, tb:tb + 1], acc[:, tb * P:(tb + 1) * P], ones[:, 0:1], start=True, stop=True)
            last.then_inc(nm.sum_ready, 1)

        def norm_spread(pe, nm):
            pe.wait_ge(nm.rstd_ready, nm.nth + 1)
            for tb in range(TB):
                last = pe.matmul(ps[:, 7, tb * P:(tb + 1) * P], tok_rstd[:, tb:tb + 1].broadcast_to([P, P]), ident, start=True, stop=True)
            last.then_inc(nm.rstd_spread, 1)

        def norm_root(act, nm):
            act.wait_ge(nm.mean_ready, nm.nth + 1)
            act.activation(tok_rstd[:], tok_mean[:], ACT.Sqrt).then_inc(nm.std_ready, 1)

        def token_factors(dve, nm):
            dve.wait_ge(nm.sum_ready, nm.nth + 1)
            dve.tensor_scalar(tok_mean[:], ps[:, 7, 0:TB], 1.0 / D, EPS, ALU.mult, ALU.add).then_inc(nm.mean_ready, 1)
            dve.wait_ge(nm.std_ready, nm.nth + 1)
            root_reciprocal(dve, tok_rstd[:], tok_mean[:], tok_tmp[:])
            dve.sem_inc(nm.rstd_ready, 1)

        def gain_of(nm, o):
            return vec[:, VEC_AT[nm.name] + o:VEC_AT[nm.name] + o + 1]

        def norm_high(act, nm, o):
            act.activation(h_hi[:, o, :], xT[:, o, :], ACT.Copy, scale=gain_of(nm, o)).then_inc(nm.hi_done, 1)

        def norm_low(dve, nm, o):
            dve.wait_ge(nm.hi_done, nm.before + o + 1)
            dve.scalar_tensor_tensor(h_lo[:, o, :], xT[:, o, :], gain_of(nm, o), h_hi[:, o, :].bitcast(F32), ALU.mult, ALU.subtract)\
                .then_inc(nm.h_ready, 1)

        def glu_norm_scalar(act, nm, ph):
            act.wait_ge(unit_used, done(FIRST[ph.name] + PHASES[ph.name] - 1))
            for o in range(KT):
                act.wait_ge(ph.pair_done, ph.before + o + 3)
                norm_high(act, nm, o)

        def glu_norm_vector(dve, nm):
            for o in range(KT):
                norm_low(dve, nm, o)

        BLOCKS = [3, 2, 0, 1]
        P_AT = {3: 0, 2: 4 * P, 0: 7 * P, 1: 8 * P}
        L_AT = {3: (0, 0), 2: (1, 0), 0: (1, 3 * P), 1: (2, 0)}
        T_AT = {0: (3, 0), 1: (4, 0), 3: (4, 3 * P), 2: (5, 0)}
        PT_AT = {kb: (bank - 3) * T + c for kb, (bank, c) in T_AT.items()}
        N_P = P * TB * (TB + 1) // 2
        PR_BUFS, PT_BUFS = 3, 2

        class Attention:

            def __init__(self, name, heads, qT, kT, val, mask, pr, pt, nmax, den, hi, lo):
                self.heads, self.qT, self.kT, self.val, self.mask = heads, qT, kT, val, mask
                self.pr, self.pt, self.nmax, self.den, self.hi, self.lo = pr, pt, nmax, den, hi, lo
                self.L_ready = sem(name + "_L_ready")
                self.masked = sem(name + "_masked")
                self.p_ready = sem(name + "_p_ready")
                self.r_ready = sem(name + "_r_ready")
                self.scaled = sem(name + "_scaled")
                self.pT_ready = sem(name + "_pT_ready")
                self.pt_out = sem(name + "_pt_out")
                self.pv_done = sem(name + "_pv_done")
                self.o_hi = sem(name + "_o_hi")
                self.o_done = sem(name + "_o_done")

            def tiles_ready(self, n):
                return self.o_done, 2 * n

        def attn_tensor(pe, a, banks_free=None):
            def logits(h):
                rows = slice(HD * (h % 2), HD * (h % 2 + 1))
                for k, tb in enumerate(BLOCKS):
                    bank, c = L_AT[tb]
                    if h and tb != 0:
                        pe.wait_ge(a.masked, TB * (h - 1) + {3: 1, 2: 3, 1: 4}[tb])
                    keys = (tb + 1) * P
                    last = pe.matmul(ps[:, bank, c:c + keys], a.qT[rows, h // 2, tb * P:(tb + 1) * P], a.kT[rows, h // 2, 0:keys],
                                     start=True, stop=True)
                    if tb != 2:
                        last.then_inc(a.L_ready, 1)

            def turn(h):
                pe.wait_ge(a.scaled, h + 1)
                for bank, kbs in ((3, (0,)), (4, (1, 3)), (5, (2,))):
                    if h:
                        pe.wait_ge(a.pt_out, 3 * (h - 1) + bank - 2)
                    for kb in kbs:
                        for tb in range(kb, TB):
                            c = T_AT[kb][1] + (tb - kb) * P
                            p = P_AT[tb] + kb * P
                            last = pe.transpose(ps[:, bank, c:c + P], a.pr[h % PR_BUFS][:, p:p + P], ident)
                    last.then_inc(a.pT_ready, 1)

            def values(h):
                pe.wait_ge(a.pt_out, 3 * (h + 1))
                if h >= 2:
                    pe.wait_ge(a.o_done, h - 1)
                for kb in range(TB):
                    n = T - kb * P
                    last = pe.matmul(ps[:, 6 + h % 2, kb * P:T], a.val[:, kb, (h // 2) * P:(h // 2 + 1) * P],
                                     a.pt[h % PT_BUFS][:, PT_AT[kb]:PT_AT[kb] + n], start=(kb == 0), stop=(kb == TB - 1))
                last.then_inc(a.pv_done, 1)

            logits(0)
            logits(1)
            if banks_free is not None:
                pe.wait_ge(*banks_free)
            for h in range(a.heads):
                turn(h)
                if h + 2 < a.heads:
                    logits(h + 2)
                if h:
                    values(h - 1)
            values(a.heads - 1)

        def attn_scalar(act, a):
            def block(tb):
                return slice(P_AT[tb], P_AT[tb] + (tb + 1) * P)

            def exps(h):
                for k, tb in enumerate(BLOCKS):
                    act.wait_ge(a.masked, TB * h + k + 1)
                    p, n = a.pr[h % PR_BUFS][:, block(tb)], h * TB + tb
                    last = act.activation(p, p, ACT.Exp, bias=a.nmax[:, n:n + 1], scale=-1.0, accum_out=a.den[:, n:n + 1])
                last.then_inc(a.p_ready, 1)

            def scale(h):
                act.wait_ge(a.r_ready, h + 1)
                for tb in BLOCKS:
                    p, n = a.pr[h % PR_BUFS][:, block(tb)], h * TB + tb
                    last = act.activation(p, p, ACT.Copy, scale=a.den[:, n:n + 1])
                last.then_inc(a.scaled, 1)

            def high(h):
                act.wait_ge(a.pv_done, h + 1)
                rows = slice(HD * (h % 2), HD * (h % 2 + 1))
                act.activation(a.hi[rows, h // 2, :], ps[rows, 6 + h % 2, :], ACT.Copy).then_inc(a.o_hi, 1)

            exps(0)
            scale(0)
            exps(1)
            for h in range(a.heads):
                if h + 1 < a.heads:
                    scale(h + 1)
                if h >= 2:
                    high(h - 2)
                if h + 2 < a.heads:
                    exps(h + 2)
            high(a.heads - 2)
            high(a.heads - 1)

        def attn_vector(dve, a):
            def masks(h):
                if h >= PR_BUFS:
                    dve.wait_ge(a.pT_ready, 3 * (h - PR_BUFS + 1))
                for tb in BLOCKS:
                    bank, c = L_AT[tb]
                    keys, n = (tb + 1) * P, h * TB + tb
                    dve.wait_ge(a.L_ready, 3 * h + bank + 1)
                    dve.tensor_tensor_reduce(out=a.pr[h % PR_BUFS][:, P_AT[tb]:P_AT[tb] + keys], in0=ps[:, bank, c:c + keys],
                                             in1=a.mask(tb, h), scale=-(HD ** -0.5), scalar=3e38, op0=ALU.add, op1=ALU.min,
                                             accum_out=a.nmax[:, n:n + 1]).then_inc(a.masked, 1)

            def reciprocals(h):
                dve.wait_ge(a.p_ready, h + 1)
                r = a.den[:, h * TB:(h + 1) * TB]
                dve.reciprocal(r, r).then_inc(a.r_ready, 1)

            def turned_out(h):
                if h >= PT_BUFS:
                    dve.wait_ge(a.pv_done, h - PT_BUFS + 1)
                for k in range(3):
                    n = T if k < 2 else N_P - 2 * T
                    dve.wait_ge(a.pT_ready, 3 * h + k + 1)
                    dve.tensor_copy(a.pt[h % PT_BUFS][:, k * T:k * T + n], ps[:, 3 + k, 0:n]).then_inc(a.pt_out, 1)

            def low(h):
                dve.wait_ge(a.o_hi, h + 1)
                rows = slice(HD * (h % 2), HD * (h % 2 + 1))
                dve.tensor_tensor(a.lo[rows, h // 2, :], ps[rows, 6 + h % 2, :], a.hi[rows, h // 2, :].bitcast(F32), ALU.subtract)\
                    .then_inc(a.o_done, 1)

            masks(0)
            reciprocals(0)
            masks(1)
            for h in range(a.heads):
                if h + 1 < a.heads:
                    reciprocals(h + 1)
                turned_out(h)
                if h + 2 < a.heads:
                    masks(h + 2)
                if h >= 2:
                    low(h - 2)
            low(a.heads - 2)
            low(a.heads - 1)

        o6 = [BIGR]

        def dsabuf(name, shape, parts=P):
            off = o6[0]
            o6[0] += -(-4 * int(np.prod(shape)) // 32) * 32
            assert o6[0] <= end, name
            return at(name, shape, off)

        qT = dsabuf("qT", [KT, T])
        kT = dsabuf("kT", [KT, T])
        val = dsabuf("val", [TB, D])
        raw_off = o6[0]
        rawp = [dsabuf(f"rawp{n}", [TB, GROUP]) for n in range(2)]
        rope_off = o6[0]
        rope_a = dsabuf("rope_a", [2, GROUP])
        rope_b = dsabuf("rope_b", [2, GROUP])
        qi_off = o6[0]
        qiT = dsabuf("qiT", [IH // 2, T])
        kiT = dsabuf("kiT", [T])
        kin = dsabuf("kin", [TB, 2 * HD])
        rope = dsabuf("rope", [2, TB, HD])
        hgain = dsabuf("hgain", [2, HD])
        rtab = dsabuf("rtab", [2, 2, TB, HD])
        wi = dsabuf("wi", [TB, IH])
        hsum, hstd, htmp = (dsabuf(n, [TB * 8]) for n in ("hsum", "hstd", "htmp"))
        kisum, kistd, kitmp = (dsabuf(n, [TB]) for n in ("kisum", "kistd", "kitmp"))
        nmax = dsabuf("nmax", [TB * NH])
        den = dsabuf("den", [TB * NH])
        top8 = dsabuf("top8", [3, 8])
        hsq = at("hsq", [TB, GROUP], rope_off)
        pr = [at(f"pr{n}", [N_P], raw_off + 4 * N_P * n) for n in range(PR_BUFS)]
        pt = [at(f"pt{n}", [N_P], raw_off + 4 * N_P * (PR_BUFS + n)) for n in range(PT_BUFS)]
        assert raw_off + 4 * N_P * (PR_BUFS + PT_BUFS) <= qi_off + 8 * KB
        score = [None] + [at(f"score{n}", [T], SCR + 2 * KB * (1 + n)) for n in range(3)]
        relu = [at(f"relu{n}", [T], SCR + 8 * KB + 2 * KB * n) for n in range(2)]

        A = {n: sem("dsa_" + n) for n in (
            "par_landed", "raw_ready", "sums_ready", "std_ready", "roped", "tr_ready", "tr_evac", "rem_copied", "wi_scale", "rem_turned", "rem_ready", 
            "ki_ready", "val_ready", "idx_ready", "relu_ready", "relu_used")}
        att1 = Attention("att1", NH, qT, kT, val,
                         lambda tb, h: const("causal") if tb == 0 else score[tb][:, 0:(tb + 1) * P], pr, pt, nmax, den, h_hi, h_lo)
        QI, REM, Q0, Q1, K0, K1, V0, V1 = range(8)
        HALF = {QI: 0, REM: 1, Q0: 0, Q1: 1, K0: 0, K1: 1, V0: 0, V1: 1}
        UNIT_OF = {QI: 0, REM: 4, Q0: 5, Q1: 9, K0: 13, K1: 17, V0: 21, V1: 25}
        ROT = [QI, Q0, Q1, K0, K1]
        HALF_T = {QI: 1, Q0: 1, Q1: 0, K0: 1, K1: 0}
        RAWBUF = {g: n % 2 for n, g in enumerate(ROT)}
        n_dsa = FIRST["dsa"] if "dsa" in FIRST else 0

        def end_of(g):
            return n_dsa + UNIT_OF[g] + (0 if g == REM else 3)

        def project_narrow(pe, w0, width, copied, buf):
            slot, number, _ = unit(w0)
            pe.wait_ge(lo_ready, number + 1)
            for kt in range(KT):
                cols = slice(kt * P, kt * P + width)
                last = mm3(pe, ps[0:width, 4, :], w_hi[slot][:, cols], w_lo[slot][:, cols], h_hi[:, kt, :], h_lo[:, kt, :],
                           kt == 0, kt == KT - 1)
            last.then_inc(unit_used, 1)
            pe.wait_ge(copied, 1)
            for tb in range(TB):
                last = pe.transpose(ps[:, 4 + tb, 0:width], buf[0:width, tb * P:(tb + 1) * P], ident[0:width, 0:width])
            return last

        def project(pe, w0, group_half, units, in_ready=None, width=GROUP, n_kt=2, nm=None, aside=None, before_unit=2):
            for u in range(units):
                slot, number, _ = unit(w0 + u)
                pe.wait_ge(lo_ready, number + 1)
                for k2 in range(n_kt):
                    kt = u * n_kt + k2
                    if in_ready is not None:
                        pe.wait_ge(*in_ready(kt + 1))
                    step = UNIT // n_kt
                    wh, wl = w_hi[slot][:, k2 * step:k2 * step + width], w_lo[slot][:, k2 * step:k2 * step + width]
                    for tb in range(TB):
                        toks = slice(tb * P, (tb + 1) * P)
                        o = ps[:, 4 * group_half + tb, 0:width]
                        pe.matmul(o, h_hi[:, kt, toks], wh, start=(kt == 0), stop=False)
                        pe.matmul(o, h_hi[:, kt, toks], wl, start=False, stop=False)
                        last = pe.matmul(o, h_lo[:, kt, toks], wh, start=False, stop=(kt == KT - 1))
                last.then_inc(unit_used, 1)
                if nm is not None and u == 1:
                    norm_sums(pe, nm)
                if aside is not None and u == before_unit - 1:
                    aside()

        def dsa_tensor(pe, nm):
            def proj(g, in_ready=None, aside=None):
                if g == REM:
                    project_narrow(pe, n_dsa + UNIT_OF[g], HD + IH, A["rem_copied"], relu[1]).then_inc(A["rem_turned"], 1)
                else:
                    project(pe, n_dsa + UNIT_OF[g], HALF[g], 4, in_ready, nm=nm if g == QI else None, aside=aside)

            def transposes(g):
                n = ROT.index(g)
                pe.wait_ge(A["roped"], n + 1)
                for c in range(4):
                    for tb in range(TB):
                        last = pe.transpose(ps[:, 4 * HALF_T[g] + c, tb * P:(tb + 1) * P], rawp[RAWBUF[g]][:, tb, c * P:(c + 1) * P], ident)
                    last.then_inc(A["tr_ready"], 1)

            pe.wait_ge(down0.x_ready, down0.before + TB)
            proj(QI, after(nm.h_ready, nm.before))
            proj(REM)
            pe.wait_ge(A["raw_ready"], 1)
            proj(Q0)
            pe.wait_ge(A["rem_ready"], 1)
            transposes(QI)
            pe.wait_ge(A["ki_ready"], 1)
            pe.wait_ge(A["tr_evac"], 1)
            for tb in range(TB):
                last = pe.transpose(ps[:, 4, tb * P:(tb + 1) * P], kin[:, tb, :], ident)
            last.then_inc(A["tr_ready"], 1)
            pe.wait_ge(A["tr_evac"], 5)
            for n in range(3 * IH):
                tb, h = 1 + n // IH, n % IH
                rows = slice(HD * (h % 2), HD * (h % 2 + 1))
                keys = (tb + 1) * P
                if n >= 2:
                    pe.wait_ge(A["relu_ready"], n - 1)
                pe.matmul(ps[:, 4 + n % 2, 0:keys], qiT[rows, h // 2, tb * P:(tb + 1) * P], kiT[rows, 0:keys],
                          start=True, stop=True).then_inc(A["idx_ready"], 1)
            pe.wait_ge(A["relu_ready"], 3 * IH)
            proj(Q1)
            for g, last, before in ((K0, Q1, Q0), (K1, K0, Q1), (V0, K1, K0)):
                pe.wait_ge(A["raw_ready"], ROT.index(before) + 1)
                if before != Q0:
                    pe.wait_ge(A["tr_evac"], 5 + 4 * (ROT.index(before) - 1))

                def turn_before():
                    pe.wait_ge(A["raw_ready"], ROT.index(last) + 1)
                    transposes(before)

                proj(g, aside=turn_before)
            pe.wait_ge(A["raw_ready"], ROT.index(K1) + 1)
            pe.wait_ge(A["tr_evac"], 5 + 4 * ROT.index(K0))

            def turn_last():
                pe.wait_ge(A["val_ready"], 1)
                transposes(K1)

            proj(V1, aside=turn_last)
            pe.wait_ge(A["tr_evac"], 5 + 4 * ROT.index(K1))
            attn_tensor(pe, att1, banks_free=(A["val_ready"], 2))

        def dsa_scalar(act, nm):
            def factor(tb):
                return tok_rstd[:, tb:tb + 1]

            def split(g, u):
                split_hi(act, n_dsa + UNIT_OF[g] + u + LOOK)

            def raw_out(g):
                n = ROT.index(g)
                act.wait_ge(unit_used, done(end_of(g)))
                if n >= 2:
                    act.wait_ge(A["tr_ready"], 4 * (n - 1) + (1 if n >= 2 else 0))
                for tb in range(TB):
                    last = act.activation(rawp[RAWBUF[g]][:, tb, :], ps[:, 4 * HALF[g] + tb, :], ACT.Copy, scale=factor(tb))
                if g != QI:
                    act.wait_ge(A["roped"], n)
                    for tb in range(TB):
                        last = act.activation(hsq[:, tb, :], ps[:, 4 * HALF[g] + tb, :], ACT.Square, scale=factor(tb))
                last.then_inc(A["raw_ready"], 1)

            def std(g):
                n = ROT.index(g)
                act.wait_ge(A["sums_ready"], n)
                act.activation(hstd[:], hsum[:], ACT.Sqrt).then_inc(A["std_ready"], 1)

            def tr_out(g):
                n = ROT.index(g)
                first = 4 * n + (1 if n else 0)
                for c in range(4):
                    act.wait_ge(A["tr_ready"], first + c + 1)
                    o = {QI: qiT[:, c, :], Q0: qT[:, c, :], Q1: qT[:, 4 + c, :], K0: kT[:, c, :], K1: kT[:, 4 + c, :]}[g]
                    act.activation(o, ps[:, 4 * HALF_T[g] + c, :], ACT.Copy).then_inc(A["tr_evac"], 1)

            split(QI, 0)
            split(QI, 1)
            norm_root(act, nm)
            split(QI, 2)
            split(QI, 3)
            act.wait_ge(nm.rstd_ready, nm.nth + 1)
            raw_out(QI)
            split(REM, 0)
            act.wait_ge(unit_used, done(end_of(REM)))
            act.activation(relu[1][0:HD + IH, :], ps[0:HD + IH, 4, :], ACT.Copy).then_inc(A["rem_copied"], 1)
            act.wait_ge(A["rem_turned"], 1)
            act.wait_ge(A["wi_scale"], 1)
            for tb in range(TB):
                act.activation(kin[:, tb, 0:HD], ps[:, 4 + tb, 0:HD], ACT.Copy, scale=factor(tb))
                act.activation(wi[:, tb, :], ps[:, 4 + tb, HD:HD + IH], ACT.Copy, scale=tok_wi[:, tb:tb + 1])
                last = act.activation(relu[0][:, 0:HD], ps[:, 4 + tb, 0:HD], ACT.Square, scale=factor(tb), accum_out=kisum[:, tb:tb + 1])
                act.drain()
            last = act.activation(kistd[:], kisum[:], ACT.Sqrt, bias=eps, scale=1.0 / HD)
            last.then_inc(A["rem_ready"], 1)
            for u in range(4):
                split(Q0, u)
            tr_out(QI)
            act.wait_ge(A["tr_ready"], 5)
            act.activation(kiT[:], ps[:, 4, :], ACT.Copy).then_inc(A["tr_evac"], 1)
            for n in range(3 * IH):
                tb = 1 + n // IH
                keys = (tb + 1) * P
                act.wait_ge(A["idx_ready"], n + 1)
                if n >= 2:
                    act.wait_ge(A["relu_used"], n - 1)
                act.activation(relu[n % 2][:, 0:keys], ps[:, 4 + n % 2, 0:keys], ACT.Relu).then_inc(A["relu_ready"], 1)
            for g, before in ((Q1, Q0), (K0, Q1), (K1, K0), (V0, K1)):
                split(g, 0)
                raw_out(before)
                split(g, 1)
                std(before)
                split(g, 2)
                split(g, 3)
                if before != Q0:
                    tr_out(ROT[ROT.index(before) - 1])
            for half, g in ((0, V0), (1, V1)):
                if g == V1:
                    for u in range(4):
                        split(V1, u)
                    tr_out(K1)
                act.wait_ge(unit_used, done(end_of(g)))
                for tb in range(TB):
                    last = act.activation(val[:, tb, half * GROUP:(half + 1) * GROUP], ps[:, 4 * HALF[g] + tb, :], ACT.Copy,
                                          scale=factor(tb))
                last.then_inc(A["val_ready"], 1)
            attn_scalar(act, att1)

        def dsa_vector(dve, nm):
            token_factors(dve, nm)
            dve.tensor_scalar(tok_wi[:], tok_rstd[:], float(np.float32(IH ** -0.5)) * HD ** -0.5, None, ALU.mult)\
                .then_inc(A["wi_scale"], 1)
            dve.wait_ge(A["par_landed"], 32)
            for which in range(2):
                for part in range(2):
                    dve.tensor_tensor(rtab[:, which, part, :, :], rope[:, part, :, :], bc(hgain[:, which, :], 1, TB), ALU.mult)
            dve.drain()
            HH = HD // 2

            def rotate(g):
                buf = rawp[RAWBUF[g]]
                cs = [rope[:, part, :, :] for part in range(2)] if g == QI else \
                    [rtab[:, 0 if g in (Q0, Q1) else 1, part, :, :] for part in range(2)]
                for half in range(2):
                    tbs = slice(2 * half, 2 * half + 2)
                    x = buf[:, tbs, :].rearrange("p b (h d) -> p b h d", d=HD)
                    a, b = (t[:].rearrange("p b (h d) -> p b h d", d=HD) for t in (rope_a, rope_b))
                    dve.tensor_tensor(a, x, bc(cs[0][:, tbs, :], 2, 8), ALU.mult)
                    dve.tensor_tensor(b, x, bc(cs[1][:, tbs, :], 2, 8), ALU.mult)
                    dve.drain()
                    dve.tensor_tensor(x[:, :, :, 0:HH], a[:, :, :, 0:HH], b[:, :, :, HH:HD], ALU.subtract)
                    last = dve.tensor_tensor(x[:, :, :, HH:HD], a[:, :, :, HH:HD], b[:, :, :, 0:HH], ALU.add)
                    if half == 0:
                        dve.drain()
                last.then_inc(A["roped"], 1)

            def head_sums(g):
                dve.wait_ge(A["raw_ready"], ROT.index(g) + 1)
                dve.tensor_reduce(hsum[:], hsq[:].rearrange("p b (h d) -> p (b h) d", d=HD), AX_X, ALU.add)
                dve.drain()
                dve.tensor_scalar(hsum[:], hsum[:], 1.0 / HD, EPS, ALU.mult, ALU.add).then_inc(A["sums_ready"], 1)

            def head_norm(g):
                dve.wait_ge(A["std_ready"], ROT.index(g))
                root_reciprocal(dve, hstd[:], hsum[:], htmp[:])
                x = rawp[RAWBUF[g]][:].rearrange("p b (h d) -> p (b h) d", d=HD)
                dve.tensor_tensor(x, x, bc(hstd[:], 2, HD), ALU.mult)
                dve.drain()
                rotate(g)

            dve.wait_ge(A["raw_ready"], 1)
            rotate(QI)
            dve.wait_ge(A["rem_ready"], 1)
            dve.tensor_scalar(kisum[:], kisum[:], 1.0 / HD, EPS, ALU.mult, ALU.add)
            dve.drain()
            root_reciprocal(dve, kistd[:], kisum[:], kitmp[:])
            ki = kin[:, :, 0:HD]
            dve.tensor_tensor(ki, ki, bc(kistd[:], 2, HD), ALU.mult)
            dve.drain()
            a, b = (t[:].rearrange("p b n -> p (b n)")[:, 0:TB * HD].rearrange("p (b d) -> p b d", d=HD) for t in (rope_a, rope_b))
            dve.tensor_tensor(a, ki, rope[:, 0, :, :], ALU.mult)
            dve.tensor_tensor(b, ki, rope[:, 1, :, :], ALU.mult)
            dve.drain()
            for copy in range(2):
                o = kin[:, :, copy * HD:(copy + 1) * HD]
                dve.tensor_tensor(o[:, :, 0:HH], a[:, :, 0:HH], b[:, :, HH:HD], ALU.subtract)
                last = dve.tensor_tensor(o[:, :, HH:HD], a[:, :, HH:HD], b[:, :, 0:HH], ALU.add)
            last.then_inc(A["ki_ready"], 1)
            for tb in range(1, TB):
                dve.memset(score[tb][:, 0:tb * P], 0.0)
                dve.tensor_copy(score[tb][:, tb * P:(tb + 1) * P], const("causal"))
            dve.drain()
            for n in range(3 * IH):
                tb, h = 1 + n // IH, n % IH
                keys = (tb + 1) * P
                dve.wait_ge(A["relu_ready"], n + 1)
                if n:
                    dve.wait_ge(A["relu_used"], n)
                dve.scalar_tensor_tensor(score[tb][:, 0:keys], relu[n % 2][:, 0:keys], wi[:, tb, h:h + 1], score[tb][:, 0:keys],
                                         ALU.mult, ALU.add).then_inc(A["relu_used"], 1)
            dve.drain()

            def select(rounds):
                def one():
                    for tb in range(1, TB):
                        dve.max(top8[:, tb - 1, :], score[tb][:, 0:(tb + 1) * P])
                    dve.drain()
                    for tb in range(1, TB):
                        s = score[tb][:, 0:(tb + 1) * P]
                        dve.match_replace(s, top8[:, tb - 1, :], s, TAKEN)
                    dve.drain()

                for _ in range(rounds % 2):
                    one()
                if rounds >= 4:
                    with dve.Fori(0, rounds // 2):
                        one()
                        one()
                else:
                    for _ in range(rounds // 2 * 2):
                        one()

            for g in (Q0, Q1, K0, K1):
                head_sums(g)
                select(1)
                head_norm(g)
                select(2)
            select(TOPK // 8 - 12)
            for tb in range(1, TB):
                s = score[tb][:, 0:(tb + 1) * P]
                dve.tensor_scalar(s, s, -1e37, -BIG, ALU.is_gt, ALU.mult)
            dve.drain()

            attn_vector(dve, att1)

        o7 = [BIGR]

        def mixbuf(name, shape, dt=F32):
            off = o7[0]
            o7[0] += -(-4 * int(np.prod(shape)) // 32) * 32
            assert o7[0] <= end, name
            return at(name, shape, off, dt)

        v2 = mixbuf("v2", [TB, GROUP])
        conv_off = o7[0]
        convT = mixbuf("convT", [XT + LT, T])
        gqk_off = o7[0]
        gqkT = mixbuf("gqkT", [12, T])
        z2 = mixbuf("z2", [TB, GROUP])
        bias_off = o7[0]
        abias = mixbuf("abias", [AH, T])
        gates = mixbuf("gates", [LT, 2, P])
        normw = mixbuf("normw", [GROUP])
        convw = mixbuf("convw", [XT + LT, CW + 1])
        lvec = mixbuf("lvec", [3, LT])
        svec = mixbuf("svec", [3, SH])
        sp8 = mixbuf("sp8", [6, LT])
        factors = mixbuf("factors", [T])
        dts = mixbuf("dts", [6, TB * SH])
        dt_, dtA, acs, tot, eacs, cdec = (mixbuf(n, [TB * SH]) for n in ("dt_", "dtA", "acs", "tot", "eacs", "cdec"))
        dtdec, gsum, gstd, gtmp = mixbuf("dtdec", [TB * SH]), *(mixbuf(n, [2]) for n in ("gsum", "gstd", "gtmp"))
        nmax2, den2 = mixbuf("nmax2", [TB * AH]), mixbuf("den2", [TB * AH])
        lmat_off = o7[0]
        lmat = mixbuf("lmat", [SH, P])
        r4, i4 = at("r4", [LT, T], bias_off), at("i4", [LT, T], bias_off + 8 * KB)
        a4 = at("a4", [LT, T], SCR)
        asq = [at(f"asq{n}", [T], SCR + 8 * KB + 2 * KB * n) for n in range(2)]
        H2 = HT + 24 * KB
        xdt, xdec, ysk0, ysk1, prev, junk = (at(n, [GROUP], SCR + 2 * KB * m)
                                             for m, n in enumerate(("xdt", "xdec", "ysk0", "ysk1", "prev", "junk")))
        ysk = [ysk0, ysk1]
        btok_off = o7[0]
        btok = mixbuf("btok", [SG * SN])
        assert btok_off == lmat_off + 4 * KB
        pr2 = [at(f"pr2_{n}", [N_P], o) for n, o in enumerate((SCR, SCR + 4 * N_P, H2))]
        pt2 = [at(f"pt2_{n}", [N_P], o) for n, o in enumerate((gqk_off, lmat_off))]
        mix_hi = at("mix_hi", [12, T], HT, F32R)
        mix_lo = at("mix_lo", [12, T], conv_off, F32R)
        xT3 = convT[:, XT:XT + LT, :]
        gT = gqkT[:, 0:LT, :]
        dt_cols = gqkT[:, 0, :]
        q2T, k2T = gqkT[:, 4:8, :], gqkT[:, 8:12, :]

        M = {n: sem("mix_" + n) for n in (
            "par_landed", "bias_landed", "factors", "scaled", "tap_ready", "conv_done", "silu_ready", "copied", "gelu_ready", "z_ready", "v_ready",
            "lru_ps", "lru_gates", "lru_small", "lru_e", "lru_sp", "lru_a", "lru_sq", "lru_u2", "lru_root", "lru_scan", "lru_done", "yo_out",
            "dt_copied", "dt_turned", "dt_e", "dt_sum", "dt_ready", "acs_ps", "acs_out", "dec_in", "dec_out", "x_ps", "b_ps", "b_out",
            "g_ps", "bc_ps", "x_out", "seg_ready", "L_exp", "S_ready", "yd_ps", "yo_ps", "st_ps", "prev_ready", "y_ready",
            "y_std", "y_done", "yT_ready", "l_hi")}
        att2 = Attention("att2", AH, q2T, k2T, v2, lambda tb, h: abias[:, h, (TB - 1 - tb) * P:T], pr2, pt2, nmax2, den2, mix_hi, mix_lo)
        n_mix = FIRST["mix"]
        DT0, Z0, VV0, TILE0 = 12, 13, 17, 21
        PER_CHUNK = (PHASES["mix"] - TILE0) // TB

        def log1p_series(dve, e, s, s2, p):
            dve.tensor_scalar(s, e, 2.0, None, ALU.add)
            dve.drain()
            dve.reciprocal(s, s)
            dve.drain()
            dve.tensor_tensor(s, s, e, ALU.mult)
            dve.drain()
            dve.tensor_tensor(s2, s, s, ALU.mult)
            dve.drain()
            dve.tensor_scalar(p, s2, 1.0 / 17, None, ALU.mult)
            for k in (15, 13, 11, 9, 7, 5, 3):
                dve.drain()
                dve.scalar_tensor_tensor(p, p, 1.0 / k, s2, ALU.add, ALU.mult)
            dve.drain()
            dve.scalar_tensor_tensor(p, p, 1.0, s, ALU.add, ALU.mult)
            dve.drain()
            dve.tensor_scalar(p, p, 2.0, None, ALU.mult)
            dve.drain()

        def mix_tensor(pe, nm):
            def tile(k, it, bank, in_ready):
                slot, number, _ = unit(k, it)
                pe.wait_ge(lo_ready, number + 1)
                for kt in range(KT):
                    if in_ready is not None:
                        pe.wait_ge(*in_ready(kt + 1))
                    cols = slice(kt * P, (kt + 1) * P)
                    last = mm3(pe, ps[:, bank, :], w_hi[slot][:, cols], w_lo[slot][:, cols], h_hi[:, kt, :], h_lo[:, kt, :],
                               kt == 0, kt == KT - 1)
                last.then_inc(unit_used, 1)

            first = [unit(n_mix + b) for b in range(2)]
            pe.wait_ge(down1.x_ready, down1.before + 2)
            pe.wait_ge(lo_ready, first[1][1] + 1)
            for kt in range(KT):
                pe.wait_ge(nm.h_ready, nm.before + kt + 1)
                for b in range(2):
                    cols = slice(kt * P, (kt + 1) * P)
                    slot = first[b][0]
                    last = mm3(pe, ps[:, b, :], w_hi[slot][:, cols], w_lo[slot][:, cols], h_hi[:, kt, :], h_lo[:, kt, :],
                               kt == 0, kt == KT - 1)
                    if kt == KT - 1:
                        last.then_inc(unit_used, 1)
            norm_sums(pe, nm)
            tile(n_mix + 2, None, 2, None)
            norm_spread(pe, nm)
            tile(n_mix + 3, None, 3, None)

            def gates_of(j0):
                pe.wait_ge(M["conv_done"], 4 + j0 + 2)
                for j in range(j0, j0 + 2):
                    for which in range(2):
                        if j >= 2:
                            pe.wait_ge(M["lru_gates"], 2 * (j - 2) + which + 1)
                        pe.matmul(ps[:, 4 + 2 * (j % 2) + which, :], gates[:, j, which, :], xT3[:, j, :], start=True, stop=True)\
                            .then_inc(M["lru_ps"], 1)

            for it in range(1, 3):
                for b in range(4):
                    if it == 2 and b % 2 == 0:
                        pe.wait_ge(M["par_landed"], 16 * 5)
                        gates_of(b)
                    pe.wait_ge(M["conv_done"], it * 4 + (b + 1))
                    tile(n_mix + b, it, b, None)
            pe.wait_ge(M["lru_gates"], 2 * LT)
            project_narrow(pe, n_mix + DT0, SH, M["dt_copied"], dt_cols).then_inc(M["dt_turned"], 1)
            pe.wait_ge(M["conv_done"], 12 + 4)

            def running_sums():
                pe.wait_ge(M["dt_ready"], 1)
                pe.matmul(ps[:, 4, 0:TB * SH], const("tri"), dtA[:], start=True, stop=True)
                pe.matmul(ps[:, 5, 0:TB * SH], ones, dtA[:], start=True, stop=True).then_inc(M["acs_ps"], 1)

            project(pe, n_mix + Z0, 0, 4, aside=running_sums, before_unit=3)
            pe.wait_ge(M["acs_out"], 1)
            project(pe, n_mix + VV0, 1, 4)
            pe.wait_ge(M["silu_ready"], 1)
            pe.wait_ge(M["z_ready"], 1)
            pe.wait_ge(M["v_ready"], 2)

            def plain(j):
                if j >= 2:
                    pe.wait_ge(M["copied"], j - 1)
                tile(n_mix + TILE0 + j, None, 5 + j % 2, None)

            for c in range(TB):
                toks = slice(c * P, (c + 1) * P)
                plain(PER_CHUNK * c)
                if c:
                    pe.wait_ge(M["prev_ready"], c)
                for m in range(4):
                    last = pe.transpose(ps[:, 0, m * P:(m + 1) * P], convT[:, m, toks], ident)
                last.then_inc(M["x_ps"], 1)
                if c:
                    pe.wait_ge(M["b_out"], c)
                if c >= 2:
                    pe.wait_ge(M["yo_out"], c - 1)
                for g in range(SG):
                    last = pe.transpose(ps[:, 1, g * SN:(g + 1) * SN], convT[:, 4 + g, toks], ident)
                last.then_inc(M["b_ps"], 1)
                if c:
                    pe.wait_ge(M["seg_ready"], c)
                for h in range(SH):
                    col = dtA[:, c * SH + h:c * SH + h + 1]
                    last = pe.matmul(ps[:, 2 + h // 4, (h % 4) * P:(h % 4 + 1) * P], col.broadcast_to([P, P]), const("tri"),
                                     start=True, stop=True)
                last.then_inc(M["bc_ps"], 1)
                if c:
                    pe.wait_ge(M["S_ready"], c)
                for g in range(SG):
                    last = pe.matmul(ps[:, 4, g * P:(g + 1) * P], convT[:, 4 + g, toks], convT[:, 6 + g, toks], start=True, stop=True)
                last.then_inc(M["g_ps"], 1)
                plain(PER_CHUNK * c + 1)
                pe.wait_ge(M["x_out"], c + 1)
                pe.wait_ge(M["b_out"], c + 1)
                if c < TB - 1:
                    for g in range(SG):
                        last = pe.matmul(ps[:, 0, g * 256:(g + 1) * 256], btok[:, g * SN:(g + 1) * SN], xdec[:, g * 256:(g + 1) * 256],
                                         start=True, stop=True)
                    last.then_inc(M["st_ps"], 1)
                if c:
                    for g in range(SG):
                        last = pe.matmul(ps[:, 1, g * 256:(g + 1) * 256], convT[:, 6 + g, toks], prev[:, g * 256:(g + 1) * 256],
                                         start=True, stop=True)
                    last.then_inc(M["yo_ps"], 1)
                plain(PER_CHUNK * c + 2)
                pe.wait_ge(M["S_ready"], c + 1)
                if c:
                    pe.wait_ge(M["y_ready"], c)
                for h in range(SH):
                    last = pe.matmul(ps[:, 7, h * HD:(h + 1) * HD], lmat[:, h, :], xdt[:, h * HD:(h + 1) * HD], start=True, stop=True)
                last.then_inc(M["yd_ps"], 1)
            pe.wait_ge(M["y_ready"], TB)
            pe.wait_ge(M["copied"], PER_CHUNK * TB)
            pe.wait_ge(M["lru_done"], 1)
            attn_tensor(pe, att2)
            pe.wait_ge(att2.o_done, AH)
            for m in range(4):
                pe.wait_ge(M["y_done"], TB)
                for c in range(TB):
                    last = pe.transpose(ps[:, 4 + m, c * P:(c + 1) * P], z2[:, c, m * P:(m + 1) * P], ident)
                last.then_inc(M["yT_ready"], 1)

        def mix_scalar(act, nm):
            def tap(index, b, n):
                w = convw[:, index, :].rearrange("p a k -> p (a k)")
                act.wait_ge(M["scaled"], n)
                act.activation(convT[:, index, :].rearrange("p a t -> p (a t)"), t32[b % 2][:], ACT.Identity,
                               bias=w[:, CW:CW + 1], scale=w[:, CW - 1:CW]).then_inc(M["tap_ready"], 1)

            def split(u):
                split_hi(act, n_mix + u + LOOK)

            act.wait_ge(M["par_landed"], 16 * 5)
            split(0)
            split(1)
            norm_root(act, nm)
            split(2)
            split(3)
            act.wait_ge(nm.rstd_spread, nm.spreads + 1)
            act.activation(factors[:], ps[:, 7, :], ACT.Copy).then_inc(M["factors"], 1)
            for b in range(4):
                tap(bass.ds(XT + b, 1), b, b + 1)

            def sigmoids(j0):
                for j in range(j0, j0 + 2):
                    for which in range(2):
                        act.wait_ge(M["lru_ps"], 2 * j + which + 1)
                        act.activation((r4, i4)[which][:, j, :], ps[:, 4 + 2 * (j % 2) + which, :], ACT.Sigmoid,
                                       bias=lvec[:, which, j:j + 1]).then_inc(M["lru_gates"], 1)

            for it in range(2):
                for b in range(4):
                    split_hi(act, n_mix + 4 + b + LOOK, it)
                    tap(bass.ds(it * 4 + b, 1), b, it * 4 + (b + 5))
                    if it == 1 and b % 2 == 0:
                        sigmoids(b)
            split(DT0)
            split(Z0)
            act.activation(dt_cols[0:SH, :], ps[0:SH, 4, :], ACT.Copy).then_inc(M["dt_copied"], 1)
            act.wait_ge(M["lru_small"], 1)
            act.activation(sp8[:, 0, :], sp8[:, 0, :], ACT.Exp, scale=-1.0).then_inc(M["lru_e"], 1)
            act.activation(svec[:, 1, :], svec[:, 1, :], ACT.Exp).then_inc(M["lru_e"], 1)
            act.wait_ge(M["lru_sp"], 1)
            for j in range(LT):
                act.activation(a4[:, j, :], r4[:, j, :], ACT.Exp, scale=sp8[:, 4, j:j + 1])
            act.wait_ge(M["dt_e"], 1)
            act.activation(dts[:, 2, :], dts[:, 1, :], ACT.Exp, scale=-1.0).then_inc(M["dt_sum"], 1)
            split(Z0 + 1)
            for j in range(LT):
                last = act.activation(r4[:, j, :], r4[:, j, :], ACT.Tanh, scale=sp8[:, 5, j:j + 1])
            last.then_inc(M["lru_a"], 1)
            act.drain()
            for j in range(LT):
                if j >= 2:
                    act.wait_ge(M["lru_u2"], j - 1)
                act.activation(asq[j % 2][:], a4[:, j, :], ACT.Square).then_inc(M["lru_sq"], 1)
            split(Z0 + 2)
            act.wait_ge(M["lru_u2"], LT)
            act.activation(r4[:], r4[:], ACT.Sqrt).then_inc(M["lru_root"], 1)
            split(Z0 + 3)
            act.wait_ge(M["acs_ps"], 1)
            act.activation(acs[:], ps[:, 4, 0:TB * SH], ACT.Copy)
            act.activation(tot[:], ps[:, 5, 0:TB * SH], ACT.Copy).then_inc(M["acs_out"], 1)
            act.wait_ge(M["conv_done"], 12 + 4)
            act.activation(convT[:, 0:XT, :], convT[:, 0:XT, :], ACT.Silu).then_inc(M["silu_ready"], 1)
            act.wait_ge(unit_used, done(n_mix + Z0 + 3))
            for tb in range(TB):
                last = act.activation(z2[:, tb, :], ps[:, tb, :], ACT.Silu, scale=tok_rstd[:, tb:tb + 1])
            last.then_inc(M["z_ready"], 1)
            split(VV0)
            act.drain()
            act.activation(eacs[:], acs[:], ACT.Exp)
            act.activation(cdec[:], tot[:], ACT.Exp)
            act.wait_ge(M["dec_in"], 1)
            act.activation(dtdec[:], dtdec[:], ACT.Exp).then_inc(M["dec_out"], 1)
            for u in range(1, 4):
                split(VV0 + u)
            act.wait_ge(M["lru_scan"], 1)
            act.dma_start(abias[:], d["abias"]).then_inc(M["bias_landed"], 16)
            act.wait_ge(unit_used, done(n_mix + VV0 + 3))
            for tb in range(TB // 2):
                last = act.activation(v2[:, tb, :], ps[:, 4 + tb, :], ACT.Copy, scale=tok_rstd[:, tb:tb + 1])
            last.then_inc(M["v_ready"], 1)

            def group_roots(c):
                act.wait_ge(M["y_ready"], c + 1)
                if c:
                    act.wait_ge(M["y_done"], c)
                for g in range(SG):
                    act.activation(junk[:, g * 256:(g + 1) * 256], z2[:, c, g * 256:(g + 1) * 256], ACT.Square, accum_out=gsum[:, g:g + 1])
                act.drain()
                act.activation(gstd[:], gsum[:], ACT.Sqrt, bias=const("eps_ssd"), scale=1.0 / 256).then_inc(M["y_std"], 1)

            for c in range(TB):
                j = PER_CHUNK * c
                split(TILE0 + j)
                act.wait_ge(M["b_ps"], c + 1)
                if c:
                    act.wait_ge(M["st_ps"], c)
                act.activation(btok[:], ps[:, 1, 0:SG * SN], ACT.Copy).then_inc(M["b_out"], 1)
                split(TILE0 + j + 1)
                act.wait_ge(M["seg_ready"], c + 1)
                act.activation(lmat[:], lmat[:], ACT.Exp).then_inc(M["L_exp"], 1)
                split(TILE0 + j + 2)
                if c:
                    group_roots(c - 1)
                if c == 1:
                    act.wait_ge(M["copied"], LT)
                    act.activation(gT, gT, ACT.Gelu_apprx_tanh).then_inc(M["gelu_ready"], 1)
            group_roots(TB - 1)
            attn_scalar(act, att2)
            for m in range(4):
                act.wait_ge(M["yT_ready"], m + 1)
                act.activation(mix_hi[:, 4 + m, :], ps[:, 4 + m, :], ACT.Copy).then_inc(M["l_hi"], 1)
            for j in range(LT):
                act.activation(mix_hi[:, 8 + j, :], xT3[:, j, :], ACT.Copy).then_inc(M["l_hi"], 1)

        def mix_vector(dve, nm):
            dve.sem_inc(M["conv_done"], 4)
            token_factors(dve, nm)
            dve.wait_ge(M["factors"], 1)

            def taps(index, bank, n, number):
                w = convw[:, index, :].rearrange("p a k -> p (a k)")
                y = convT[:, index, :].rearrange("p a t -> p (a t)")
                x = t32[bank % 2]
                dve.wait_ge(unit_used, done(number))
                dve.tensor_tensor(x[:], ps[:, bank, :], factors[:], ALU.mult).then_inc(M["scaled"], 1)
                dve.wait_ge(M["tap_ready"], n)
                for back in range(1, CW):
                    last = dve.scalar_tensor_tensor(y[:, back:T], x[:, 0:T - back], w[:, CW - 1 - back:CW - back], y[:, back:T],
                                                    ALU.mult, ALU.add)
                    if back < CW - 1:
                        dve.drain()
                last.then_inc(M["conv_done"], 1)

            for b in range(4):
                taps(bass.ds(XT + b, 1), b, b + 1, n_mix + b)
            with dve.Fori(0, 2) as it:
                for b in range(4):
                    taps(bass.ds(it * 4 + b, 1), b, it * 4 + (b + 5), unit(n_mix + 4 + b, it)[1])
            e, m_, s, s2, p, n8 = (sp8[:, k, :] for k in (0, 1, 2, 3, 4, 5))
            lam = lvec[:, 2, :]
            dve.scalar_tensor_tensor(e, lam, -1.0, lam, ALU.mult, ALU.max)
            dve.tensor_scalar(m_, lam, -1.0, 0.0, ALU.mult, ALU.max).then_inc(M["lru_small"], 1)
            dve.wait_ge(M["lru_e"], 1)
            log1p_series(dve, e, s, s2, p)
            dve.tensor_tensor(p, p, m_, ALU.add)
            dve.drain()
            dve.tensor_scalar(n8, p, 8.0, None, ALU.mult)
            dve.drain()
            dve.tensor_scalar(p, n8, -1.0, None, ALU.mult).then_inc(M["lru_sp"], 1)
            raw_dt, ab, e, s, s2, p = (dts[:, k, :] for k in range(6))
            dve.wait_ge(M["dt_turned"], 1)
            dt3 = raw_dt.rearrange("p (c h) -> p c h", h=SH)
            dve.tensor_tensor(dt3, ps[:, 4:8, 0:SH], bc(tok_rstd[:], 2, SH), ALU.mult)
            dve.drain()
            dve.tensor_tensor(dt3, dt3, bc(svec[:, 0, :], 1, TB), ALU.add)
            dve.drain()
            dve.scalar_tensor_tensor(ab, raw_dt, -1.0, raw_dt, ALU.mult, ALU.max).then_inc(M["dt_e"], 1)
            dve.tensor_tensor(i4[:], i4[:], xT3, ALU.mult)
            dve.wait_ge(M["dt_sum"], 1)
            log1p_series(dve, e, s, s2, p)
            dve.scalar_tensor_tensor(dt_[:], raw_dt, 0.0, p, ALU.max, ALU.add)
            dve.drain()
            dve.wait_ge(M["lru_e"], 2)
            dve.tensor_tensor(dtA[:].rearrange("p (c h) -> p c h", h=SH), dt_[:].rearrange("p (c h) -> p c h", h=SH),
                              bc(svec[:, 1, :], 1, TB), ALU.mult)
            dve.drain()
            dve.tensor_scalar(dtA[:], dtA[:], -1.0, None, ALU.mult).then_inc(M["dt_ready"], 1)
            dve.wait_ge(M["lru_a"], 1)
            for j in range(LT):
                dve.wait_ge(M["lru_sq"], j + 1)
                dve.scalar_tensor_tensor(r4[:, j, :], asq[j % 2][:], 1.0, r4[:, j, :], ALU.add, ALU.mult).then_inc(M["lru_u2"], 1)
            dve.wait_ge(M["lru_root"], 1)
            dve.tensor_tensor(r4[:], r4[:], i4[:], ALU.mult)
            dve.drain()
            for j in range(LT):
                last = dve.tensor_tensor_scan(xT3[:, j, :], a4[:, j, :], r4[:, j, :], 0.0, ALU.mult, ALU.add)
            last.then_inc(M["lru_scan"], 1)
            dve.wait_ge(M["acs_out"], 1)
            dve.tensor_tensor(dtdec[:], tot[:], acs[:], ALU.subtract).then_inc(M["dec_in"], 1)
            dve.wait_ge(M["dec_out"], 1)
            dve.tensor_tensor(dtdec[:], dtdec[:], dt_[:], ALU.mult)
            dve.memset(prev[:], 0.0)
            dve.wait_ge(unit_used, done(n_mix + VV0 + 3))
            for tb in range(TB // 2, TB):
                last = dve.tensor_scalar(v2[:, tb, :], ps[:, 4 + tb, :], tok_rstd[:, tb:tb + 1], None, ALU.mult)
            last.then_inc(M["v_ready"], 1)
            dve.drain()

            def heads(ap):
                return ap.rearrange("p (h d) -> p h d", d=HD)

            def gated(c):
                y = ysk[c % 2]
                dve.wait_ge(M["yd_ps"], c + 1)
                dve.tensor_tensor(y[:], y[:], ps[:, 7, :], ALU.add)
                dve.drain()
                dve.tensor_tensor(z2[:, c, :], z2[:, c, :], y[:], ALU.mult).then_inc(M["y_ready"], 1)

            def group_norm(c):
                dve.wait_ge(M["y_std"], c + 1)
                dve.tensor_scalar(gsum[:], gsum[:], 1.0 / 256, SSD_EPS, ALU.mult, ALU.add)
                dve.drain()
                root_reciprocal(dve, gstd[:], gsum[:], gtmp[:])
                for g in range(SG):
                    cols = slice(g * 256, (g + 1) * 256)
                    z = z2[:, c, cols]
                    last = dve.scalar_tensor_tensor(z, z, gstd[:, g:g + 1], normw[:, cols], ALU.mult, ALU.mult)
                last.then_inc(M["y_done"], 1)

            def plain(j):
                dve.wait_ge(unit_used, done(n_mix + TILE0 + j))
                dve.tensor_tensor(gqkT[:, j, :], ps[:, 5 + j % 2, :], factors[:], ALU.mult).then_inc(M["copied"], 1)

            for c in range(TB):
                hs = slice(c * SH, (c + 1) * SH)
                if c:
                    gated(c - 1)
                plain(PER_CHUNK * c)
                dve.wait_ge(M["x_ps"], c + 1)
                x = heads(ps[:, 0, :])
                dve.tensor_tensor(heads(xdt[:]), x, bc(dt_[:, hs], 2, HD), ALU.mult)
                dve.tensor_tensor(heads(xdec[:]), x, bc(dtdec[:, hs], 2, HD), ALU.mult)
                dve.tensor_tensor(heads(ysk[c % 2][:]), x, bc(svec[:, 2, :], 2, HD), ALU.mult).then_inc(M["x_out"], 1)
                dve.wait_ge(M["bc_ps"], c + 1)
                for h in range(SH):
                    last = dve.scalar_tensor_tensor(lmat[:, h, :], ps[:, 2 + h // 4, (h % 4) * P:(h % 4 + 1) * P],
                                                    acs[:, c * SH + h:c * SH + h + 1], const("causal_t"), ALU.subtract, ALU.add)
                last.then_inc(M["seg_ready"], 1)
                plain(PER_CHUNK * c + 1)
                dve.wait_ge(M["g_ps"], c + 1)
                dve.wait_ge(M["L_exp"], c + 1)
                lm = lmat[:].rearrange("p (g h) i -> p g h i", g=SG)
                dve.tensor_tensor(lm, lm, bc(ps[:, 4, 0:SG * P].rearrange("p (g i) -> p g i", g=SG), 2, SH // SG), ALU.mult)\
                    .then_inc(M["S_ready"], 1)
                if c:
                    dve.wait_ge(M["yo_ps"], c)
                    dve.tensor_tensor(heads(xdec[:]), heads(ps[:, 1, :]), bc(eacs[:, hs], 2, HD), ALU.mult).then_inc(M["yo_out"], 1)
                    dve.drain()
                    dve.tensor_tensor(ysk[c % 2][:], ysk[c % 2][:], xdec[:], ALU.add)
                    dve.drain()
                if c < TB - 1:
                    dve.wait_ge(M["st_ps"], c + 1)
                    dve.tensor_tensor(heads(prev[:]), heads(prev[:]), bc(cdec[:, hs], 2, HD), ALU.mult)
                    dve.drain()
                    dve.tensor_tensor(prev[:], prev[:], ps[:, 0, :], ALU.add).then_inc(M["prev_ready"], 1)
                if c:
                    group_norm(c - 1)
                plain(PER_CHUNK * c + 2)
                if c == 2:
                    dve.wait_ge(M["gelu_ready"], 1)
                    dve.tensor_tensor(xT3, xT3, gT, ALU.mult).then_inc(M["lru_done"], 1)
            gated(TB - 1)
            group_norm(TB - 1)
            dve.wait_ge(M["bias_landed"], 16)
            attn_vector(dve, att2)
            for m in range(8):
                dve.wait_ge(M["l_hi"], m + 1)
                src = ps[:, 4 + m, :] if m < 4 else xT3[:, m - 4, :]
                dve.tensor_tensor(mix_lo[:, 4 + m, :], src, mix_hi[:, 4 + m, :].bitcast(F32), ALU.subtract).then_inc(mix_in, 1)

        def final_vector(dve, nm):
            token_factors(dve, nm)
            dve.wait_ge(nm.rstd_spread, nm.spreads + 1)
            for o in range(KT):
                dve.scalar_tensor_tensor(xT[:, o, :], xT[:, o, :], gain_of(nm, o), ps[:, 7, :], ALU.mult, ALU.mult)\
                    .then_inc(out_ready, 1)

        mix_in = sem("mix_parts")
        norms, rows = count(), count()
        glu = Gated(0, "glu", KT, after(S["ylo_ready"], 2))

        def norm(name, acc_ready):
            nth = next(norms)
            return Norm(nth, nth - (nth > 1), name, acc_ready)

        def rows_of(name, k_tiles, hi, lo, in_ready, **early):
            return Rows(next(rows), name, k_tiles, hi, lo, in_ready, **early)

        def normed(nm):
            return after(nm.h_ready, nm.before)

        def mixed(n):
            return att2.tiles_ready(n) if isinstance(n, int) and n <= 4 else (mix_in, n - 4)

        def squared(ph):
            return after(ph.acc_ready, ph.before)

        norm_f0 = norm("norm_ffn0", after(glu.out_ready))
        gu0 = Gated(KT + 0 * FT, "gu0", FT, normed(norm_f0))
        down0 = rows_of("down0", FT, hid_hi, hid_lo, after(gu0.out_ready, gu0.before))
        norm_m1 = norm("norm_mix1", squared(down0))
        wo = rows_of("wo", KT, h_hi, h_lo, att1.tiles_ready, hi_early=KT - LAST, lo_early=KT - LAST)
        norm_f1 = norm("norm_ffn1", squared(wo))
        gu1 = Gated(KT + 1 * FT, "gu1", FT, normed(norm_f1))
        down1 = rows_of("down1", FT, hid_hi, hid_lo, after(gu1.out_ready, gu1.before))
        norm_m2 = norm("norm_mix2", squared(down1))
        w_out = rows_of("out", 12, mix_hi, mix_lo, mixed, lo_early=12 - KT - LAST)
        norm_f2 = norm("norm_ffn2", squared(w_out))
        gu2 = Gated(KT + 2 * FT, "gu2", FT, normed(norm_f2))
        down2 = rows_of("down2", FT, hid_hi, hid_lo, after(gu2.out_ready, gu2.before))
        norm_end = norm("norm_final", squared(down2))
        out_ready, out_landed = sem("out_ready"), sem("out_landed")

        def after_pairs(ph):
            n = ph.before + ph.pairs
            return [(o, None) for o in range(4, 7)] + [(0, (ph.pair_done, n + 1)), (1, None), (2, (ph.pair_done, n + 2)), (3, None), (7, None)]

        block = ctx.enter_context(nc.Block())

        @block.sync
        def _(sp):
            s5_sync(sp)
            load_units(sp, "glu", d["w_glu"], after_head=residual)
            load_units(sp, "gu0", d["w_gu0"])
            load_units(sp, "down0", d["w_down0"])
            load_units(sp, "dsa", d["w_dsa"])
            load_units(sp, "wo", d["w_o"])
            load_units(sp, "gu1", d["w_gu1"])
            load_units(sp, "down1", d["w_down1"])
            load_units(sp, "mix", d["w_mix"])
            load_units(sp, "out", d["w_out"])
            load_units(sp, "gu2", d["w_gu2"])
            load_units(sp, "down2", d["w_down2"])
            for o in range(KT):
                sp.wait_ge(out_ready, o + 1)
                sp.dma_start(out[:, o, :], xT[:, o, :]).then_inc(out_landed, 16)
            sp.wait_ge(out_landed, 16 * KT)

        @block.gpsimd
        def _(pool):
            s5_gpsimd(pool)
            split_lo_all(pool)

        @block.scalar
        def _(act):
            s5_scalar(act)
            glu_scalar(act, glu)
            glu_norm_scalar(act, norm_f0, glu)
            norm_root(act, norm_f0)
            ffn_scalar(act, gu0)
            rows_scalar(act, down0, norm_m1)
            act.wait_ge(down0.tile_done, down0.before + KT)
            act.dma_start(rope[:], d["rope"]).then_inc(A["par_landed"], 16)
            act.dma_start(hgain[:], d["hgain"]).then_inc(A["par_landed"], 16)
            dsa_scalar(act, norm_m1)
            rows_scalar(act, wo, norm_f1)
            norm_root(act, norm_f1)
            ffn_scalar(act, gu1)
            rows_scalar(act, down1, norm_m2)
            act.wait_ge(down1.tile_done, down1.before + KT)
            for buf, name in ((convw, "convw"), (gates, "gates"), (lvec, "lvec"), (svec, "svec"), (normw, "normw")):
                act.dma_start(buf[:], d[name]).then_inc(M["par_landed"], 16)
            mix_scalar(act, norm_m2)
            rows_scalar(act, w_out, norm_f2)
            norm_root(act, norm_f2)
            ffn_scalar(act, gu2)
            rows_scalar(act, down2)
            norm_root(act, norm_end)

        @block.vector
        def _(dve):
            def factors_of(nm):
                token_factors(dve, nm)
                dve.wait_ge(nm.rstd_spread, nm.spreads + 1)
                dve.tensor_copy(spread[:], ps[:, 7, :])
                dve.drain()

            s5_vector(dve)
            glu_vector(dve, glu)
            glu_norm_vector(dve, norm_f0)
            factors_of(norm_f0)
            ffn_vector(dve, gu0)
            rows_vector(dve, down0, norm_m1)
            dsa_vector(dve, norm_m1)
            rows_vector(dve, wo, norm_f1)
            factors_of(norm_f1)
            ffn_vector(dve, gu1)
            rows_vector(dve, down1, norm_m2)
            mix_vector(dve, norm_m2)
            rows_vector(dve, w_out, norm_f2)
            factors_of(norm_f2)
            ffn_vector(dve, gu2)
            rows_vector(dve, down2)
            final_vector(dve, norm_end)

        @block.tensor
        def _(pe):
            pe.sem_inc(unit_used, 1)
            s5_tensor(pe)
            gated_tensor(pe, glu)
            gated_tensor(pe, gu0, norm_f0)
            rows_tensor(pe, down0, after_pairs(gu0))
            dsa_tensor(pe, norm_m1)
            rows_tensor(pe, wo, [(o, None) for o in range(6)] + [(o, (att1.o_done, NH - 7 + o)) for o in (6, 7)])
            gated_tensor(pe, gu1, norm_f1, (wo.x_ready, wo.before + 2))
            rows_tensor(pe, down1, after_pairs(gu1))
            mix_tensor(pe, norm_m2)
            rows_tensor(pe, w_out, [(o, None) for o in range(4)] + [(o, (mix_in, o - 3)) for o in range(4, KT)])
            gated_tensor(pe, gu2, norm_f2, (w_out.x_ready, w_out.before + 2))
            rows_tensor(pe, down2, after_pairs(gu2))
            norm_sums(pe, norm_end)
            norm_spread(pe, norm_end)


def kernel(**inputs):
    import concourse.bacc as bacc
    from concourse.bass_utils import run_bass_kernel_spmd

    i = {k: np.asarray(v) for k, v in inputs.items()}
    x = i["x"][0]

    def tiles(w):
        k, n = w.shape
        return w.reshape(k // P, P, n // P, P).transpose(2, 1, 0, 3).reshape(n // P, P, k)

    def pairs(gate, value):
        return np.stack([tiles(gate), tiles(value)], 1).reshape(-1, P, gate.shape[0])

    def token_major(w):
        return w.reshape(KT // 2, 2, P, GROUP).transpose(0, 2, 1, 3).reshape(KT // 2, P, UNIT)

    def narrow(w):
        u = np.zeros((P, KT, P), w.dtype)
        u[:, :, :w.shape[1]] = w.reshape(KT, P, -1).transpose(1, 0, 2)
        return u.reshape(1, P, UNIT)

    def two(name):
        return i[name + "_2"][0]

    def block_diagonal(w):
        o = np.zeros((P, LT, P), w.dtype)
        for b in range(2 * LT):
            at = slice(HD * (b % 2), HD * (b % 2 + 1))
            o[at, b // 2, at] = w[b]
        return o

    w2 = two("w_in")
    w_in = i["dsa_w_in"][0]
    rest = narrow(w_in[:, 3 * D + IH * HD:])

    def states(a):
        return np.moveaxis(a, 1, 0)

    s5 = {k: i["s5_" + k][0] for k in ("lambda_re", "lambda_im", "log_dt", "b_re", "b_im", "c_re", "c_im", "d", "w_glu")}
    twice = lambda a, b: np.concatenate([states(a), states(b)], 0)
    gain = np.tile(i["norm_mix"][0].reshape(G, GH).T, (CH, 1))
    par = np.stack([twice(s5["lambda_re"], s5["lambda_re"]), twice(s5["lambda_im"], s5["lambda_im"]),
                    np.broadcast_to(s5["log_dt"], (P, G)), gain], 1)
    ct = {k: s5[k].transpose(0, 2, 1) for k in ("c_re", "c_im")}
    vecs = {"norm_ffn0": i["norm_ffn"][0], "norm_mix1": i["norm_mix"][1], "norm_ffn1": i["norm_ffn"][1],
            "norm_mix2": i["norm_mix_2"][0], "norm_ffn2": i["norm_ffn_2"][0], "norm_final": i["norm_final_2"]}
    wg = s5["w_glu"]
    arrays = {
        "cst": np.concatenate(list(constant_columns().values()), 1),
        "vec": np.concatenate([vecs[k].reshape(-1, P).T for k in VEC], 1),
        "xT": x.T.reshape(KT, P, T).transpose(1, 0, 2),
        "xs5": x.reshape(NC, CH, G, GH)[:, ::-1].transpose(1, 3, 2, 0).reshape(P, G, NC),
        "s5_par": par,
        "s5_b": np.stack([twice(s5["b_re"], s5["b_im"]), twice(s5["b_im"], s5["b_re"])], 1).reshape(P, 2, G * GH),
        "s5_c": np.stack([twice(ct["c_re"], ct["c_im"]), twice(ct["c_im"], ct["c_re"])], 1).reshape(P, 2, G * GH),
        "s5_d": s5["d"].reshape(G, GH).T,
        "w_glu": pairs(wg[:, D:], wg[:, :D]),
        "w_gu0": pairs(i["ffn_w_gate_up"][0][:, :FF], i["ffn_w_gate_up"][0][:, FF:]),
        "w_down0": i["ffn_w_down"][0].reshape(FT, P, D),
        "rope": rope_tables(),
        "hgain": np.broadcast_to(np.stack([i["dsa_q_norm"][0], i["dsa_k_norm"][0]]), (P, 2, HD)),
        "w_dsa": np.concatenate([token_major(w_in[:, 3 * D:3 * D + IH * HD]), rest]
                                + [token_major(w_in[:, n * GROUP:(n + 1) * GROUP]) for n in range(6)]),
        "w_o": i["dsa_w_o"][0].reshape(KT, P, D),
        "w_gu1": pairs(i["ffn_w_gate_up"][1][:, :FF], i["ffn_w_gate_up"][1][:, FF:]),
        "w_down1": i["ffn_w_down"][1].reshape(FT, P, D),
        "abias": dilated_bias(),
        "gates": np.stack([block_diagonal(two("lru_wa")), block_diagonal(two("lru_wx"))], 2),
        "normw": np.broadcast_to(two("ssd_norm"), (P, GROUP)),
        "convw": np.concatenate([np.concatenate([two(n + "_conv_w").T, two(n + "_conv_b")[:, None]], 1) for n in ("ssd", "lru")])
                 .reshape(XT + LT, P, CW + 1).transpose(1, 0, 2),
        "lvec": np.stack([two(n).reshape(LT, P).T for n in ("lru_ba", "lru_bx", "lru_lambda")], 1),
        "svec": np.broadcast_to(np.stack([two(n) for n in ("ssd_dt_bias", "ssd_a_log", "ssd_d")]), (P, 3, SH)),
        "w_mix": np.concatenate([tiles(w2[:, 3592:4104]), tiles(w2[:, 2048:3072]), narrow(w2[:, 3072:3080]),
                                 token_major(w2[:, 1536:2048]), token_major(w2[:, 1024:1536]), tiles(w2[:, 3080:3592]),
                                 tiles(w2[:, 0:1024])]),
        "w_out": two("w_out").reshape(12, P, D),
        "w_gu2": pairs(two("w_gate"), two("w_up")),
        "w_down2": two("w_down").reshape(FT, P, D),
    }
    arrays = {"in_" + k: np.ascontiguousarray(v) for k, v in arrays.items()}
    nc = bacc.Bacc("TRN2", target_bir_lowering=False, num_devices=1)
    d = {k[3:]: nc.dram_tensor(k, v.shape, mybir.dt.from_np(v.dtype), kind="ExternalInput").ap() for k, v in arrays.items()}
    out = nc.dram_tensor("out_x", (P, KT, T), F32, kind="ExternalOutput").ap()
    build(nc, d, out)
    r = run_bass_kernel_spmd(nc, [arrays], core_ids=[0])
    got = np.asarray(r.results[0]["out_x"])
    return got.transpose(2, 1, 0).reshape(1, T, D)
```
